# Optimizing a Trainium2 kernel written in Bass

```python
import math
import jax
import jax.numpy as jnp
from jax import lax
import numpy as np

D_MODEL = 1024
BATCH = 1
SEQ = 128
DEPTH = 1
DEC_BATCH = 1
DEC_SEQ = 1024
PAST_LEN = 128

GRID_W = 64
D_MIX = D_MODEL
D_HY = D_MIX // 2
D_ML = D_MIX - D_HY
ML_HEADS = 4
ML_HD = D_ML // ML_HEADS
CHUNK = 128
HY_BANDS = 16
HY_EMB = 2 * HY_BANDS + 1
HY_FFN = 64
HY_DECAY_TARGET = 1e-2
HY_FAST_DECAY_PCT = 0.3
HY_SLOW_DECAY_PCT = 1.5
HY_MIN_DECAY = math.log(HY_DECAY_TARGET) / HY_SLOW_DECAY_PCT
HY_MAX_DECAY = math.log(HY_DECAY_TARGET) / HY_FAST_DECAY_PCT
D_FF = 2816
N_GATES = 4 * ML_HEADS
N_IN = 3 * D_HY + 4 * D_ML + N_GATES
N_MOD = 6 * D_MODEL
EPS = 1e-6
F32 = jnp.float32

kernel_name = 'hyena_mlstm_prefix_diffusion_step'

def _rmsnorm(x, w):
    xf = x.astype(F32)
    y = xf * lax.rsqrt(jnp.mean(xf * xf, axis=-1, keepdims=True) + EPS)
    return (y * w.astype(F32)).astype(x.dtype)

def _dwconv1d(u, w, b):
    up = jnp.pad(u, ((0, 0), (1, 1), (0, 0)))
    return up[:, :-2] * w[0] + up[:, 1:-1] * w[1] + up[:, 2:] * w[2] + b

def _dwconv2d(u, w, b):
    y = lax.conv_general_dilated(u, w[:, :, None, :].astype(u.dtype), (1, 1), 'SAME',
                                 dimension_numbers=('NHWC', 'HWIO', 'NHWC'),
                                 feature_group_count=u.shape[-1])
    return y + b

def _hyena_kernel(L, w1, b1, w2, b2, w3, b3, w4, freq):
    t = jnp.linspace(0.0, 1.0, L, dtype=F32)[:, None]
    wpos = (2.0 * math.pi / L) * jnp.arange(L, dtype=F32)[:, None]
    bands = jnp.linspace(1e-4, HY_BANDS - 1, HY_BANDS, dtype=F32)[None, :]
    z = jnp.concatenate([t, jnp.cos(bands * wpos), -jnp.sin(bands * wpos)], axis=-1)
    fr = freq.astype(F32)
    h = jnp.sin(fr * (z @ w1.astype(F32) + b1.astype(F32)))
    h = jnp.sin(fr * (h @ w2.astype(F32) + b2.astype(F32)))
    h = jnp.sin(fr * (h @ w3.astype(F32) + b3.astype(F32)))
    h = h @ w4.astype(F32)
    deltas = jnp.linspace(HY_MIN_DECAY, HY_MAX_DECAY, D_HY, dtype=F32)
    decay = jnp.exp(-t * jnp.abs(deltas)[None, :])
    h = h * jnp.concatenate([decay, decay], axis=-1)
    hf, hb = h[:, :D_HY], h[:, D_HY:]
    k = jnp.concatenate([hf, jnp.zeros((1, D_HY), F32), hb[:0:-1]], axis=0)
    return k / jnp.sum(jnp.abs(k), axis=0, keepdims=True)

def _hyena(u, p):
    dt = u.dtype
    B, L, _ = u.shape
    u = _dwconv1d(u, p['hy_conv_w'], p['hy_conv_b']).astype(F32)
    x0, x1, v = jnp.split(u, 3, axis=-1)
    v = v * x1
    k = _hyena_kernel(L, *p['hy_filt'])
    n = 2 * L
    y = jnp.fft.irfft(jnp.fft.rfft(v, n=n, axis=1) * jnp.fft.rfft(k, n=n, axis=0)[None],
                      n=n, axis=1)[:, :L]
    y = (y + p['hy_bias'].astype(F32) * v) * x0
    return y.astype(dt)

def _mlstm_scan(q, k, v, i_pre, f_pre, C0, n0, m0):
    B, L, H, dh = q.shape
    nc = L // CHUNK

    def chunks(a):
        a = a.reshape((B, nc, CHUNK) + a.shape[2:])
        return jnp.moveaxis(jnp.moveaxis(a, 1, 0), 3, 2)

    causal = jnp.tril(jnp.ones((CHUNK, CHUNK), dtype=bool))

    def step(carry, xs):
        C, n, m = carry
        qc, kc, vc, ic, lfc = xs
        b = jnp.cumsum(lfc, axis=-1)
        dmat = jnp.where(causal, b[..., :, None] - b[..., None, :] + ic[..., None, :], -jnp.inf)
        inter = b + m[..., None]
        m_t = jnp.maximum(inter, jnp.max(dmat, axis=-1))
        s = jnp.einsum('bhtd,bhsd->bhts', qc, kc) * jnp.exp(dmat - m_t[..., None])
        w_inter = jnp.exp(inter - m_t)
        num = jnp.einsum('bhts,bhse->bhte', s, vc) + w_inter[..., None] * jnp.einsum('bhed,bhtd->bhte', C, qc)
        den = jnp.sum(s, axis=-1) + w_inter * jnp.einsum('bhd,bhtd->bht', n, qc)
        h = num / jnp.maximum(jnp.abs(den), jnp.exp(-m_t))[..., None]
        b_end = b[..., -1]
        w_log = b_end[..., None] - b + ic
        m_new = jnp.maximum(b_end + m, jnp.max(w_log, axis=-1))
        w_s = jnp.exp(w_log - m_new[..., None])
        w_c = jnp.exp(b_end + m - m_new)
        C_new = w_c[..., None, None] * C + jnp.einsum('bhs,bhse,bhsd->bhed', w_s, vc, kc)
        n_new = w_c[..., None] * n + jnp.einsum('bhs,bhsd->bhd', w_s, kc)
        return (C_new, n_new, m_new), h

    xs = (chunks(q), chunks(k), chunks(v), chunks(i_pre), chunks(jax.nn.log_sigmoid(f_pre)))
    (C, n, m), hs = lax.scan(step, (C0.astype(F32), n0.astype(F32), m0.astype(F32)), xs)
    h = jnp.swapaxes(jnp.moveaxis(hs, 0, 1), 2, 3).reshape(B, L, H, dh)
    return h, C, n, m

def _mlstm(u, g, p, C0, n0, m0):
    dt = u.dtype
    B, L, _ = u.shape
    qk = jax.nn.silu(_dwconv1d(u[..., :2 * D_ML], p['ml_conv_w'], p['ml_conv_b']).astype(F32))
    q = qk[..., :D_ML].reshape(B, L, ML_HEADS, ML_HD)
    k = qk[..., D_ML:].reshape(B, L, ML_HEADS, ML_HD) * (ML_HD ** -0.5)
    v = u[..., 2 * D_ML:3 * D_ML].astype(F32).reshape(B, L, ML_HEADS, ML_HD)
    o = u[..., 3 * D_ML:].astype(F32)
    i_f, f_f, i_b, f_b = jnp.split(g.astype(F32), 4, axis=-1)
    h_f, Cf, nf, mf = _mlstm_scan(q, k, v, i_f, f_f, C0[:, 0], n0[:, 0], m0[:, 0])
    h_b, Cb, nb, mb = _mlstm_scan(q[:, ::-1], k[:, ::-1], v[:, ::-1], i_b[:, ::-1], f_b[:, ::-1],
                                  C0[:, 1], n0[:, 1], m0[:, 1])
    h = h_f + h_b[:, ::-1]
    h = h * lax.rsqrt(jnp.mean(h * h, axis=-1, keepdims=True) + EPS)
    h = h * p['ml_norm_w'].astype(F32).reshape(ML_HEADS, ML_HD)
    y = h.reshape(B, L, D_ML) * jax.nn.sigmoid(o)
    return (y.astype(dt), jnp.stack([Cf, Cb], axis=1), jnp.stack([nf, nb], axis=1),
            jnp.stack([mf, mb], axis=1))

def _layer(x, mod, p, C0, n0, m0, rows):
    B, L, _ = x.shape
    shift_m, scale_m, gate_m, shift_f, scale_f, gate_f = jnp.split(mod, 6, axis=-1)
    h = _rmsnorm(x, p['norm_mix_w']) * (1 + scale_m) + shift_m
    proj = h @ p['w_in']
    u_hy = proj[..., :3 * D_HY]
    u_ml = proj[..., 3 * D_HY:3 * D_HY + 4 * D_ML]
    g_ml = proj[..., 3 * D_HY + 4 * D_ML:] + p['b_gate']
    y_hy = _hyena(u_hy, p)
    y_ml, C, n, m = _mlstm(u_ml, g_ml, p, C0, n0, m0)
    x = x + gate_m * (jnp.concatenate([y_hy, y_ml], axis=-1) @ p['w_out'])
    h = _rmsnorm(x, p['norm_ffn_w']) * (1 + scale_f) + shift_f
    up = (h @ p['ffn_w_up']).reshape(B, rows, L // rows, 2 * D_FF)
    up = _dwconv2d(up, p['ffn_conv_w'], p['ffn_conv_b']).reshape(B, L, 2 * D_FF)
    a, val = jnp.split(up, 2, axis=-1)
    x = x + gate_f * ((jax.nn.silu(a) * val) @ p['ffn_w_down'])
    return x, C, n, m

def setup_inputs(seed: int = 0) -> dict:
    key = jax.random.key(seed)
    ks = jax.random.split(key, 34)

    def nrm(i, shape, scale):
        return jax.random.normal(ks[i], shape, F32) * scale

    f_bias = jnp.linspace(3.0, 6.0, ML_HEADS, dtype=F32)
    z_h = jnp.zeros((ML_HEADS,), F32)
    gate_base = jnp.concatenate([z_h, f_bias, z_h, f_bias])
    return {
        'x_prompt': nrm(0, (BATCH, SEQ, D_MODEL), 1.0),
        'x_sample': nrm(1, (DEC_BATCH, DEC_SEQ, D_MODEL), 1.0),
        'state_mlstm_C': nrm(2, (DEC_BATCH, DEPTH, 2, ML_HEADS, ML_HD, ML_HD), 0.1),
        'state_mlstm_n': nrm(3, (DEC_BATCH, DEPTH, 2, ML_HEADS, ML_HD), 0.5),
        'state_mlstm_m': nrm(4, (DEC_BATCH, DEPTH, 2, ML_HEADS), 0.5),
        'c': nrm(5, (DEC_BATCH, D_MODEL), 1.0),
        'c_ctx': nrm(6, (D_MODEL,), 1.0),
        'ada_w': nrm(7, (DEPTH, D_MODEL, N_MOD), 0.5 * D_MODEL ** -0.5),
        'ada_b': nrm(8, (DEPTH, N_MOD), 0.02),
        'norm_mix_w': 1.0 + nrm(9, (DEPTH, D_MODEL), 0.05),
        'w_in': nrm(10, (DEPTH, D_MODEL, N_IN), D_MODEL ** -0.5),
        'b_gate': gate_base[None, :] + nrm(11, (DEPTH, N_GATES), 0.1),
        'hy_conv_w': nrm(12, (DEPTH, 3, 3 * D_HY), 3 ** -0.5),
        'hy_conv_b': nrm(13, (DEPTH, 3 * D_HY), 0.02),
        'hy_filt_w1': nrm(14, (DEPTH, HY_EMB, HY_FFN), HY_EMB ** -0.5),
        'hy_filt_b1': nrm(15, (DEPTH, HY_FFN), 0.1),
        'hy_filt_w2': nrm(16, (DEPTH, HY_FFN, HY_FFN), HY_FFN ** -0.5),
        'hy_filt_b2': nrm(17, (DEPTH, HY_FFN), 0.1),
        'hy_filt_w3': nrm(18, (DEPTH, HY_FFN, HY_FFN), HY_FFN ** -0.5),
        'hy_filt_b3': nrm(19, (DEPTH, HY_FFN), 0.1),
        'hy_filt_w4': nrm(20, (DEPTH, HY_FFN, 2 * D_HY), HY_FFN ** -0.5),
        'hy_freq': 1.0 + nrm(21, (DEPTH, HY_FFN), 0.1),
        'hy_bias': nrm(22, (DEPTH, D_HY), 1.0),
        'ml_conv_w': nrm(23, (DEPTH, 3, 2 * D_ML), 3 ** -0.5),
        'ml_conv_b': nrm(24, (DEPTH, 2 * D_ML), 0.02),
        'ml_norm_w': 1.0 + nrm(25, (DEPTH, D_ML), 0.05),
        'w_out': nrm(26, (DEPTH, D_MIX, D_MODEL), D_MIX ** -0.5),
        'norm_ffn_w': 1.0 + nrm(27, (DEPTH, D_MODEL), 0.05),
        'ffn_w_up': nrm(28, (DEPTH, D_MODEL, 2 * D_FF), D_MODEL ** -0.5),
        'ffn_conv_w': nrm(29, (DEPTH, 3, 3, 2 * D_FF), 1.0 / 3.0),
        'ffn_conv_b': nrm(30, (DEPTH, 2 * D_FF), 0.02),
        'ffn_w_down': nrm(31, (DEPTH, D_FF, D_MODEL), D_FF ** -0.5),
        'final_norm_w': 1.0 + nrm(32, (D_MODEL,), 0.05),
    }

def reference(x_prompt, x_sample, state_mlstm_C, state_mlstm_n, state_mlstm_m, c, c_ctx,
              ada_w, ada_b, norm_mix_w, w_in, b_gate, hy_conv_w, hy_conv_b,
              hy_filt_w1, hy_filt_b1, hy_filt_w2, hy_filt_b2, hy_filt_w3, hy_filt_b3, hy_filt_w4,
              hy_freq, hy_bias, ml_conv_w, ml_conv_b, ml_norm_w, w_out, norm_ffn_w,
              ffn_w_up, ffn_conv_w, ffn_conv_b, ffn_w_down, final_norm_w):
    rows_lat = x_sample.shape[1] // GRID_W
    bp = x_prompt.shape[0]
    zC = jnp.zeros((bp, 2, ML_HEADS, ML_HD, ML_HD), F32)
    zn = jnp.zeros((bp, 2, ML_HEADS, ML_HD), F32)
    zm = jnp.zeros((bp, 2, ML_HEADS), F32)
    xp, xs = x_prompt, x_sample
    new_C, new_n, new_m = [], [], []
    for l in range(DEPTH):
        p = {
            'norm_mix_w': norm_mix_w[l], 'w_in': w_in[l], 'b_gate': b_gate[l],
            'hy_conv_w': hy_conv_w[l], 'hy_conv_b': hy_conv_b[l],
            'hy_filt': (hy_filt_w1[l], hy_filt_b1[l], hy_filt_w2[l], hy_filt_b2[l],
                        hy_filt_w3[l], hy_filt_b3[l], hy_filt_w4[l], hy_freq[l]),
            'hy_bias': hy_bias[l], 'ml_conv_w': ml_conv_w[l], 'ml_conv_b': ml_conv_b[l],
            'ml_norm_w': ml_norm_w[l], 'w_out': w_out[l], 'norm_ffn_w': norm_ffn_w[l],
            'ffn_w_up': ffn_w_up[l], 'ffn_conv_w': ffn_conv_w[l], 'ffn_conv_b': ffn_conv_b[l],
            'ffn_w_down': ffn_w_down[l],
        }
        mod_ctx = (jax.nn.silu(c_ctx) @ ada_w[l] + ada_b[l])[None, None, :]
        mod_lat = (jax.nn.silu(c) @ ada_w[l] + ada_b[l])[:, None, :]
        xp, Cl, nl, ml = _layer(xp, mod_ctx, p, zC, zn, zm, 1)
        new_C.append(Cl)
        new_n.append(nl)
        new_m.append(ml)
        xs, _, _, _ = _layer(xs, mod_lat, p, state_mlstm_C[:, l], state_mlstm_n[:, l],
                             state_mlstm_m[:, l], rows_lat)
    y_prompt = _rmsnorm(xp, final_norm_w)
    y_sample = _rmsnorm(xs, final_norm_w)
    new_mlstm_C = jnp.stack(new_C, axis=1)
    new_mlstm_n = jnp.stack(new_n, axis=1)
    new_mlstm_m = jnp.stack(new_m, axis=1)
    return (y_prompt, y_sample, new_mlstm_C, new_mlstm_n, new_mlstm_m)


_drawn_inputs = setup_inputs


def setup_inputs(seed=0):
    import zlib

    import numpy as np

    out = dict(_drawn_inputs(seed))
    spreads = {}
    factors = {'state_mlstm_C': 8.0,
     'state_mlstm_n': 8.0,
     'state_mlstm_m': 8.0,
     'hy_conv_b': 6.642,
     'hy_filt_b1': 8.0,
     'hy_filt_b2': 6.21,
     'hy_filt_b3': 5.882,
     'hy_freq': 8.0,
     'ml_norm_w': 8.0,
     'norm_ffn_w': 4.347,
     'ffn_conv_b': 8.0}
    for name, (base, spread) in spreads.items():
        noise = np.random.default_rng([zlib.crc32(name.encode()), seed]).standard_normal(out[name].shape)
        drawn = base * np.exp(spread * noise) if base else spread * noise
        out[name] = jnp.asarray(drawn.astype(out[name].dtype))
    for name, factor in factors.items():
        out[name] = (out[name] * factor).astype(out[name].dtype)
    return out
```

```python
import math
from contextlib import ExitStack

import numpy as np

import concourse.bass as bass
from concourse import mybir

F32 = mybir.dt.float32
F32R = mybir.dt.float32r
ALU = mybir.AluOpType
ACT = mybir.ActivationFunctionType

P = 128
D = 1024
KD = D // P
LS, LP = 1024, 128
T = LS + LP
NB, BW = 3, 384
assert NB * BW == T
DH = 512
CH = DH // P
HEADS, HD = 4, 128
DFF = 2816
JF = DFF // P
NIN = 3 * DH + 4 * DH + 16
QOFF, KOFF, VOFF, OOFF, GOFF = 3 * DH, 4 * DH, 5 * DH, 6 * DH, 7 * DH
EPS = 1e-6
UNIT = 2048
NT = T // P
ROWS = 64

PA = {}
at = 0
for name, n in (("ada_b", 48), ("norm_mix_w", 8), ("norm_ffn_w", 8), ("final_norm_w", 8),
                ("hy_conv_b", 12), ("hy_bias", 4), ("ml_conv_b", 8), ("ml_norm_w", 4)):
    PA[name] = at
    at += n
NROW1 = at
PA["hy_conv_w"] = 128
PA["ml_conv_w"] = 128 + 36
PA["cond"] = 128 + 60
PA["filter_vec"] = 128 + 76
PA["ffn_conv_w"] = 256
PA["ffn_conv_b"] = 256 + 9 * 44
NPAR = 256 + 440
FROWS = 110


def lin(start, stop, n):
    step = np.arange(n, dtype=np.float32) / np.float32(n - 1)
    out = np.float32(start) * (np.float32(1) - step) + np.float32(stop) * step
    out[-1] = np.float32(stop)
    return out.astype(np.float32)


def positions(L):
    t = lin(0.0, 1.0, L)[:, None]
    wpos = np.float32(2.0 * math.pi / L) * np.arange(L, dtype=np.float32)[:, None]
    arg = (lin(1e-4, 15, 16)[None, :] * wpos).astype(np.float32).astype(np.float64)
    z = np.concatenate([t, np.cos(arg), -np.sin(arg)], axis=1).astype(np.float32)
    dmin, dmax = math.log(1e-2) / 1.5, math.log(1e-2) / 0.3
    deltas = np.abs(lin(dmin, dmax, DH))
    decay = np.exp((-t * deltas[None, :]).astype(np.float64)).astype(np.float32)
    return z, decay


def constants():
    zs, ds = positions(LS)
    zp, dp = positions(LP)
    zT = np.concatenate([zs, zp], 0).T.copy()
    decay = np.stack([ds[p + 256 * b:p + 256 * (b + 1):2] for p in (0, 1) for b in range(4)] + [dp])
    k = np.arange(512)[None, :]
    s = np.arange(512)[:, None]
    fwd = []
    for p in (0, 1):
        fwd.append(np.cos(2 * np.pi * ((k * (2 * s + p)) % 2048) / 2048))
    for p in (0, 1):
        m = np.sin(2 * np.pi * ((k * (2 * s + p)) % 2048) / 2048)
        m[:, 0] = (-1.0) ** s[:, 0]
        fwd.append(m)
    weight = np.full((512, 1), 2.0 / 2048)
    weight[0] = 1.0 / 2048
    inv = [fwd[0].T * weight, None, fwd[1].T * weight, None]
    for p in (0, 1):
        m = fwd[2 + p].T * (2.0 / 2048)
        inv[2 * p + 1] = m
    f = np.stack(fwd).reshape(4, 4, P, 4, P)
    fwd_units = f.transpose(3, 2, 0, 1, 4).reshape(4, P, UNIT)
    inv_units = np.stack(inv).reshape(4, 4, P, 512).transpose(0, 2, 1, 3).reshape(4, P, UNIT)
    tt = np.arange(P)[:, None]
    kk = np.arange(P)[None, :]
    c = np.cos(2 * np.pi * (tt * kk % 256) / 256)
    sn = np.sin(2 * np.pi * (tt * kk % 256) / 256)
    sn[:, 0] = (-1.0) ** tt[:, 0]
    wc = np.full((P, 1), 2.0 / 256)
    wc[0] = 1.0 / 256
    prompt = np.stack([c, sn, c.T * wc, sn.T * wc], 1).reshape(P, 4 * P)
    ident = np.eye(P)
    i = np.arange(P)
    mask = np.stack([np.where(i[:, None] <= i[None, :], 0.0, 1e30),
                     np.where(i[:, None] >= i[None, :], 0.0, 1e30)], 1)
    sel = np.zeros((ROWS, 8, P))
    for d in range(2):
        for h in range(HEADS):
            sel[32 * d + h, 4 * d + h] = 1.0
    reset = np.ones((ROWS, T))
    reset[0:32, 0::P] = 0.0
    reset[32:64, P - 1::P] = 0.0
    return {n: np.ascontiguousarray(a, dtype=np.float32) for n, a in dict(
        k_z=zT, k_decay=decay, k_fwd=fwd_units, k_inv=inv_units, k_prompt=prompt,
        k_ident=ident, k_mask=mask, k_sel=sel, k_reset=reset).items()}


class Chain:

    def __init__(self, eng, sem):
        self.eng, self.sem, self.n = eng, sem, 0

    def do(self, ins):
        self.n += 1
        ins.then_inc(self.sem, 1)
        self.eng.wait_ge(self.sem, self.n)


class WeightRing:

    def __init__(self, nc, ph, mem, used_at):
        self.nc, self.mem = nc, mem
        self.raw_in = [ph.sem(f"weights_loaded{i}") for i in range(2)]
        self.hi_done = ph.sem("weights_hi")
        self.lo_done = ph.sem("weights_lo")
        self.used_at = used_at

    def raw(self, u):
        return self.mem["w_raw"][:, u % 2, :]

    def hi(self, u):
        return self.mem["w_hi"][:, u % 2, :]

    def lo(self, u):
        return self.mem["w_lo"][:, u % 2, :]

    def load(self, sp, u, src, view=None):
        if u >= 2:
            sp.wait_ge(self.lo_done, u - 1)
        dst = self.raw(u) if view is None else view(self.raw(u))
        sp.dma_start(dst, src).then_inc(self.raw_in[u % 2], 16)

    def split_hi(self, act, u, n=UNIT):
        act.wait_ge(self.raw_in[u % 2], 16 * (u // 2 + 1))
        if u >= 2:
            act.wait_ge(*self.used_at(u - 2))
        self.nc.scalar.activation(self.hi(u)[:, 0:n], self.raw(u)[:, 0:n], ACT.Copy).then_inc(self.hi_done, 1)

    def split_lo(self, pool, u, n=UNIT):
        pool.wait_ge(self.hi_done, u + 1)
        self.nc.gpsimd.tensor_tensor(self.lo(u)[:, 0:n], self.raw(u)[:, 0:n], self.hi(u)[:, 0:n].bitcast(F32),
                                     ALU.subtract).then_inc(self.lo_done, 1)

    def ready(self, pe, u):
        pe.wait_ge(self.lo_done, u + 1)


def cols(u, width):
    return u.rearrange("p (k c) -> p k c", c=width)


def product(nc, banks, w_hi, w_lo, x_hi, x_lo, chunks, first=True, last=True):
    ins = None
    for n, k in enumerate(chunks):
        wh, wl = w_hi(k), w_lo(k)
        begin, end = first and n == 0, last and n == len(chunks) - 1
        for i, out in enumerate(banks):
            ins = nc.tensor.matmul(out, wh, x_hi(k, i), start=begin, stop=False)
        for i, out in enumerate(banks):
            ins = nc.tensor.matmul(out, wh, x_lo(k, i), start=False, stop=False)
        for i, out in enumerate(banks):
            ins = nc.tensor.matmul(out, wl, x_hi(k, i), start=False, stop=end)
    return ins


class Phase:
    def __init__(self, nc, name):
        self.nc, self.name, self.ctx, self.sems = nc, name, ExitStack(), []

    def __enter__(self):
        self.in_block = None
        self.ctx.__enter__()
        return self

    def __exit__(self, *a):
        if self.in_block:
            self.in_block.close()
        if self.sems:
            for s in self.sems:
                self.nc.gpsimd.sem_clear(s)
            self.nc.all_engine_barrier()
        return self.ctx.__exit__(*a)

    def sb(self, name, shape, dt=F32):
        return self.ctx.enter_context(self.nc.sbuf_tensor(f"{self.name}_{name}", shape, dt))

    def sem(self, name):
        self.sems.append(self.ctx.enter_context(self.nc.semaphore(f"{self.name}_{name}")))
        return self.sems[-1]

    def block(self):
        self.in_block = ExitStack()
        return self.in_block.enter_context(self.nc.Block())


def phase_modulation(nc, io, mem, dram):
    NP_ = 12
    with Phase(nc, "mod") as ph:
        xin = ph.sb("xin", [P, 3, D])
        ada = ph.sb("ada", [P, 2, KD, 512])
        rows = ph.sb("rows", [P, 6, P])
        cond_silu = ph.sb("cond_silu", [P, KD, 2])
        xout = ph.sb("xout", [P, 2, KD, P])
        consts_in = ph.sem("consts_in")
        rows_in = ph.sem("rows_in")
        x_in = [ph.sem(f"x_in{i}") for i in range(3)]
        ada_in = [ph.sem(f"ada_in{i}") for i in range(2)]
        par_t = ph.sem("params_transposed")
        par_c = ph.sem("params_copied")
        x_t = ph.sem("x_transposed")
        x_c = ph.sem("x_copied")
        x_out = [ph.sem(f"x_out{i}") for i in range(2)]
        silu_done = ph.sem("silu_done")
        part_done = ph.sem("part_done")
        zeroed = ph.sem("zeroed")
        dve_step = ph.sem("dve_step")
        ps, par = mem["psum"], mem["par"]
        blk = ph.block()

        x_src = [io["x_sample"][0, t * P:(t + 1) * P, :] for t in range(8)] + [io["x_prompt"][0]]
        small = [(io["ada_b"].rearrange("l (b p) -> (l b) p", p=P), PA["ada_b"], 48)]
        for n in ("norm_mix_w", "norm_ffn_w", "hy_conv_b", "hy_bias", "ml_conv_b", "ml_norm_w"):
            small.append((io[n].rearrange("l (b p) -> (l b) p", p=P), PA[n], io[n].shape[1] // P))
        small.append((io["final_norm_w"].rearrange("(b p) -> b p", p=P), PA["final_norm_w"], 8))
        conv = [(io["hy_conv_w"].rearrange("l j (b p) -> (l j b) p", p=P), 0, 36),
                (io["ml_conv_w"].rearrange("l j (b p) -> (l j b) p", p=P), 36, 24)]
        taps = io["ffn_conv_w"].rearrange("l y x (b p) -> (l y x b) p", p=P)
        bias = io["ffn_conv_b"].rearrange("l (b p) -> (l b) p", p=P)
        conv += [(io["c"][0].rearrange("(b p) -> b p", p=P), 60, 8), (io["c_ctx"].rearrange("(b p) -> b p", p=P), 68, 8)]
        filt = [(io[n], 76 + i) for i, n in enumerate(("hy_filt_b1", "hy_filt_b2", "hy_filt_b3", "hy_freq"))]
        n_rows = len(small) + len(conv) + len(filt) + 5

        @blk.sync
        def _(sp):
            for dst, src in (("ident", "k_ident"), ("mask", "k_mask"), ("sel", "k_sel")):
                sp.dma_start(mem[dst][:], io[src]).then_inc(consts_in, 16)
            sp.wait_ge(zeroed, 1)
            for src, r, n in small:
                sp.dma_start(rows[r:r + n, 0, :], src).then_inc(rows_in, 16)
            for src, r, n in conv:
                sp.dma_start(rows[r:r + n, 1, :], src).then_inc(rows_in, 16)
            for i in range(4):
                n = FROWS if i < 3 else 66
                sp.dma_start(rows[0:n, 2 + i, :], taps[FROWS * i:FROWS * i + n, :]).then_inc(rows_in, 16)
            sp.dma_start(rows[66:110, 5, :], bias).then_inc(rows_in, 16)
            for src, r in filt:
                sp.dma_start(rows[r:r + 1, 1, 0:64], src).then_inc(rows_in, 16)
            for t in range(NT):
                if t >= 3:
                    sp.wait_ge(x_t, 2 * (t - 2))
                sp.dma_start(xin[:, t % 3, :], x_src[t]).then_inc(x_in[t % 3], 16)
                if t >= 1:
                    sp.wait_ge(x_c, 2 * t)
                    sp.dma_start(dram["xT"].rearrange("k p t -> p k t")[:, :, (t - 1) * P:t * P],
                                 xout[:, (t - 1) % 2]).then_inc(x_out[(t - 1) % 2], 16)
            sp.wait_ge(x_c, 2 * NT)
            sp.dma_start(dram["xT"].rearrange("k p t -> p k t")[:, :, LS:T],
                         xout[:, (NT - 1) % 2]).then_inc(x_out[(NT - 1) % 2], 16)
            for j in range(NP_):
                if j >= 2:
                    sp.wait_ge(part_done, j - 1)
                sp.dma_start(ada[:, j % 2], io["ada_w"][0, :, 512 * j:512 * (j + 1)]
                             .rearrange("(k p) c -> p k c", p=P)).then_inc(ada_in[j % 2], 16)
            sp.wait_ge(x_out[0], 16 * 5)
            sp.wait_ge(x_out[1], 16 * 4)

        @blk.gpsimd
        def _(pool):
            nc.gpsimd.memset(rows[:], 0.0).then_inc(zeroed, 1)

        @blk.tensor
        def _(pe):
            pe.wait_ge(consts_in, 48)
            pe.wait_ge(rows_in, 16 * n_rows)
            for i in range(6):
                nc.tensor.transpose(ps[:, 7 - i // 4, (i % 4) * P:(i % 4 + 1) * P], rows[:, i, :],
                                    mem["ident"][:]).then_inc(par_t, 1)
            for t in range(NT):
                pe.wait_ge(x_in[t % 3], 16 * (t // 3 + 1))
                for half in range(2):
                    n = 2 * t + half
                    if n >= 4:
                        pe.wait_ge(x_c, n - 3)
                    for j in range(4):
                        k = 4 * half + j
                        last = nc.tensor.transpose(ps[:, n % 4, j * P:(j + 1) * P],
                                                   xin[:, t % 3, k * P:(k + 1) * P], mem["ident"][:])
                    last.then_inc(x_t, 1)
            pe.wait_ge(silu_done, 1)
            for j in range(NP_):
                pe.wait_ge(ada_in[j % 2], 16 * (j // 2 + 1))
                for b in range(4):
                    for k in range(KD):
                        last = nc.tensor.matmul(ps[:, 5, 2 * (4 * j + b):2 * (4 * j + b) + 2],
                                                ada[:, j % 2, k, b * P:(b + 1) * P], cond_silu[:, k, :],
                                                start=(k == 0), stop=(k == KD - 1))
                last.then_inc(part_done, 1)

        @blk.scalar
        def _(act):
            act.wait_ge(par_c, 1)
            c0 = PA["cond"]
            nc.scalar.activation(cond_silu[:], par[:, c0:c0 + 16].rearrange("p (j k) -> p k j", j=2), ACT.Silu)\
              .then_inc(silu_done, 1)
            for n in range(2 * NT):
                act.wait_ge(x_t, n + 1)
                if n // 2 >= 2:
                    act.wait_ge(x_out[(n // 2) % 2], 16 * (n // 4))
                nc.scalar.activation(xout[:, (n // 2) % 2, 4 * (n % 2):4 * (n % 2) + 4, :],
                                     ps[:, n % 4, :].rearrange("p (k t) -> p k t", t=P), ACT.Copy).then_inc(x_c, 1)

        @blk.vector
        def _(dve):
            step = Chain(dve, dve_step)
            dve.wait_ge(par_t, 6)
            nc.vector.tensor_copy(par[:, 0:256], ps[:, 7, 0:256]).then_inc(par_c, 1)
            fp = par[:, 256:256 + 4 * FROWS].rearrange("p (i r) -> p i r", r=FROWS)
            nc.vector.tensor_copy(fp[:, 0:2], ps[:, 7, 256:512].rearrange("p (i r) -> p i r", r=P)[:, :, 0:FROWS])\
              .then_inc(par_c, 1)
            nc.vector.tensor_copy(fp[:, 2:4], ps[:, 6, 0:256].rearrange("p (i r) -> p i r", r=P)[:, :, 0:FROWS])\
              .then_inc(par_c, 1)
            dve.wait_ge(par_c, 3)
            dve.wait_ge(part_done, NP_)
            mod = mem["mod"]
            for j in range(2):
                step.do(nc.vector.tensor_tensor(mod[:, :, j], ps[:, 5, j:j + 95:2],
                                                par[:, PA["ada_b"]:PA["ada_b"] + 48], ALU.add))
            for dst, w, blk_at in (("gain_mix", "norm_mix_w", 8), ("gain_ffn", "norm_ffn_w", 32)):
                for j in range(2):
                    step.do(nc.vector.scalar_tensor_tensor(
                        out=mem[dst][:, :, j], in0=mod[:, blk_at:blk_at + 8, j], scalar=1.0,
                        in1=par[:, PA[w]:PA[w] + 8], op0=ALU.add, op1=ALU.mult))


def norm_steps(nc, ph, mem, x, n_out, square_ring, finish):
    sq_ready = ph.sem("squares_ready")
    sq_used = ph.sem("squares_used")
    sum_done = ph.sem("sum_done")
    ms_done = ph.sem("mean_square_done")
    root_done = ph.sem("root_done")
    rstd_done = ph.sem("rstd_done")
    normed = ph.sem("normed")
    normed_used = ph.sem("normed_used")
    ms = ph.sb("ms", [P, T])
    rstd = ph.sb("rstd", [P, T])
    norm_t = ph.sb("norm_t", [P, 2, T])
    ps = mem["psum"]

    def on_act(x_ready):
        act = nc.scalar
        for k in range(KD):
            x_ready(act, k)
            if k >= 2:
                act.wait_ge(sq_used, k - 1)
            act.activation(square_ring[:, k % 2, :], x[:, k, :], ACT.Square).then_inc(sq_ready, 1)
        act.wait_ge(ms_done, 1)
        act.activation(ms[:], ms[:], ACT.Sqrt).then_inc(root_done, 1)
        for k in range(KD):
            act.wait_ge(normed, k + 1)
            finish(act, k, norm_t[:, k % 2, :], normed_used)

    def on_pe():
        pe = nc.tensor
        for k in range(KD):
            pe.wait_ge(sq_ready, k + 1)
            for b in range(NB):
                last = nc.tensor.matmul(ps[:, b, 0:BW], mem["ones"][:], square_ring[:, k % 2, b * BW:(b + 1) * BW],
                                        start=(k == 0), stop=(k == KD - 1))
            last.then_inc(sq_used, 1)
        last_sem = sq_used
        return last_sem

    def on_dve(x_ready):
        dve = nc.vector
        dve.wait_ge(sq_used, KD)
        nc.vector.tensor_scalar(ms[:].rearrange("p (b c) -> p b c", c=BW), ps[:, 0:NB, 0:BW], 1.0 / D, EPS,
                                ALU.mult, ALU.add).then_inc(ms_done, 1)
        dve.wait_ge(root_done, 1)
        nc.vector.reciprocal(rstd[:], ms[:]).then_inc(rstd_done, 1)
        dve.wait_ge(rstd_done, 1)
        for k in range(KD):
            x_ready(dve, k)
            if k >= 2:
                dve.wait_ge(normed_used, k - 1)
            nc.vector.tensor_tensor(norm_t[:, k % 2, :], x[:, k, :], rstd[:], ALU.mult).then_inc(normed, 1)

    return on_act, on_pe, on_dve


def modulated_norm(nc, ph, mem, x, h_hi, h_lo, gain, shift_block):
    square_ring = ph.sb("squares", [P, 2, T])
    full = ph.sb("h_full", [P, 2, T])
    full_done = ph.sem("h_full_done")
    hi_done = ph.sem("h_hi_done")
    lo_done = ph.sem("h_lo_done")

    def finish(act, k, t, used):
        if k >= 2:
            act.wait_ge(lo_done, k - 1)
        for j, (a, b) in enumerate(((0, LS), (LS, T))):
            ins = act.activation(full[:, k % 2, a:b], t[:, a:b], ACT.Identity,
                                 scale=mem[gain][:, k, j:j + 1], bias=mem["mod"][:, shift_block + k, j:j + 1])
            if j == 1:
                ins.then_inc(used, 1)
            else:
                ins.then_inc(full_done, 1)
        act.wait_ge(full_done, k + 1)
        act.wait_ge(used, k + 1)
        act.activation(h_hi[:, k, :], full[:, k % 2, :], ACT.Copy).then_inc(hi_done, 1)

    def on_pool():
        for k in range(KD):
            nc.gpsimd.wait_ge(hi_done, k + 1)
            nc.gpsimd.tensor_tensor(h_lo[:, k, :], full[:, k % 2, :], h_hi[:, k, :].bitcast(F32),
                                    ALU.subtract).then_inc(lo_done, 1)

    return norm_steps(nc, ph, mem, x, None, square_ring, finish) + (on_pool, lo_done)


def phase_project(nc, io, mem, dram):
    with Phase(nc, "proj") as ph:
        h_hi = ph.sb("h_hi", [P, KD, T], F32R)
        h_lo = ph.sb("h_lo", [P, KD, T], F32R)
        ps = mem["psum"]
        with Phase(nc, "norm1") as nh:
            xT = nh.sb("xT", [P, KD, T])
            x_in = [nh.sem(f"x_in{k}") for k in range(KD)]
            on_act, on_pe, on_dve, on_pool, _ = modulated_norm(nc, nh, mem, xT, h_hi, h_lo, "gain_mix", 0)
            blk = nh.block()

            def x_ready(eng, k):
                eng.wait_ge(x_in[k], 16)

            @blk.sync
            def _(sp):
                for k in range(KD):
                    sp.dma_start(xT[:, k, :], dram["xT"][k]).then_inc(x_in[k], 16)

            @blk.scalar
            def _(act):
                on_act(x_ready)

            @blk.tensor
            def _(pe):
                on_pe()

            @blk.vector
            def _(dve):
                on_dve(x_ready)

            @blk.gpsimd
            def _(pool):
                on_pool()

        gw = ph.sb("gate_w", [P, KD, P])
        gh = ph.sb("gate_w_hi", [P, KD, P], F32R)
        gl = ph.sb("gate_w_lo", [P, KD, P], F32R)
        gb = ph.sb("gate_bias", [P, 1])
        pad = ph.sb("pad", [P, 2, T + 4])
        taps = ph.sb("taps", [P, T])
        x1 = ph.sb("x1", [P, CH, T])
        silu = ph.sb("silu", [P, 2, T])
        stage = ph.sb("stage", [P, 2, T])
        gw_zero = ph.sem("gate_w_zero")
        gw_in = ph.sem("gate_w_in")
        gw_hi = ph.sem("gate_w_hi_done")
        gw_lo = ph.sem("gate_w_lo_done")
        gates_done = ph.sem("gates_done")
        full = ph.sem("product_done")
        evac = ph.sem("product_copied")
        conved = ph.sem("conv_done")
        silued = ph.sem("silu_done")
        staged = ph.sem("staged")
        stored = [ph.sem(f"stored{i}") for i in range(2)]
        step_sem = ph.sem("dve_step")
        pads_zero = ph.sem("pads_zero")

        w = io["w_in"][0]
        G = io["w_in"][0, :, GOFF:GOFF + 16].rearrange("(k p) c -> p k c", p=P)
        gate_at = ((0, 0), (8, 32), (4, 64), (12, 96))
        units = [QOFF + 256 * i for i in range(4)] + [VOFF + 256 * i for i in range(4)] + [256 * i for i in range(6)]
        items = [("gates", 0, -1)]
        for u, c0 in enumerate(units):
            if VOFF <= c0 < GOFF:
                items += [("tokens", g, u) for g in range(3)]
            else:
                items += [("block", c0 // P + b, u) for b in range(2)]
        NQ = QOFF // P
        ring = WeightRing(nc, ph, mem, lambda u: (full, 1 + max(n for n, item in enumerate(items) if item[2] == u)))

        def kinds():
            conv = ml = st = 0
            for n, (what, b, u) in enumerate(items):
                yield n, what, b, u, conv, ml, st
                if what == "block":
                    conv += 1
                    ml += b >= NQ
                    st += not (CH <= b < 2 * CH)
                elif what == "tokens":
                    st += 1
        blk = ph.block()

        @blk.sync
        def _(sp):
            sp.wait_ge(gw_zero, 2)
            for c, p in gate_at:
                with nc.allow_non_contiguous_dma(reason="16 gate columns"):
                    sp.dma_start(gw[:, :, p:p + 4], G[:, :, c:c + 4]).then_inc(gw_in, 16)
                    sp.dma_start(gb[p:p + 4, :], io["b_gate"][0, c:c + 4].rearrange("(c o) -> c o", o=1)).then_inc(gw_in, 16)
            done = -1
            for n, what, b, u, conv, ml, st in kinds():
                if u > done:
                    if u == 0:
                        ring.load(sp, 0, w[:, units[0]:units[0] + 256].rearrange("(k p) c -> p k c", p=P), lambda r: cols(r, 256))
                    if u + 1 < len(units):
                        c0 = units[u + 1]
                        ring.load(sp, u + 1, w[:, c0:c0 + 256].rearrange("(k p) c -> p k c", p=P), lambda r: cols(r, 256))
                    done = u
                if what == "gates":
                    continue
                if what == "block" and CH <= b < 2 * CH:
                    continue
                sp.wait_ge(staged, st + 1)
                src = stage[:, st % 2, :]
                if what == "tokens":
                    c0 = units[u]
                    name, off = ("v", c0 - VOFF) if c0 < OOFF else ("o", c0 - OOFF)
                    sp.dma_start(dram[name][3 * b:3 * b + 3, :, off:off + 256].rearrange("t p c -> p t c"),
                                 src[:, 0:768].rearrange("p (t c) -> p t c", c=256)).then_inc(stored[st % 2], 16)
                else:
                    name, j = (("x0", b) if b < CH else ("hv", b - 2 * CH) if b < NQ else
                               ("q", b - NQ) if b < NQ + 4 else ("k", b - NQ - 4))
                    sp.dma_start(dram[name][j], src).then_inc(stored[st % 2], 16)
            n_st = st + 1
            sp.wait_ge(stored[0], 16 * ((n_st + 1) // 2))
            sp.wait_ge(stored[1], 16 * (n_st // 2))

        @blk.gpsimd
        def _(pool):
            nc.gpsimd.memset(gw[:], 0.0).then_inc(gw_zero, 1)
            nc.gpsimd.memset(gb[:], 0.0).then_inc(gw_zero, 1)
            nc.gpsimd.memset(pad[:], 0.0).then_inc(pads_zero, 1)
            pool.wait_ge(gw_hi, 1)
            nc.gpsimd.tensor_tensor(gl[:], gw[:], gh[:].bitcast(F32), ALU.subtract).then_inc(gw_lo, 1)
            done = -1
            ring.split_lo(pool, 0)
            for n, what, b, u, conv, ml, st in kinds():
                if u > done and u + 1 < len(units):
                    ring.split_lo(pool, u + 1)
                done = u
                if what == "block" and b >= NQ:
                    pool.wait_ge(silued, ml + 1)
                    if st >= 2:
                        pool.wait_ge(stored[st % 2], 16 * (st // 2))
                    scale = 1.0 if b < NQ + 4 else HD ** -0.5
                    nc.gpsimd.tensor_scalar(stage[:, st % 2, :], silu[:, ml % 2, :], scale, 0.0, ALU.mult, ALU.add)\
                      .then_inc(staged, 1)

        @blk.scalar
        def _(act):
            act.wait_ge(gw_in, 16 * 8)
            nc.scalar.activation(gh[:], gw[:], ACT.Copy).then_inc(gw_hi, 1)
            ring.split_hi(act, 0)
            done = -1
            prev = None

            def silu_step(b, conv, ml, st):
                act.wait_ge(conved, conv + 1)
                if ml >= 2:
                    act.wait_ge(staged, st - 1)
                nc.scalar.activation(silu[:, ml % 2, :], taps[:], ACT.Silu).then_inc(silued, 1)

            for n, what, b, u, conv, ml, st in kinds():
                if u > done and u + 1 < len(units):
                    ring.split_hi(act, u + 1)
                done = u
                act.wait_ge(full, n + 1)
                slot = ps[:, 3 * (n % 2):3 * (n % 2) + 3, :]
                if what == "gates":
                    nc.scalar.activation(mem["gates"][:].rearrange("p (b c) -> p b c", c=BW), slot[:, :, 0:BW],
                                         ACT.Identity, bias=gb[:, 0:1]).then_inc(evac, 1)
                elif what == "tokens":
                    if st >= 2:
                        act.wait_ge(stored[st % 2], 16 * (st // 2))
                    func = ACT.Copy if units[u] < OOFF else ACT.Sigmoid
                    nc.scalar.activation(stage[:, st % 2, 0:768].rearrange("p (t c) -> p t c", c=256),
                                         slot[:, :, 0:256], func).then_inc(evac, 1)
                    act.wait_ge(evac, n + 1)
                    act.sem_inc(staged, 1)
                else:
                    if conv >= 2:
                        act.wait_ge(conved, conv - 1)
                    else:
                        act.wait_ge(pads_zero, 1)
                    pd = pad[:, conv % 2, :]
                    nc.scalar.activation(pd[:, 1:769].rearrange("p (b c) -> p b c", c=BW), slot[:, 0:2, 0:BW], ACT.Copy)
                    nc.scalar.activation(pd[:, 769:1025], slot[:, 2, 0:256], ACT.Copy)
                    nc.scalar.activation(pd[:, 1027:1155], slot[:, 2, 256:384], ACT.Copy).then_inc(evac, 1)
                    if b >= NQ:
                        silu_step(b, conv, ml, st)

        @blk.vector
        def _(dve):
            step = Chain(dve, step_sem)
            for n, what, b, u, conv, ml, st in kinds():
                if what != "block":
                    continue
                dve.wait_ge(evac, n + 1)
                pd = pad[:, conv % 2, :]
                hy = b < NQ
                if hy:
                    wt, bt, width = PA["hy_conv_w"], PA["hy_conv_b"], 12
                    j = b
                else:
                    wt, bt, width = PA["ml_conv_w"], PA["ml_conv_b"], 8
                    j = b - NQ
                par = mem["par"]
                if hy and b < CH:
                    out, final = stage[:, st % 2, :], staged
                    if st >= 2:
                        dve.wait_ge(stored[st % 2], 16 * (st // 2))
                elif hy and b < 2 * CH:
                    out, final = x1[:, b - CH, :], None
                elif hy:
                    out, final = taps[:], None
                else:
                    out, final = taps[:], None
                    if ml >= 1:
                        dve.wait_ge(silued, ml)
                for k in range(3):
                    wk = par[:, wt + k * width + j:wt + k * width + j + 1]
                    for (a, z, o) in ((0, LS, 0), (LS, T, 2)):
                        src = pd[:, a + o + k:z + o + k]
                        if k == 0:
                            ins = nc.vector.tensor_scalar(out[:, a:z], src, wk, par[:, bt + j:bt + j + 1], ALU.mult, ALU.add)
                        else:
                            ins = nc.vector.scalar_tensor_tensor(out=out[:, a:z], in0=src, scalar=wk, in1=out[:, a:z],
                                                                 op0=ALU.mult, op1=ALU.add)
                        if k == 2 and a:
                            ins.then_inc(conved, 1)
                        else:
                            step.n += 1
                            ins.then_inc(step_sem, 1)
                    if k < 2:
                        dve.wait_ge(step_sem, step.n)
                dve.wait_ge(conved, conv + 1)
                dve.wait_ge(step_sem, step.n)
                if hy and b < CH:
                    dve.sem_inc(staged, 1)
                elif hy and b >= 2 * CH:
                    if st >= 2:
                        dve.wait_ge(stored[st % 2], 16 * (st // 2))
                    nc.vector.tensor_tensor(stage[:, st % 2, :], taps[:], x1[:, b - 2 * CH, :], ALU.mult).then_inc(staged, 1)
                    dve.wait_ge(staged, st + 1)

        @blk.tensor
        def _(pe):
            for n, what, b, u, conv, ml, st in kinds():
                if n >= 2:
                    pe.wait_ge(evac, n - 1)
                slot = ps[:, 3 * (n % 2):3 * (n % 2) + 3, :]
                if what == "gates":
                    pe.wait_ge(gw_lo, 1)
                    product(nc, [slot[:, i, 0:BW] for i in range(NB)], lambda k: gh[:, k, :], lambda k: gl[:, k, :],
                            lambda k, i: h_hi[:, k, i * BW:(i + 1) * BW], lambda k, i: h_lo[:, k, i * BW:(i + 1) * BW],
                            range(KD)).then_inc(full, 1)
                    continue
                ring.ready(pe, u)
                wh, wl = cols(ring.hi(u), 256), cols(ring.lo(u), 256)
                if what == "tokens":
                    for i in range(3):
                        t = 3 * b + i
                        ins = product(nc, [slot[:, i, 0:256]], lambda k: h_hi[:, k, t * P:(t + 1) * P],
                                      lambda k: h_lo[:, k, t * P:(t + 1) * P], lambda k, i: wh[:, k, :], lambda k, i: wl[:, k, :],
                                      range(KD))
                else:
                    c = (b % 2) * P
                    ins = product(nc, [slot[:, i, 0:BW] for i in range(NB)], lambda k: wh[:, k, c:c + P], lambda k: wl[:, k, c:c + P],
                                  lambda k, i: h_hi[:, k, i * BW:(i + 1) * BW], lambda k, i: h_lo[:, k, i * BW:(i + 1) * BW],
                                  range(KD))
                ins.then_inc(full, 1)


TWO_PI_PARTS = (6.28125, 0.0019350051879882812, 3.019916050561733e-07)
ROUND = 12582912.0


def phase_filters(nc, io, mem, dram):
    with Phase(nc, "spec") as outer:
        k_hi = outer.sb("k_hi", [P, 2, NT, DH], F32R)
        k_lo = outer.sb("k_lo", [P, 2, NT, DH], F32R)
        filter_taps(nc, io, mem, k_hi, k_lo)
        transform(nc, io, mem, dram, "kt", k_hi, k_lo, True)


def filter_taps(nc, io, mem, k_hi, k_lo):
    with Phase(nc, "filt") as ph:
        z = ph.sb("z", [33, T])
        w1 = ph.sb("w1", [33, 64])
        w2 = ph.sb("w2", [64, 64])
        w3 = ph.sb("w3", [64, 64])
        w4 = ph.sb("w4", [64, 2 * DH])
        vec = mem["par"][0:64, PA["filter_vec"]:PA["filter_vec"] + 4]
        h = ph.sb("h", [64, T])
        arg = ph.sb("arg", [64, T])
        turns = ph.sb("turns", [64, T])
        decay = ph.sb("decay", [P, NT, DH])
        kf = ph.sb("kf", [P, DH])
        kb = ph.sb("kb", [P, DH])
        absum = ph.sb("absum", [P, 2, DH])
        summed = ph.sb("summed", [P, 2, 2, DH])
        norm = ph.sb("norm", [P, 2 * CH])
        ins_in = ph.sem("inputs_in")
        mm = ph.sem("mlp_product")
        arg_done = ph.sem("arg_done")
        sin_done = ph.sem("sin_done")
        w4_done = ph.sem("w4_product")
        w4_read = ph.sem("w4_read")
        sums = ph.sem("sums")
        k_hi_done = ph.sem("k_hi_done")
        k_lo_done = ph.sem("k_lo_done")
        abs_done = ph.sem("abs_done")
        norm_mm = ph.sem("norm_product")
        step_sem = ph.sem("dve_step")
        ps = mem["psum"]
        blk = ph.block()

        @blk.sync
        def _(sp):
            if True:
                for dst, src in ((z[:], io["k_z"]), (w1[:], io["hy_filt_w1"][0]), (w2[:], io["hy_filt_w2"][0]),
                                 (w3[:], io["hy_filt_w3"][0]), (w4[:], io["hy_filt_w4"][0]),
                                 (decay[:], io["k_decay"].rearrange("t p c -> p t c"))):
                    sp.dma_start(dst, src).then_inc(ins_in, 16)

        @blk.tensor
        def _(pe):
            pe.wait_ge(ins_in, 96)
            for layer, w in enumerate((w1, w2, w3)):
                x = z if layer == 0 else h
                if layer:
                    pe.wait_ge(sin_done, layer)
                for b in range(NB):
                    last = nc.tensor.matmul(ps[0:64, b, 0:BW], w[:], x[:, b * BW:(b + 1) * BW], start=True, stop=True)
                last.then_inc(mm, 1)
            pe.wait_ge(sin_done, 3)
            for j in range(NT):
                if j >= 2:
                    pe.wait_ge(w4_read, 2 * (j - 1))
                s0 = (j // 4) + 256 * (j % 4) if j < 8 else LS
                x = h[:, s0:s0 + 255:2] if j < 8 else h[:, LS:T]
                for half in range(2):
                    last = nc.tensor.matmul(ps[:, 3 + 2 * (j % 2) + half, :], x, w4[:, half * DH:(half + 1) * DH],
                                            start=True, stop=True)
                last.then_inc(w4_done, 1)
            pe.wait_ge(abs_done, 2)
            for j in range(2):
                for c in range(CH):
                    last = nc.tensor.matmul(ps[:, 0, CH * j + c:CH * j + c + 1], absum[:, j, c * P:(c + 1) * P],
                                            mem["ones"][:, 0:1], start=True, stop=True)
            last.then_inc(norm_mm, 1)

        @blk.scalar
        def _(act):
            for layer in range(3):
                act.wait_ge(arg_done, layer + 1)
                nc.scalar.activation(h[:], arg[:], ACT.Sin).then_inc(sin_done, 1)
            for j in range(NT):
                act.wait_ge(sums, 2 * j + 2)
                nc.scalar.activation(k_hi[:, :, j, :], summed[:, j % 2, :, :], ACT.Copy).then_inc(k_hi_done, 1)

        @blk.gpsimd
        def _(pool):
            for j in range(NT):
                pool.wait_ge(k_hi_done, j + 1)
                nc.gpsimd.tensor_tensor(k_lo[:, :, j, :], summed[:, j % 2, :, :], k_hi[:, :, j, :].bitcast(F32),
                                        ALU.subtract).then_inc(k_lo_done, 1)

        @blk.vector
        def _(dve):
            step = Chain(dve, step_sem)
            dve.wait_ge(ins_in, 96)
            for layer in range(3):
                dve.wait_ge(mm, layer + 1)
                step.do(nc.vector.tensor_scalar(arg[:].rearrange("p (b c) -> p b c", c=BW), ps[0:64, 0:NB, 0:BW],
                                                vec[:, layer:layer + 1], vec[:, 3:4], ALU.add, ALU.mult))
                step.do(nc.vector.tensor_scalar(turns[:], arg[:], 1.0 / (2 * math.pi), ROUND, ALU.mult, ALU.add))
                step.do(nc.vector.tensor_scalar_add(turns[:], turns[:], -ROUND))
                for part in TWO_PI_PARTS:
                    step.do(nc.vector.scalar_tensor_tensor(out=arg[:], in0=turns[:], scalar=-part, in1=arg[:],
                                                           op0=ALU.mult, op1=ALU.add))
                nc.vector.tensor_scalar(arg[:], arg[:], 3.1415925, -3.1415925, ALU.min, ALU.max).then_inc(arg_done, 1)
            step.do(nc.vector.memset(absum[:], 0.0))
            for j in range(NT):
                dve.wait_ge(w4_done, j + 1)
                bank = 3 + 2 * (j % 2)
                ins = nc.vector.tensor_tensor(kf[:], ps[:, bank, :], decay[:, j, :], ALU.mult)
                ins.then_inc(w4_read, 1)
                ins = nc.vector.tensor_tensor(kb[:], ps[:, bank + 1, :], decay[:, j, :], ALU.mult)
                ins.then_inc(w4_read, 1)
                dve.wait_ge(w4_read, 2 * j + 2)
                if j in (0, 8):
                    step.do(nc.vector.memset(kb[0:1, :], 0.0))
                if j >= 2:
                    dve.wait_ge(k_lo_done, j - 1)
                nc.vector.tensor_tensor(summed[:, j % 2, 0, :], kf[:], kb[:], ALU.add).then_inc(sums, 1)
                nc.vector.tensor_tensor(summed[:, j % 2, 1, :], kf[:], kb[:], ALU.subtract).then_inc(sums, 1)
                ab = absum[:, j // 8, :]
                dve.wait_ge(sums, 2 * j + 2)
                for tap in (kf, kb):
                    step.do(nc.vector.scalar_tensor_tensor(out=tap[:], in0=tap[:], scalar=-1.0, in1=tap[:],
                                                           op0=ALU.mult, op1=ALU.max))
                    step.do(nc.vector.tensor_tensor(ab, ab, tap[:], ALU.add))
            dve.sem_inc(abs_done, 2)
            dve.wait_ge(norm_mm, 1)
            step.do(nc.vector.tensor_copy(norm[:], ps[:, 0, 0:2 * CH]))
            step.do(nc.vector.reciprocal(mem["filter_gain"][:], norm[:]))


def transform(nc, io, mem, dram, name, x_hi, x_lo, two, pre=None):
    with Phase(nc, name) as ph:
        full = ph.sem("sums_done")
        odd = ph.sem("odd_copied")
        odd_used = ph.sem("odd_used")
        spec_done = ph.sem("spectrum_done")
        row_done = ph.sem("row_done")
        spec_out = [ph.sem(f"spectrum_out{i}") for i in range(2)]
        ring = WeightRing(nc, ph, mem, lambda u: (full, u + 1))
        odd_s = ph.sb("odd", [P, 2, DH])
        spec = ph.sb("spec", [P, 2, 4, DH])
        rows = ph.sb("rows", [1, 2, DH])
        row_out = ph.sem("row_out")
        prompt_done = ph.sem("prompt_done")
        ps = mem["psum"]
        blk = ph.block()

        @blk.sync
        def _(sp):
            for kt in range(4):
                ring.load(sp, kt, io["k_fwd"][kt])
            sp.wait_ge(row_done, 1)
            sp.dma_start(dram[name + "_row"], rows[:]).then_inc(row_out, 16)
            ring.load(sp, 4, io["k_prompt"], lambda r: r[:, 0:4 * P])
            for kt in range(5):
                if kt < 4:
                    sp.wait_ge(spec_done, 4 * (kt + 1))
                else:
                    sp.wait_ge(prompt_done, 2 if two else 1)
                if kt < 4:
                    sp.dma_start(dram[name][kt], spec[:, kt % 2]).then_inc(spec_out[kt % 2], 16)
                else:
                    sp.dma_start(dram[name + "_prompt"], spec[:, 0, 0:2]).then_inc(spec_out[0], 16)
            sp.wait_ge(row_out, 16)
            sp.wait_ge(spec_out[0], 48)
            sp.wait_ge(spec_out[1], 32)

        @blk.gpsimd
        def _(pool):
            for kt in range(4):
                ring.split_lo(pool, kt)
            ring.split_lo(pool, 4, 4 * P)

        @blk.tensor
        def _(pe):
            for kt in range(4):
                ring.ready(pe, kt)
                if kt == 1:
                    pe.wait_ge(row_done, 1)
                if kt >= 2:
                    pe.wait_ge(spec_done, 4 * (kt - 1))
                wh = ring.hi(kt).rearrange("p (t s k) -> p t s k", t=4, s=4)
                wl = ring.lo(kt).rearrange("p (t s k) -> p t s k", t=4, s=4)
                for t in range(4):
                    i, par_ = (t // 2 if two else 0), t % 2
                    last = product(nc, [ps[:, 4 * (kt % 2) + t, :]], lambda s: wh[:, t, s, :], lambda s: wl[:, t, s, :],
                                   lambda s, _: x_hi[:, i, 4 * par_ + s, :], lambda s, _: x_lo[:, i, 4 * par_ + s, :], range(4))
                if two and kt == 0:
                    last = product(nc, [ps[:, 4, :]], lambda s: wh[:, 2, s, :], lambda s: wl[:, 2, s, :],
                                   lambda s, _: x_hi[:, 0, s, :], lambda s, _: x_lo[:, 0, s, :], range(4))
                last.then_inc(full, 1)
            ring.ready(pe, 4)
            pe.wait_ge(spec_done, 12)
            wh = ring.hi(4)[:, 0:4 * P].rearrange("p (t k) -> p t k", t=4)
            wl = ring.lo(4)[:, 0:4 * P].rearrange("p (t k) -> p t k", t=4)
            for t in range(2):
                i = t if two else 0
                last = product(nc, [ps[:, t, :]], lambda s: wh[:, t, :], lambda s: wl[:, t, :],
                               lambda s, _: x_hi[:, i, 8, :], lambda s, _: x_lo[:, i, 8, :], range(1))
            if two:
                last = product(nc, [ps[:, 2, :]], lambda s: wh[:, 1, :], lambda s: wl[:, 1, :],
                               lambda s, _: x_hi[:, 0, 8, :], lambda s, _: x_lo[:, 0, 8, :], range(1))
            last.then_inc(full, 1)

        @blk.scalar
        def _(act):
            ring.split_hi(act, 0)
            for kt in range(4):
                ring.split_hi(act, kt + 1, UNIT if kt < 3 else 4 * P)
                act.wait_ge(full, kt + 1)
                b = 4 * (kt % 2)
                if kt >= 1:
                    act.wait_ge(odd_used, kt)
                if kt == 0:
                    nc.scalar.activation(rows[:, 0, :], ps[0:1, 4 if two else 2, :], ACT.Copy)
                    nc.scalar.activation(rows[:, 1, :], ps[0:1, 3, :], ACT.Copy).then_inc(row_done, 1)
                nc.scalar.activation(odd_s[:, 0:2, :], ps[:, b + 1:b + 4:2, :], ACT.Copy).then_inc(odd, 1)

        @blk.vector
        def _(dve):
            for kt in range(4):
                b = 4 * (kt % 2)
                dve.wait_ge(odd, kt + 1)
                if kt == 0:
                    dve.wait_ge(row_done, 1)
                if kt >= 2:
                    dve.wait_ge(spec_out[kt % 2], 16)
                sp_ = spec[:, kt % 2]
                nc.vector.tensor_tensor(sp_[:, 0, :], ps[:, b, :], odd_s[:, 0, :], ALU.add).then_inc(spec_done, 1)
                nc.vector.tensor_tensor(sp_[:, 1, :], ps[:, b, :], odd_s[:, 0, :], ALU.subtract).then_inc(spec_done, 1)
                nc.vector.tensor_tensor(sp_[:, 2, :], ps[:, b + 2, :], odd_s[:, 1, :], ALU.add).then_inc(spec_done, 1)
                nc.vector.scalar_tensor_tensor(out=sp_[:, 3, :], in0=ps[:, b + 2, :], scalar=-1.0, in1=odd_s[:, 1, :],
                                               op0=ALU.mult, op1=ALU.add).then_inc(spec_done, 1)
                dve.wait_ge(spec_done, 4 * (kt + 1))
                dve.sem_inc(odd_used, 1)
            dve.wait_ge(full, 5)
            dve.wait_ge(spec_out[0], 32)
            nc.vector.tensor_copy(spec[:, 0, 0:2, :], ps[:, 0:2, :]).then_inc(prompt_done, 1)
            if two:
                dve.wait_ge(prompt_done, 1)
                nc.vector.tensor_copy(spec[0:1, 0, 1, :], ps[0:1, 2, :]).then_inc(prompt_done, 1)


def phase_hyena(nc, io, mem, dram):
    ps = mem["psum"]
    with Phase(nc, "vspec") as outer:
        v_hi = outer.sb("v_hi", [P, 1, NT, DH], F32R)
        v_lo = outer.sb("v_lo", [P, 1, NT, DH], F32R)
        with Phase(nc, "vtok") as ph:
            v = ph.sb("v", [P, CH, T])
            v_in = [ph.sem(f"v_in{c}") for c in range(CH)]
            tr = ph.sem("transposed")
            hi = ph.sem("hi")
            lo = ph.sem("lo")
            blk = ph.block()

            @blk.sync
            def _(sp):
                for c in range(CH):
                    sp.dma_start(v[:, c, :], dram["hv"][c]).then_inc(v_in[c], 16)

            @blk.tensor
            def _(pe):
                for j in range(NT):
                    if j >= 4:
                        pe.wait_ge(lo, j - 3)
                    for c in range(CH):
                        if j == 0:
                            pe.wait_ge(v_in[c], 16)
                        s0 = (j // 4) + 256 * (j % 4)
                        src = v[:, c, s0:s0 + 255:2] if j < 8 else v[:, c, LS:T]
                        last = nc.tensor.transpose(ps[:, j % 4, c * P:(c + 1) * P], src, mem["ident"][:])
                    last.then_inc(tr, 1)

            @blk.scalar
            def _(act):
                for j in range(NT):
                    act.wait_ge(tr, j + 1)
                    nc.scalar.activation(v_hi[:, 0, j, :], ps[:, j % 4, :], ACT.Copy).then_inc(hi, 1)

            @blk.vector
            def _(dve):
                for j in range(NT):
                    dve.wait_ge(hi, j + 1)
                    nc.vector.tensor_tensor(v_lo[:, 0, j, :], ps[:, j % 4, :], v_hi[:, 0, j, :].bitcast(F32),
                                            ALU.subtract).then_inc(lo, 1)
        transform(nc, io, mem, dram, "vt", v_hi, v_lo, False)

    with Phase(nc, "iconv") as outer:
        y_hi = outer.sb("y_hi", [P, 4, 4, DH], F32R)
        y_lo = outer.sb("y_lo", [P, 4, 4, DH], F32R)
        yp_hi = outer.sb("yp_hi", [P, 2, DH], F32R)
        yp_lo = outer.sb("yp_lo", [P, 2, DH], F32R)
        spectrum_product(nc, mem, dram, y_hi, y_lo, yp_hi, yp_lo)
        inverse_transform(nc, io, mem, dram, y_hi, y_lo, yp_hi, yp_lo)


def spectrum_product(nc, mem, dram, y_hi, y_lo, yp_hi, yp_lo):
    with Phase(nc, "sprod") as ph:
        ks = ph.sb("ks", [P, 2, 4, DH])
        vs = ph.sb("vs", [P, 2, 4, DH])
        rows = ph.sb("rows", [1, 2, 2, DH])
        t = ph.sb("t", [P, 4, 2, DH])
        q = t[:, 2]
        out = ph.sb("out", [P, 2, 4, DH])
        row_t = t[0:1, :, 0]
        spec_in = [ph.sem(f"spec_in{i}") for i in range(2)]
        rows_in = ph.sem("rows_in")
        step_sem = ph.sem("dve_step")
        read = ph.sem("spectra_read")
        folded = ph.sem("folded")
        hi = ph.sem("hi")
        lo = ph.sem("lo")
        blk = ph.block()

        @blk.sync
        def _(sp):
            sp.dma_start(rows[:, 0], dram["vt_row"]).then_inc(rows_in, 16)
            sp.dma_start(rows[:, 1], dram["kt_row"]).then_inc(rows_in, 16)
            for kt in range(5):
                if kt >= 2:
                    sp.wait_ge(read, kt - 1)
                for dst, name in ((ks, "kt"), (vs, "vt")):
                    if kt < 4:
                        sp.dma_start(dst[:, kt % 2], dram[name][kt]).then_inc(spec_in[kt % 2], 16)
                    else:
                        sp.dma_start(dst[:, 0, 0:2], dram[name + "_prompt"]).then_inc(spec_in[0], 16)

        @blk.vector
        def _(dve):
            step = Chain(dve, step_sem)
            tt = nc.vector.tensor_tensor
            for kt in range(5):
                dve.wait_ge(spec_in[kt % 2], 32 * (kt // 2 + 1))
                i = kt % 2
                w = 2 if kt < 4 else 1
                ka, kb = ks[:, i, 0:w], ks[:, i, w:2 * w]
                va, vb = vs[:, i, 0:w], vs[:, i, w:2 * w]
                step.do(tt(t[:, 0, 0:w], va, ka, ALU.mult))
                step.do(tt(t[:, 1, 0:w], vb, kb, ALU.mult))
                step.do(tt(t[:, 2, 0:w], va, kb, ALU.mult))
                step.do(tt(t[:, 3, 0:w], vb, ka, ALU.mult))
                if kt >= 2:
                    dve.wait_ge(lo, kt - 1)
                o = out[:, kt % 2]
                if kt == 4:
                    step.do(tt(o[:, 0, :], t[:, 0, 0], t[:, 1, 0], ALU.subtract))
                    step.do(tt(o[:, 1, :], t[:, 2, 0], t[:, 3, 0], ALU.add))
                    step.do(nc.vector.tensor_copy(o[0:1, 0:2, :], t[0:1, 0:2, 0, :]))
                    dve.sem_inc(folded, 1)
                    continue
                step.do(tt(q, t[:, 2], t[:, 3], ALU.add))
                if kt == 0:
                    step.do(nc.vector.memset(t[0:1, 1], 0.0))
                step.do(tt(t[:, 0], t[:, 0], t[:, 1], ALU.subtract))
                step.do(tt(o[:, 0, :], t[:, 0, 0], t[:, 0, 1], ALU.add))
                step.do(tt(o[:, 2, :], t[:, 0, 0], t[:, 0, 1], ALU.subtract))
                step.do(tt(o[:, 1, :], q[:, 0], q[:, 1], ALU.subtract))
                step.do(tt(o[:, 3, :], q[:, 0], q[:, 1], ALU.add))
                if kt == 0:
                    dve.wait_ge(rows_in, 32)
                    v, k = rows[:, 0], rows[:, 1]
                    step.do(tt(row_t[:, 0, :], v[:, 0], k[:, 0], ALU.mult))
                    step.do(tt(row_t[:, 1, :], v[:, 1], k[:, 1], ALU.mult))
                    step.do(tt(row_t[:, 2, :], v[:, 0], k[:, 1], ALU.mult))
                    step.do(tt(row_t[:, 3, :], v[:, 1], k[:, 0], ALU.mult))
                    step.do(tt(o[0:1, 1, :], row_t[:, 0], row_t[:, 1], ALU.subtract))
                    step.do(tt(o[0:1, 3, :], row_t[:, 2], row_t[:, 3], ALU.add))
                dve.sem_inc(folded, 1)
                dve.sem_inc(read, 1)

        @blk.scalar
        def _(act):
            for kt in range(5):
                act.wait_ge(folded, kt + 1)
                if kt < 4:
                    nc.scalar.activation(y_hi[:, :, kt, :], out[:, kt % 2], ACT.Copy).then_inc(hi, 1)
                else:
                    nc.scalar.activation(yp_hi[:], out[:, 0, 0:2], ACT.Copy).then_inc(hi, 1)

        @blk.gpsimd
        def _(pool):
            for kt in range(5):
                pool.wait_ge(hi, kt + 1)
                if kt < 4:
                    nc.gpsimd.tensor_tensor(y_lo[:, :, kt, :], out[:, kt % 2], y_hi[:, :, kt, :].bitcast(F32),
                                            ALU.subtract).then_inc(lo, 1)
                else:
                    nc.gpsimd.tensor_tensor(yp_lo[:], out[:, 0, 0:2], yp_hi[:].bitcast(F32), ALU.subtract).then_inc(lo, 1)


def inverse_transform(nc, io, mem, dram, y_hi, y_lo, yp_hi, yp_lo):
    ps = mem["psum"]
    with Phase(nc, "inv") as ph:
        full = ph.sem("product_done")
        ring = WeightRing(nc, ph, mem, lambda u: (full, 4 * (u // 2 + 1)))
        v = ph.sb("v", [P, CH, T])
        x0 = ph.sb("x0", [P, CH, T])
        v_in = [ph.sem(f"v_in{c}") for c in range(CH)]
        bias_done = ph.sem("bias_done")
        summed = ph.sem("summed")
        gated = ph.sem("gated")
        y_out = ph.sem("y_out")
        blk = ph.block()

        @blk.sync
        def _(sp):
            ring.load(sp, 0, io["k_inv"][0])
            ring.load(sp, 1, io["k_inv"][1])
            for c in range(CH):
                sp.dma_start(v[:, c, :], dram["hv"][c]).then_inc(v_in[c], 16)
                sp.dma_start(x0[:, c, :], dram["x0"][c]).then_inc(v_in[c], 16)
            ring.load(sp, 2, io["k_inv"][2])
            ring.load(sp, 3, io["k_inv"][3])
            ring.load(sp, 4, io["k_prompt"], lambda r: r[:, 0:4 * P])
            sp.wait_ge(gated, 12)
            sp.dma_start(dram["y"].rearrange("k p t -> p k t")[:, 0:CH, :], x0[:]).then_inc(y_out, 16)
            sp.wait_ge(y_out, 16)

        @blk.gpsimd
        def _(pool):
            for u in range(5):
                ring.split_lo(pool, u, UNIT if u < 4 else 4 * P)

        @blk.tensor
        def _(pe):
            for par_ in range(2):
                ring.ready(pe, 2 * par_ + 1)
                xh = [ring.hi(2 * par_ + t).rearrange("p (k s) -> p k s", k=4) for t in range(2)]
                xl = [ring.lo(2 * par_ + t).rearrange("p (k s) -> p k s", k=4) for t in range(2)]
                for c in range(CH):
                    n = 4 * par_ + c
                    terms = [(t, k) for t in range(2) for k in range(4)]
                    product(nc, [ps[:, n % 8, :]], lambda a: y_hi[:, 2 * par_ + a[0], a[1], c * P:(c + 1) * P],
                            lambda a: y_lo[:, 2 * par_ + a[0], a[1], c * P:(c + 1) * P],
                            lambda a, _: xh[a[0]][:, a[1], :], lambda a, _: xl[a[0]][:, a[1], :], terms).then_inc(full, 1)
            ring.ready(pe, 4)
            pe.wait_ge(summed, 1)
            xh = ring.hi(4)[:, 0:4 * P].rearrange("p (t k) -> p t k", t=4)
            xl = ring.lo(4)[:, 0:4 * P].rearrange("p (t k) -> p t k", t=4)
            for c in range(CH):
                last = product(nc, [ps[:, 0, c * P:(c + 1) * P]], lambda t: yp_hi[:, t, c * P:(c + 1) * P],
                               lambda t: yp_lo[:, t, c * P:(c + 1) * P], lambda t, _: xh[:, 2 + t, :],
                               lambda t, _: xl[:, 2 + t, :], range(2))
            last.then_inc(full, 1)

        @blk.scalar
        def _(act):
            for u in range(3):
                ring.split_hi(act, u)
            for u in range(3, 5):
                ring.split_hi(act, u, UNIT if u < 4 else 4 * P)

        @blk.vector
        def _(dve):
            par = mem["par"]
            for c in range(CH):
                dve.wait_ge(v_in[c], 32)
                nc.vector.tensor_scalar_mul(v[:, c, :], v[:, c, :], par[:, PA["hy_bias"] + c:PA["hy_bias"] + c + 1])\
                  .then_inc(bias_done, 1)
            dve.wait_ge(bias_done, CH)
            for n in range(12):
                c = n % 4
                dve.wait_ge(full, n + 1 if n < 8 else 9)
                if n < 8:
                    seg = slice(n // 4, LS, 2)
                    src, gain = ps[:, n, :], mem["filter_gain"][:, c:c + 1]
                else:
                    seg = slice(LS, T)
                    src, gain = ps[:, 0, c * P:(c + 1) * P], mem["filter_gain"][:, CH + c:CH + c + 1]
                nc.vector.scalar_tensor_tensor(out=v[:, c, seg], in0=src, scalar=gain, in1=v[:, c, seg],
                                               op0=ALU.mult, op1=ALU.add).then_inc(summed, 1)
                dve.wait_ge(summed, n + 1)
                nc.vector.tensor_tensor(x0[:, c, seg], v[:, c, seg], x0[:, c, seg], ALU.mult).then_inc(gated, 1)


G_SRC, G_INTER, G_FLOOR, G_STATE = range(4)


def gate_rows(nc, io, mem, col, wcb, mrow):
    ps = mem["psum"]
    gates = mem["gates"]
    with Phase(nc, "rows") as ph:
        f = ph.sb("f", [ROWS, T])
        e = ph.sb("e", [ROWS, T])
        u = ph.sb("u", [ROWS, T])
        lnu = ph.sb("lnu", [ROWS, T])
        reset = ph.sb("reset", [ROWS, T])
        b = ph.sb("b", [ROWS, T])
        jump = ph.sb("jump", [ROWS, T])
        r1 = ph.sb("r1", [P, T])
        r2 = ph.sb("r2", [P, T])
        m0 = ph.sb("m0", [ROWS, 1])
        m_in = ph.sb("m_in", [ROWS, NT])
        m_end = ph.sb("m_end", [ROWS, NT])
        wc = ph.sb("wc", [ROWS, NT])
        m_new = ph.sb("m_new", [ROWS, 1])
        ins_in = ph.sem("inputs_in")
        zeroed = ph.sem("zeroed")
        act_step = ph.sem("act_step")
        dve_sem = ph.sem("dve_step")
        lin = ph.sem("log_parts")
        ready = ph.sem("exponents_ready")
        tr = ph.sem("transposed")
        stored = ph.sem("m_stored")
        g, M = r1[0:ROWS, :], mrow
        blk = ph.block()

        @blk.gpsimd
        def _(pool):
            nc.gpsimd.memset(m0[:], 0.0).then_inc(zeroed, 1)

        @blk.sync
        def _(sp):
            sp.wait_ge(zeroed, 1)
            sp.dma_start(reset[:], io["k_reset"]).then_inc(ins_in, 16)
            for d in range(2):
                sp.dma_start(m0[32 * d:32 * d + HEADS, :], io["state_mlstm_m"][0, 0, d].rearrange("(h o) -> h o", o=1))\
                  .then_inc(ins_in, 16)
            sp.wait_ge(ready, 5)
            for d in range(2):
                sp.dma_start(io["new_m"][0, 0, d].rearrange("(h o) -> h o", o=1), m_new[32 * d:32 * d + HEADS, :])\
                  .then_inc(stored, 16)
            sp.wait_ge(stored, 32)

        @blk.scalar
        def _(act):
            step = Chain(act, act_step)
            step.do(nc.scalar.activation(f[:], gates[ROWS:P, :], ACT.Copy))
            step.do(nc.scalar.activation(e[:], gates[ROWS:P, :], ACT.Abs))
            step.do(nc.scalar.activation(e[:], e[:], ACT.Exp, scale=-1.0))
            act.wait_ge(lin, 1)
            step.do(nc.scalar.activation(lnu[:], u[:], ACT.Ln))
            act.wait_ge(ready, 1)
            step.do(nc.scalar.activation(r1[ROWS:P, :], r1[ROWS:P, :], ACT.Exp))
            act.wait_ge(ready, 2)
            step.do(nc.scalar.activation(r2[0:ROWS, :], r2[0:ROWS, :], ACT.Exp, scale=-1.0))
            act.wait_ge(ready, 3)
            step.do(nc.scalar.activation(r2[ROWS:P, :], r2[ROWS:P, :], ACT.Exp))
            act.wait_ge(ready, 4)
            step.do(nc.scalar.activation(wc[:], wc[:], ACT.Exp))

        @blk.vector
        def _(dve):
            step = Chain(dve, dve_sem)
            tt, ts, scan = nc.vector.tensor_tensor, nc.vector.tensor_scalar, nc.vector.tensor_tensor_scan
            step.do(nc.vector.memset(jump[:], 0.0))
            dve.wait_ge(act_step, 3)
            nc.vector.tensor_scalar_add(u[:], e[:], 1.0).then_inc(lin, 1)
            dve.wait_ge(lin, 1)
            step.do(nc.vector.reciprocal(b[:], u[:]))
            step.do(nc.vector.scalar_tensor_tensor(out=e[:], in0=u[:], scalar=1.0, in1=e[:], op0=ALU.subtract, op1=ALU.subtract))
            step.do(tt(e[:], e[:], b[:], ALU.mult))
            dve.wait_ge(act_step, 4)
            step.do(tt(lnu[:], lnu[:], e[:], ALU.subtract))
            step.do(nc.vector.scalar_tensor_tensor(out=f[:], in0=f[:], scalar=0.0, in1=lnu[:], op0=ALU.min, op1=ALU.subtract))
            dve.wait_ge(ins_in, 48)
            F_, B_ = slice(0, 32), slice(32, 64)
            step.do(scan(out=b[F_, :], data0=reset[F_, :], data1=f[F_, :], initial=0.0, op0=ALU.mult, op1=ALU.add))
            step.do(scan(out=b[B_, ::-1], data0=reset[B_, ::-1], data1=f[B_, ::-1], initial=0.0, op0=ALU.mult, op1=ALU.add))
            step.do(tt(g, gates[0:ROWS, :], b[:], ALU.subtract))
            step.do(nc.vector.tensor_copy(jump[F_, P:LS:P], b[F_, P - 1:LS - 1:P]))
            step.do(nc.vector.tensor_copy(jump[B_, P - 1:LS - 1:P], b[B_, P:LS:P]))
            for rows, init in ((slice(0, LS), True), (slice(LS, T), False)):
                a, z = rows.start, rows.stop
                step.do(scan(out=M[F_, a:z], data0=jump[F_, a:z], data1=g[F_, a:z],
                             initial=m0[F_, :] if init else 0.0, op0=ALU.add, op1=ALU.max))
                step.do(scan(out=M[B_, a:z][:, ::-1], data0=jump[B_, a:z][:, ::-1], data1=g[B_, a:z][:, ::-1],
                             initial=m0[B_, :] if init else 0.0, op0=ALU.add, op1=ALU.max))
            step.do(nc.vector.memset(m_in[:], 0.0))
            step.do(nc.vector.tensor_copy(m_in[F_, 0:1], m0[F_, :]))
            step.do(nc.vector.tensor_copy(m_in[B_, 7:8], m0[B_, :]))
            step.do(tt(m_in[F_, 1:8], M[F_, P - 1:LS - 1:P], b[F_, P - 1:LS - 1:P], ALU.add))
            step.do(tt(m_in[B_, 0:7], M[B_, P:LS:P], b[B_, P:LS:P], ALU.add))
            step.do(nc.vector.tensor_copy(m_end[F_, :], M[F_, P - 1:T:P]))
            step.do(nc.vector.tensor_copy(m_end[B_, :], M[B_, 0:T:P]))

            def chunked(a):
                return a.rearrange("p (c t) -> p c t", t=P)

            def spread(a):
                return a.unsqueeze(2).broadcast_to([ROWS, NT, P])

            nc.vector.tensor_tensor(chunked(r1[ROWS:P, :]), spread(m_in[:]), chunked(M[:]), ALU.subtract).then_inc(ready, 1)
            tt(r2[0:ROWS, :], b[:], M[:], ALU.add).then_inc(ready, 1)
            tt(chunked(r2[ROWS:P, :]), chunked(g), spread(m_end[:]), ALU.subtract).then_inc(ready, 1)
            tt(wc[:], m_in[:], m_end[:], ALU.subtract).then_inc(ready, 1)
            step.do(tt(m_new[F_, :], m_end[F_, 8:9], b[F_, T - 1:T], ALU.add))
            step.do(tt(m_new[B_, :], m_end[B_, 8:9], b[B_, LS:LS + 1], ALU.add))
            dve.sem_inc(ready, 1)
            for i in range(5):
                dve.wait_ge(tr, i + 1)
                c0, n = 2 * i, min(4, 18 - 4 * i)
                step.do(nc.vector.tensor_copy(col[:, c0:c0 + n // 2, :, :].rearrange("p c g r -> p (c g r)"), ps[:, i, 0:n * P]))
            dve.wait_ge(tr, 6)
            step.do(nc.vector.tensor_copy(wcb[:].rearrange("p r c -> p (r c)"), ps[:, 5, 0:8 * NT]))

        @blk.tensor
        def _(pe):
            pe.wait_ge(act_step, 8)
            for c in range(NT):
                for j, r in enumerate((r1, r2)):
                    n = 2 * c + j
                    ins = nc.tensor.transpose(ps[:, n // 4, (n % 4) * P:(n % 4 + 1) * P], r[:, c * P:(c + 1) * P], mem["ident"][:])
                    if n % 4 == 3 or n == 17:
                        ins.then_inc(tr, 1)
            for r in range(8):
                ins = nc.tensor.matmul(ps[:, 5, r * NT:(r + 1) * NT], mem["sel"][:, r, :], wc[:], start=True, stop=True)
            ins.then_inc(tr, 1)


def chunk_units():
    units = [(0, 8, 0, True), (1, 8, 0, True)]
    for j in range(8):
        units += [(0, j, 1, j < 7), (1, 7 - j, 1, j < 7)]
    return units


def phase_mlstm(nc, io, mem, dram):
    ps = mem["psum"]
    HC = HEADS
    with Phase(nc, "mlstm") as outer:
        col = outer.sb("col", [P, NT, 4, ROWS])
        wcb = outer.sb("wcb", [P, 8, NT])
        mrow = outer.sb("M", [ROWS, T])
        gate_rows(nc, io, mem, col, wcb, mrow)
        q = outer.sb("q", [P, HC, T])
        k = outer.sb("k", [P, HC, T])
        kn = outer.sb("k_tok", [P, NT, HC, HD])
        v = outer.sb("v", [P, NT, HC, HD])
        hacc = outer.sb("h", [P, NT, HC, HD])
        C = outer.sb("C", [P, 2, 8, HD])
        nvec = outer.sb("n", [P, 2, 8])
        with Phase(nc, "load") as ph:
            c_rows = ph.sb("c_rows", [P, 8, HD])
            n_rows = ph.sb("n_rows", [8, HD])
            q_in = ph.sem("q_in")
            v_in = ph.sem("v_in")
            k_in = ph.sem("k_in")
            c_in = ph.sem("c_in")
            tr = ph.sem("transposed")
            cp = ph.sem("copied")
            cleared = ph.sem("cleared")
            blk = ph.block()

            @blk.sync
            def _(sp):
                sp.dma_start(k[:], dram["k"].rearrange("h p t -> p h t")).then_inc(k_in, 16)
                sp.dma_start(c_rows[:], io["state_mlstm_C"][0, 0].rearrange("d h e k -> e (d h) k")).then_inc(c_in, 16)
                sp.dma_start(n_rows[:], io["state_mlstm_n"][0, 0].rearrange("d h k -> (d h) k")).then_inc(c_in, 16)
                sp.dma_start(q[:], dram["q"].rearrange("h p t -> p h t")).then_inc(q_in, 16)
                sp.dma_start(v[:], dram["v"].rearrange("t p c -> p t c")).then_inc(v_in, 16)
                sp.wait_ge(q_in, 16)
                sp.wait_ge(v_in, 16)

            @blk.gpsimd
            def _(pool):
                nc.gpsimd.memset(hacc[:], 0.0).then_inc(cleared, 1)
                nc.gpsimd.memset(C[:, 0], 0.0).then_inc(cleared, 1)
                nc.gpsimd.memset(nvec[:, 0], 0.0).then_inc(cleared, 1)

            @blk.tensor
            def _(pe):
                pe.wait_ge(k_in, 16)
                for c in range(NT + 3):
                    if c == NT:
                        pe.wait_ge(c_in, 32)
                    if c >= 4:
                        pe.wait_ge(cp, c - 3)
                    if c == NT + 2:
                        nc.tensor.transpose(ps[:, c % 4, 0:8], n_rows[:], mem["ident"][0:8, 0:8]).then_inc(tr, 1)
                        continue
                    for h in range(HC):
                        src = k[:, h, c * P:(c + 1) * P] if c < NT else c_rows[:, 4 * (c - NT) + h, :]
                        last = nc.tensor.transpose(ps[:, c % 4, h * P:(h + 1) * P], src, mem["ident"][:])
                    last.then_inc(tr, 1)

            @blk.scalar
            def _(act):
                for c in range(NT + 3):
                    act.wait_ge(tr, c + 1)
                    if c < NT:
                        dst, src = kn[:, c].rearrange("p h d -> p (h d)"), ps[:, c % 4, :]
                    elif c < NT + 2:
                        i = c - NT
                        dst, src = C[:, 1, 4 * i:4 * i + 4, :].rearrange("p h d -> p (h d)"), ps[:, c % 4, :]
                    else:
                        dst, src = nvec[:, 1, :], ps[:, c % 4, 0:8]
                    nc.scalar.activation(dst, src, ACT.Copy).then_inc(cp, 1)
        chunk_scan(nc, io, mem, q, k, kn, v, hacc, C, nvec, col, wcb, mrow)
        mlstm_output(nc, io, mem, dram, hacc, C, nvec, q)


def chunk_scan(nc, io, mem, q, k, kn, v, hacc, C, nvec, col, wcb, mrow):
    ps = mem["psum"]
    units = chunk_units()
    N = len(units)
    ups = [n for n, un in enumerate(units) if un[3]]
    HC = HEADS

    def updates_before(n):
        return sum(1 for i in ups if i < n)

    def updates_upto_same(n):
        d, c, s, _ = units[n]
        last = [i for i in ups if i < n and units[i][0] == d and units[i][2] == s]
        return updates_before(last[-1]) + 1 if last else 0

    with Phase(nc, "scan") as ph:
        dist = ph.sb("dist", [P, 2, HC, P])
        dec = ph.sb("decay", [P, 2, HC, P])
        prob = ph.sb("prob", [P, 2, HC, P])
        wv = ph.sb("wv", [P, 2, HC, HD])
        inter = ph.sb("inter", [P, 2, HC, HD])
        den = ph.sb("den", [P, HC])
        den2 = ph.sb("den2", [P, HC])
        score = ph.sem("scores_done")
        dist_done = ph.sem("dist_done")
        dec_done = ph.sem("decay_done")
        prob_done = ph.sem("prob_done")
        wv_done = ph.sem("weighted_v_done")
        num_done = ph.sem("numerators_done")
        inter_done = ph.sem("inter_copied")
        num_read = ph.sem("num_read")
        state_mm = ph.sem("state_product_done")
        state_done = ph.sem("state_updated")
        out_done = ph.sem("h_added")
        step_sem = ph.sem("dve_step")
        B_S, B_M, B_N1, B_N2, B_C, B_DEN, B_DN = 0, 2, 3, 4, 5, 6, 7
        blk = ph.block()

        def heads(bank):
            return ps[:, bank, :].rearrange("p (h d) -> p h d", h=HC)

        @blk.tensor
        def _(pe):
            def scores(n):
                d, c, s, up = units[n]
                tok = slice(c * P, (c + 1) * P)
                if n >= 1:
                    pe.wait_ge(dist_done, n)
                for h in range(HC):
                    nc.tensor.matmul(heads(B_M)[:, h, :], mem["sel"][:, 4 * d + h, :], mrow[:, tok], start=True, stop=True)
                if n >= 2:
                    pe.wait_ge(prob_done, n - 1)
                for h in range(HC):
                    ins = nc.tensor.matmul(heads(B_S + n % 2)[:, h, :], k[:, h, tok], q[:, h, tok], start=True, stop=True)
                ins.then_inc(score, 1)

            scores(0)
            for n in range(N):
                d, c, s, up = units[n]
                tok = slice(c * P, (c + 1) * P)
                if n + 1 < N:
                    scores(n + 1)
                pe.wait_ge(state_done, updates_upto_same(n))
                if n >= 1:
                    pe.wait_ge(num_read, n)
                for h in range(HC):
                    nc.tensor.matmul(heads(B_N2)[:, h, :], q[:, h, tok], C[:, s, 4 * d + h, :], start=True, stop=True)
                for h in range(HC):
                    nc.tensor.matmul(ps[:, B_DEN, 4 + h:5 + h], q[:, h, tok], nvec[:, s, 4 * d + h:4 * d + h + 1],
                                     start=True, stop=True)
                pe.wait_ge(prob_done, n + 1)
                for h in range(HC):
                    nc.tensor.matmul(heads(B_N1)[:, h, :], prob[:, n % 2, h, :], v[:, c, h, :], start=True, stop=True)
                for h in range(HC):
                    ins = nc.tensor.matmul(ps[:, B_DEN, h:h + 1], prob[:, n % 2, h, :], mem["ones"][:, 0:1],
                                           start=True, stop=True)
                ins.then_inc(num_done, 1)
                if up:
                    j = updates_before(n)
                    pe.wait_ge(wv_done, j + 1)
                    if j >= 1:
                        pe.wait_ge(state_done, j)
                    for h in range(HC):
                        nc.tensor.matmul(heads(B_C)[:, h, :], kn[:, c, h, :], wv[:, j % 2, h, :], start=True, stop=True)
                    for h in range(HC):
                        r = 32 * d + h
                        ins = nc.tensor.matmul(ps[:, B_DN, h:h + 1], kn[:, c, h, :],
                                               col[:, c, G_STATE, r:r + 1], start=True, stop=True)
                    ins.then_inc(state_mm, 1)

        @blk.gpsimd
        def _(pool):
            for j, n in enumerate(ups):
                d, c, s, up = units[n]
                if j >= 2:
                    pool.wait_ge(state_mm, j - 1)
                w = col[:, c, G_STATE, 32 * d:32 * d + HC].unsqueeze(2).broadcast_to([P, HC, HD])
                nc.gpsimd.tensor_tensor(wv[:, j % 2], v[:, c], w, ALU.mult).then_inc(wv_done, 1)

        @blk.scalar
        def _(act):
            def decay(n):
                act.wait_ge(dist_done, n + 1)
                if n >= 2:
                    act.wait_ge(prob_done, n - 1)
                nc.scalar.activation(dec[:, n % 2], dist[:, n % 2], ACT.Exp, scale=-1.0).then_inc(dec_done, 1)

            decay(0)
            for n in range(N):
                d, c, s, up = units[n]
                if n + 1 < N:
                    decay(n + 1)
                act.wait_ge(num_done, n + 1)
                if n >= 2:
                    act.wait_ge(out_done, n - 1)
                for h in range(HC):
                    ins = nc.scalar.activation(inter[:, n % 2, h, :], heads(B_N2)[:, h, :], ACT.Copy,
                                               scale=col[:, c, G_INTER, 32 * d + h:32 * d + h + 1])
                ins.then_inc(inter_done, 1)

        @blk.vector
        def _(dve):
            step = Chain(dve, step_sem)
            tt, stt = nc.vector.tensor_tensor, nc.vector.scalar_tensor_tensor

            def distance(n):
                d, c, s, up = units[n]
                dve.wait_ge(score, n + 1)
                if n >= 2:
                    dve.wait_ge(dec_done, n - 1)
                for h in range(HC):
                    r = 32 * d + h
                    ins = stt(out=dist[:, n % 2, h, :], in0=heads(B_M)[:, h, :], scalar=col[:, c, G_SRC, r:r + 1],
                              in1=mem["mask"][:, d, :], op0=ALU.subtract, op1=ALU.max)
                ins.then_inc(dist_done, 1)

            distance(0)
            for n in range(N):
                d, c, s, up = units[n]
                rows = slice(32 * d, 32 * d + HC)
                if n + 1 < N:
                    distance(n + 1)
                dve.wait_ge(dec_done, n + 1)
                if n >= 2:
                    dve.wait_ge(num_done, n - 1)
                tt(prob[:, n % 2], heads(B_S + n % 2), dec[:, n % 2], ALU.mult).then_inc(prob_done, 1)
                dve.wait_ge(num_done, n + 1)
                step.do(tt(den2[:], ps[:, B_DEN, 4:8], col[:, c, G_INTER, rows], ALU.mult))
                step.do(tt(den[:], ps[:, B_DEN, 0:4], den2[:], ALU.add))
                step.do(stt(out=den[:], in0=den[:], scalar=-1.0, in1=den[:], op0=ALU.mult, op1=ALU.max))
                step.do(tt(den[:], den[:], col[:, c, G_FLOOR, rows], ALU.max))
                step.do(nc.vector.reciprocal(den[:], den[:]))
                dve.wait_ge(inter_done, n + 1)
                tt(inter[:, n % 2], heads(B_N1), inter[:, n % 2], ALU.add).then_inc(num_read, 1)
                dve.wait_ge(num_read, n + 1)
                for h in range(HC):
                    ins = stt(out=hacc[:, c, h, :], in0=inter[:, n % 2, h, :], scalar=den[:, h:h + 1], in1=hacc[:, c, h, :],
                              op0=ALU.mult, op1=ALU.add)
                ins.then_inc(out_done, 1)
                if up:
                    j = updates_before(n)
                    r0 = 4 * d
                    dve.wait_ge(state_mm, j + 1)
                    for h in range(HC):
                        stt(out=C[:, s, r0 + h, :], in0=C[:, s, r0 + h, :], scalar=wcb[:, r0 + h, c:c + 1],
                            in1=heads(B_C)[:, h, :], op0=ALU.mult, op1=ALU.add)
                    step.do(tt(nvec[:, s, r0:r0 + 4], nvec[:, s, r0:r0 + 4], wcb[:, r0:r0 + 4, c], ALU.mult))
                    tt(nvec[:, s, r0:r0 + 4], nvec[:, s, r0:r0 + 4], ps[:, B_DN, 0:4], ALU.add)\
                        .then_inc(state_done, 1)
                dve.wait_ge(out_done, n + 1)


def mlstm_output(nc, io, mem, dram, hacc, C, nvec, stage):
    ps = mem["psum"]
    HC = HEADS
    with Phase(nc, "mout") as ph:
        sq = ph.sb("sq", [P, HC, HD])
        ss = ph.sb("ss", [P, NT, HC])
        o = ph.sb("o", [P, NT, HC, HD])
        c_out = ph.sb("c_out", [P, 8, HD])
        n_out = ph.sb("n_out", [8, HD])
        o_in = ph.sem("o_in")
        c_tr = ph.sem("state_transposed")
        c_cp = ph.sem("state_copied")
        squares = ph.sem("squares")
        mean = ph.sem("mean_square")
        root = ph.sem("root")
        gated = ph.sem("gated")
        tr = ph.sem("transposed")
        cp = ph.sem("copied")
        step_sem = ph.sem("dve_step")
        stored = ph.sem("stored")
        blk = ph.block()

        @blk.sync
        def _(sp):
            sp.dma_start(o[:], dram["o"].rearrange("t p c -> p t c")).then_inc(o_in, 16)
            sp.wait_ge(c_cp, 3)
            sp.dma_start(io["new_C"][0, 0].rearrange("d h e k -> e (d h) k"), c_out[:]).then_inc(stored, 16)
            sp.dma_start(io["new_n"][0, 0].rearrange("d h k -> (d h) k"), n_out[:]).then_inc(stored, 16)
            sp.wait_ge(cp, NT)
            sp.dma_start(dram["y"].rearrange("k p t -> p k t")[:, CH:KD, :], stage[:]).then_inc(stored, 16)
            sp.wait_ge(stored, 48)

        @blk.tensor
        def _(pe):
            for i in range(2):
                for h in range(HC):
                    ins = nc.tensor.transpose(ps[:, 4 + i, h * P:(h + 1) * P], C[:, 0, 4 * i + h, :], mem["ident"][:])
            nc.tensor.transpose(ps[0:8, 6, 0:P], nvec[:, 0, :], mem["ident"][:]).then_inc(c_tr, 1)
            for t in range(NT):
                pe.wait_ge(gated, t + 1)
                if t >= 4:
                    pe.wait_ge(cp, t - 3)
                for h in range(HC):
                    ins = nc.tensor.transpose(ps[:, t % 4, h * P:(h + 1) * P], hacc[:, t, h, :], mem["ident"][:])
                ins.then_inc(tr, 1)

        @blk.scalar
        def _(act):
            act.wait_ge(c_tr, 1)
            for i in range(2):
                nc.scalar.activation(c_out[:, 4 * i:4 * i + 4, :].rearrange("p h d -> p (h d)"), ps[:, 4 + i, :], ACT.Copy)\
                  .then_inc(c_cp, 1)
            nc.scalar.activation(n_out[:], ps[0:8, 6, 0:P], ACT.Copy).then_inc(c_cp, 1)
            act.wait_ge(mean, 1)
            nc.scalar.activation(ss[:], ss[:], ACT.Sqrt).then_inc(root, 1)
            w0 = PA["ml_norm_w"]
            for t in range(NT):
                act.wait_ge(tr, t + 1)
                for h in range(HC):
                    ins = nc.scalar.activation(stage[:, h, t * P:(t + 1) * P], ps[:, t % 4, h * P:(h + 1) * P], ACT.Copy,
                                               scale=mem["par"][:, w0 + h:w0 + h + 1])
                ins.then_inc(cp, 1)

        @blk.vector
        def _(dve):
            step = Chain(dve, step_sem)
            tt = nc.vector.tensor_tensor
            for t in range(NT):
                step.do(tt(sq[:], hacc[:, t], hacc[:, t], ALU.mult))
                step.do(nc.vector.tensor_reduce(out=ss[:, t, :], in_=sq[:], op=ALU.add, axis=mybir.AxisListType.X))
            nc.vector.tensor_scalar(ss[:], ss[:], 1.0 / HD, EPS, ALU.mult, ALU.add).then_inc(mean, 1)
            dve.wait_ge(root, 1)
            step.do(nc.vector.reciprocal(ss[:], ss[:]))
            dve.wait_ge(o_in, 16)
            for t in range(NT):
                step.do(tt(hacc[:, t], hacc[:, t], ss[:, t, :].unsqueeze(2).broadcast_to([P, HC, HD]), ALU.mult))
                tt(hacc[:, t], hacc[:, t], o[:, t], ALU.mult).then_inc(gated, 1)


GRID_W = 64
GRID_H = LS // GRID_W
PADW = GRID_W + 2
GRID = (GRID_H + 2) * PADW
PADT = GRID + LP + 2
STEPS = JF // 2
TAPS = 9


def slot_banks(ps, n):
    return ps[:, 3 * (n % 2):3 * (n % 2) + 3, :]


def add_gated(nc, ps_slot, x, gate):
    stt = nc.vector.scalar_tensor_tensor
    a = x[:, 0:768].rearrange("p (b c) -> p b c", c=BW)
    stt(out=a, in0=ps_slot[:, 0:2, 0:BW], scalar=gate[:, 0:1], in1=a, op0=ALU.mult, op1=ALU.add)
    stt(out=x[:, 768:LS], in0=ps_slot[:, 2, 0:256], scalar=gate[:, 0:1], in1=x[:, 768:LS], op0=ALU.mult, op1=ALU.add)
    return stt(out=x[:, LS:T], in0=ps_slot[:, 2, 256:BW], scalar=gate[:, 1:2], in1=x[:, LS:T], op0=ALU.mult, op1=ALU.add)


def phase_out(nc, io, mem, dram):
    with Phase(nc, "tail") as outer:
        x = outer.sb("x", [P, KD, T])
        output_projection(nc, io, mem, dram, x)
        with Phase(nc, "ffn") as mid:
            h_hi = mid.sb("h_hi", [P, KD, T], F32R)
            h_lo = mid.sb("h_lo", [P, KD, T], F32R)
            with Phase(nc, "norm2") as nh:
                on_act, on_pe, on_dve, on_pool, _ = modulated_norm(nc, nh, mem, x, h_hi, h_lo, "gain_ffn", 24)
                blk = nh.block()

                @blk.scalar
                def _(act):
                    on_act(lambda eng, k: None)

                @blk.tensor
                def _(pe):
                    on_pe()

                @blk.vector
                def _(dve):
                    on_dve(lambda eng, k: None)

                @blk.gpsimd
                def _(pool):
                    on_pool()
            feed_forward(nc, io, mem, x, h_hi, h_lo)
        final_norm(nc, io, mem, x)


def output_projection(nc, io, mem, dram, x):
    ps = mem["psum"]
    with Phase(nc, "oproj") as ph:
        full = ph.sem("product_done")
        ring = WeightRing(nc, ph, mem, lambda u: (full, 2 * (u + 1)))
        y = ph.sb("y", [P, 2, T])
        y_hi = ph.sb("y_hi", [P, KD, T], F32R)
        y_lo = ph.sb("y_lo", [P, KD, T], F32R)
        y_in = [ph.sem(f"y_in{i}") for i in range(2)]
        x_in = ph.sem("x_in")
        hi = ph.sem("y_hi_done")
        lo = ph.sem("y_lo_done")
        added = ph.sem("added")
        blk = ph.block()
        w = io["w_out"][0]

        @blk.sync
        def _(sp):
            for k in range(KD):
                if k >= 2:
                    sp.wait_ge(lo, k - 1)
                sp.dma_start(y[:, k % 2, :], dram["y"][k]).then_inc(y_in[k % 2], 16)
                if k < 2:
                    ring.load(sp, k, w[:, 256 * k:256 * k + 256].rearrange("(k p) c -> p k c", p=P), lambda r: cols(r, 256))
            sp.dma_start(x[:], dram["xT"].rearrange("k p t -> p k t")).then_inc(x_in, 16)
            for u in range(2, 4):
                ring.load(sp, u, w[:, 256 * u:256 * u + 256].rearrange("(k p) c -> p k c", p=P), lambda r: cols(r, 256))

        @blk.scalar
        def _(act):
            ring.split_hi(act, 0)
            ring.split_hi(act, 1)
            for k in range(KD):
                act.wait_ge(y_in[k % 2], 16 * (k // 2 + 1))
                nc.scalar.activation(y_hi[:, k, :], y[:, k % 2, :], ACT.Copy).then_inc(hi, 1)
            ring.split_hi(act, 2)
            ring.split_hi(act, 3)

        @blk.gpsimd
        def _(pool):
            for u in range(4):
                ring.split_lo(pool, u)

        @blk.vector
        def _(dve):
            for k in range(KD):
                dve.wait_ge(hi, k + 1)
                nc.vector.tensor_tensor(y_lo[:, k, :], y[:, k % 2, :], y_hi[:, k, :].bitcast(F32), ALU.subtract).then_inc(lo, 1)
            dve.wait_ge(x_in, 16)
            for n in range(KD):
                dve.wait_ge(full, n + 1)
                add_gated(nc, slot_banks(ps, n), x[:, n, :], mem["mod"][:, 16 + n, :]).then_inc(added, 1)

        @blk.tensor
        def _(pe):
            for n in range(KD):
                ring.ready(pe, n // 2)
                if n == 0:
                    pe.wait_ge(lo, KD)
                if n >= 2:
                    pe.wait_ge(added, n - 1)
                wh, wl = cols(ring.hi(n // 2), 256), cols(ring.lo(n // 2), 256)
                c = (n % 2) * P
                slot = slot_banks(ps, n)
                product(nc, [slot[:, i, 0:BW] for i in range(NB)], lambda k: wh[:, k, c:c + P], lambda k: wl[:, k, c:c + P],
                        lambda k, i: y_hi[:, k, i * BW:(i + 1) * BW], lambda k, i: y_lo[:, k, i * BW:(i + 1) * BW],
                        range(KD)).then_inc(full, 1)


def feed_forward(nc, io, mem, x, h_hi, h_lo):
    ps, par = mem["psum"], mem["par"]
    up, down = io["ffn_w_up"][0], io["ffn_w_down"][0]
    with Phase(nc, "mlp") as ph:
        pad = ph.sb("pad", [P, 2, PADT])
        acc_a = ph.sb("acc_a", [P, 2, T])
        acc_v = ph.sb("acc_v", [P, 2, T])
        g_hi = ph.sb("g_hi", [P, 2, T], F32R)
        g_lo = ph.sb("g_lo", [P, 2, T], F32R)
        taps = ph.sb("taps", [P, 2, 2, TAPS + 1, 2])
        pads_zero = ph.sem("pads_zero")
        raw_in = [ph.sem(f"weights_loaded{i}") for i in range(2)]
        w_hi_done = ph.sem("weights_hi")
        w_lo_done = ph.sem("weights_lo")
        taps_ready = ph.sem("taps_ready")
        full = ph.sem("product_done")
        evac = ph.sem("product_copied")
        tap0_done = ph.sem("first_tap_done")
        conv_done = ph.sem("conv_done")
        silu_done = ph.sem("silu_done")
        gated = ph.sem("gated")
        g_hi_done = ph.sem("gated_hi")
        g_lo_done = ph.sem("gated_lo")
        added = ph.sem("down_added")
        step_sem = ph.sem("dve_step")
        row_sem = ph.sem("row_step")
        blk = ph.block()

        w_raw, w_hi, w_lo = mem["w_raw"], mem["w_hi"], mem["w_lo"]

        def products(i):
            return 12 * i - 8 if not (isinstance(i, int) and i == 0) else 0

        class Unit:

            def __init__(self, i, odd, kind):
                k = {"a": -1, "d": 0, "v": 1}[kind]
                if isinstance(i, int) and i == 0:
                    self.u, self.slot = {"a": 0, "v": 1}[kind], {"a": 0, "v": 1}[kind]
                else:
                    self.u = 3 * i + k
                    self.slot = (3 * odd + k) % 2
                self.i, self.kind = i, kind
                self.u_even = self.u - self.slot

            def loads(self):
                return 8 * self.u_even + 16

        def load(sp, un):
            if not isinstance(un.u, int) or un.u >= 2:
                sp.wait_ge(w_lo_done, un.u - 1)
            dst = w_raw[:, un.slot, :]
            if un.kind == "d":
                src = down[bass.ds(256 * (un.i - 1), 256), :].rearrange("(j p) c -> p j c", p=P)
                dst = dst.rearrange("p (j c) -> p j c", j=2)
            else:
                src = up[:, bass.ds(256 * un.i + (DFF if un.kind == "v" else 0), 256)].rearrange("(k p) c -> p k c", p=P)
                dst = cols(dst, 256)
            sp.dma_start(dst, src).then_inc(raw_in[un.slot], 16)

        def split_hi(act, un, used):
            act.wait_ge(raw_in[un.slot], un.loads())
            if used is not None:
                act.wait_ge(full, used)
            nc.scalar.activation(w_hi[:, un.slot, :], w_raw[:, un.slot, :], ACT.Copy).then_inc(w_hi_done, 1)

        def split_lo(pool, un):
            pool.wait_ge(w_hi_done, un.u + 1)
            nc.gpsimd.tensor_tensor(w_lo[:, un.slot, :], w_raw[:, un.slot, :], w_hi[:, un.slot, :].bitcast(F32),
                                    ALU.subtract).then_inc(w_lo_done, 1)

        def grid(j, dy, dx):
            return pad[:, j, 0:GRID].rearrange("p (r c) -> p r c", c=PADW)[:, dy:dy + GRID_H, dx:dx + GRID_W]

        def row(j, dx):
            return pad[:, j, GRID + dx:GRID + dx + LP]

        def image(a):
            return a[:, 0:LS].rearrange("p (r c) -> p r c", c=GRID_W)

        def steps(eng, body, last):
            body(0, 0)
            with eng.Fori(0, (STEPS - 1) // 2) as turn:
                body(2 * turn + 1, 1)
                body(2 * turn + 2, 0)
            last(STEPS, 1)

        @blk.sync
        def _(sp):
            def body(i, odd):
                if not isinstance(i, int):
                    load(sp, Unit(i, odd, "a"))
                    load(sp, Unit(i, odd, "d"))
                    load(sp, Unit(i, odd, "v"))
                else:
                    load(sp, Unit(0, 0, "a"))
                    load(sp, Unit(0, 0, "v"))

            def last(i, odd):
                un = Unit(i, odd, "a")
                un.kind = "d"
                load(sp, un)
            steps(sp, body, last)

        @blk.gpsimd
        def _(pool):
            nc.gpsimd.memset(pad[:], 0.0).then_inc(pads_zero, 1)
            view = par[:, PA["ffn_conv_w"]:PA["ffn_conv_w"] + (TAPS + 1) * 2 * JF].rearrange("p (t b) -> p t b", b=2 * JF)

            def fetch_taps(i, odd):
                if not (isinstance(i, int) and i < 2):
                    pool.wait_ge(conv_done, 4 * i - 3)
                for half in range(2):
                    nc.gpsimd.tensor_copy(taps[:, odd, half], view[:, :, bass.ds(2 * i + JF * half, 2)]).then_inc(taps_ready, 1)

            def gated_lo(i, j):
                pool.wait_ge(g_hi_done, 2 * i + j + 1)
                nc.gpsimd.tensor_tensor(g_lo[:, j, :], acc_a[:, j, :], g_hi[:, j, :].bitcast(F32), ALU.subtract)\
                  .then_inc(g_lo_done, 1)

            def body(i, odd):
                if isinstance(i, int):
                    split_lo(pool, Unit(0, 0, "a"))
                    split_lo(pool, Unit(0, 0, "v"))
                    fetch_taps(0, 0)
                else:
                    split_lo(pool, Unit(i, odd, "d"))
                    fetch_taps(i, odd)
                    gated_lo(i - 1, 0)
                    gated_lo(i - 1, 1)
                    split_lo(pool, Unit(i, odd, "v"))
                split_lo(pool, Unit(i + 1, 1 - odd, "a"))

            def last(i, odd):
                gated_lo(i - 1, 0)
                gated_lo(i - 1, 1)
            steps(pool, body, last)

        @blk.scalar
        def _(act):
            def copy_out(i, loc, odd):
                first = isinstance(i, int)
                n = products(i) + (loc if first else (0, 1, 6, 11)[loc])
                slot = ps[:, 3 * (loc % 2):3 * (loc % 2) + 3, :]
                j = loc % 2
                act.wait_ge(full, n + 1)
                if first and loc < 2:
                    act.wait_ge(pads_zero, 1)
                else:
                    act.wait_ge(conv_done, 4 * i + loc - 1)
                g = pad[:, j, 0:GRID].rearrange("p (r c) -> p r c", c=PADW)
                nc.scalar.activation(g[:, 1:13, 1:65].rearrange("p (b r) c -> p b r c", b=2),
                                     slot[:, 0:2, 0:BW].rearrange("p b (r c) -> p b r c", c=GRID_W), ACT.Copy)
                nc.scalar.activation(g[:, 13:17, 1:65], slot[:, 2, 0:256].rearrange("p (r c) -> p r c", c=GRID_W), ACT.Copy)
                nc.scalar.activation(pad[:, j, GRID + 1:GRID + 1 + LP], slot[:, 2, 256:BW], ACT.Copy).then_inc(evac, 1)
                if loc == 0:
                    act.wait_ge(taps_ready, 2 * i + 2)
                act.wait_ge(evac, 4 * i + loc + 1)
                half = loc // 2
                if half == 0:
                    if not first:
                        act.wait_ge(g_lo_done, 2 * i - 1 + j)
                    acc = acc_a[:, j, :]
                else:
                    if not first:
                        act.wait_ge(gated, 2 * i - 1 + j)
                    acc = acc_v[:, j, :]
                tp = taps[:, odd, half, :, j:j + 1]
                nc.scalar.activation(image(acc), grid(j, 0, 0), ACT.Identity, scale=tp[:, 0], bias=tp[:, TAPS])
                nc.scalar.activation(acc[:, LS:T], row(j, 0), ACT.Identity, scale=tp[:, 3], bias=tp[:, TAPS])\
                  .then_inc(tap0_done, 1)

            def silu(i, j):
                act.wait_ge(conv_done, 4 * i + j + 1)
                nc.scalar.activation(acc_a[:, j, :], acc_a[:, j, :], ACT.Silu).then_inc(silu_done, 1)

            def gated_hi(i, j):
                act.wait_ge(gated, 2 * i + j + 1)
                nc.scalar.activation(g_hi[:, j, :], acc_a[:, j, :], ACT.Copy).then_inc(g_hi_done, 1)

            def body(i, odd):
                if isinstance(i, int):
                    split_hi(act, Unit(0, 0, "a"), None)
                    split_hi(act, Unit(0, 0, "v"), None)
                else:
                    split_hi(act, Unit(i, odd, "d"), products(i))
                    gated_hi(i - 1, 0)
                copy_out(i, 0, odd)
                if not isinstance(i, int):
                    gated_hi(i - 1, 1)
                copy_out(i, 1, odd)
                if not isinstance(i, int):
                    split_hi(act, Unit(i, odd, "v"), products(i) + 2)
                silu(i, 0)
                silu(i, 1)
                copy_out(i, 2, odd)
                split_hi(act, Unit(i + 1, 1 - odd, "a"), 2 if isinstance(i, int) else products(i) + 11)
                copy_out(i, 3, odd)

            def last(i, odd):
                gated_hi(i - 1, 0)
                gated_hi(i - 1, 1)
            steps(act, body, last)

        @blk.vector
        def _(dve):
            OWN = 4 * 8

            def tap(i, loc, odd, acc, t):
                j, half = loc % 2, loc // 2
                tp = taps[:, odd, half, :, j:j + 1]
                if t == 1:
                    dve.wait_ge(tap0_done, 4 * i + loc + 1)
                else:
                    dve.wait_ge(step_sem, OWN * i + 8 * loc + t - 1)
                nc.vector.scalar_tensor_tensor(out=image(acc), in0=grid(j, t // 3, t % 3), scalar=tp[:, t], in1=image(acc),
                                               op0=ALU.mult, op1=ALU.add).then_inc(step_sem, 1)
                if t in (1, 2):
                    if t == 2:
                        dve.wait_ge(row_sem, 8 * i + 2 * loc + 1)
                    nc.vector.scalar_tensor_tensor(out=acc[:, LS:T], in0=row(j, t), scalar=tp[:, 3 + t], in1=acc[:, LS:T],
                                                   op0=ALU.mult, op1=ALU.add).then_inc(row_sem, 1)
                if t == TAPS - 1:
                    dve.wait_ge(row_sem, 8 * i + 2 * loc + 2)
                    dve.wait_ge(step_sem, OWN * i + 8 * loc + 8)
                    dve.sem_inc(conv_done, 1)

            def conv(i, loc, odd, acc):
                for t in range(1, TAPS):
                    tap(i, loc, odd, acc, t)

            def down_add(n, cb, slot):
                dve.wait_ge(full, n + 1)
                add_gated(nc, ps[:, 3 * slot:3 * slot + 3, :], x[:, cb, :], mem["mod"][:, 40 + cb, :]).then_inc(added, 1)

            def gate(i, j):
                dve.wait_ge(silu_done, 2 * i + j + 1)
                nc.vector.tensor_tensor(acc_a[:, j, :], acc_a[:, j, :], acc_v[:, j, :], ALU.mult).then_inc(gated, 1)

            def body(i, odd):
                conv(i, 0, odd, acc_a[:, 0, :])
                for loc, acc, cb0, at_ in ((1, acc_a[:, 1, :], 0, 2), (2, acc_v[:, 0, :], 4, 7)):
                    for t in range(1, TAPS):
                        if t <= 4 and not isinstance(i, int):
                            cb = cb0 + t - 1
                            down_add(products(i) + at_ + t - 1, cb, (at_ + t - 1) % 2)
                        tap(i, loc, odd, acc, t)
                gate(i, 0)
                conv(i, 3, odd, acc_v[:, 1, :])
                gate(i, 1)

            def last(i, odd):
                for cb in range(KD):
                    down_add(products(i) + cb, cb, cb % 2)
            dve.sem_inc(added, 1)
            steps(dve, body, last)

        @blk.tensor
        def _(pe):
            def up_product(un, i, loc):
                wh, wl = cols(w_hi[:, un.slot, :], 256), cols(w_lo[:, un.slot, :], 256)
                j = loc % 2
                if j == 0:
                    pe.wait_ge(w_lo_done, un.u + 1)
                slot = ps[:, 3 * j:3 * j + 3, :]
                c = j * P
                product(nc, [slot[:, b, 0:BW] for b in range(NB)], lambda k: wh[:, k, c:c + P], lambda k: wl[:, k, c:c + P],
                        lambda k, b: h_hi[:, k, b * BW:(b + 1) * BW], lambda k, b: h_lo[:, k, b * BW:(b + 1) * BW],
                        range(KD)).then_inc(full, 1)

            def down_product(un, cb, s):
                wh = w_hi[:, un.slot, :].rearrange("p (j c) -> p j c", j=2)
                wl = w_lo[:, un.slot, :].rearrange("p (j c) -> p j c", j=2)
                slot = ps[:, 3 * s:3 * s + 3, :]
                c = cb * P
                product(nc, [slot[:, b, 0:BW] for b in range(NB)], lambda k: wh[:, k, c:c + P], lambda k: wl[:, k, c:c + P],
                        lambda k, b: g_hi[:, k, b * BW:(b + 1) * BW], lambda k, b: g_lo[:, k, b * BW:(b + 1) * BW],
                        range(2)).then_inc(full, 1)

            def sums(i, n):
                pe.wait_ge(added, 8 * i - 8 + n + 1)

            def body(i, odd):
                a, v = Unit(i, odd, "a"), Unit(i, odd, "v")
                if isinstance(i, int):
                    for loc in range(4):
                        if loc >= 2:
                            pe.wait_ge(evac, loc - 1)
                        up_product(a if loc < 2 else v, i, loc)
                    return
                d = Unit(i, odd, "d")
                sums(i, 0)
                pe.wait_ge(evac, 4 * i - 1)
                up_product(a, i, 0)
                pe.wait_ge(evac, 4 * i)
                up_product(a, i, 1)
                pe.wait_ge(w_lo_done, d.u + 1)
                pe.wait_ge(g_lo_done, 2 * i)
                for cb in range(4):
                    if cb < 2:
                        pe.wait_ge(evac, 4 * i + 1 + cb)
                    else:
                        sums(i, cb - 1)
                    down_product(d, cb, cb % 2)
                sums(i, 3)
                up_product(v, i, 2)
                for cb in range(4, 8):
                    if cb == 5:
                        pe.wait_ge(evac, 4 * i + 3)
                    else:
                        sums(i, cb if cb == 4 else cb - 1)
                    down_product(d, cb, (cb + 1) % 2)
                sums(i, 7)
                up_product(v, i, 3)

            def last(i, odd):
                d = Unit(i, odd, "a")
                pe.wait_ge(w_lo_done, d.u + 1)
                pe.wait_ge(g_lo_done, 2 * i)
                pe.wait_ge(evac, 4 * i)
                for cb in range(KD):
                    sums(i, max(cb - 1, 0))
                    down_product(d, cb, cb % 2)
            steps(pe, body, last)


def final_norm(nc, io, mem, x):
    ps, par = mem["psum"], mem["par"]
    with Phase(nc, "final") as ph:
        square_ring = ph.sb("squares", [P, 2, T])
        xn = ph.sb("xn", [P, KD, T])
        y = ph.sb("y", [P, 3, D])
        xn_done = ph.sem("xn_done")
        tr = ph.sem("transposed")
        cp = ph.sem("copied")
        stored = [ph.sem(f"stored{i}") for i in range(3)]

        def finish(act, k, t, used):
            w0 = PA["final_norm_w"] + k
            act.activation(xn[:, k, :], t, ACT.Copy, scale=par[:, w0:w0 + 1]).then_inc(used, 1)

        on_act, on_pe, on_dve = norm_steps(nc, ph, mem, x, None, square_ring, finish)
        used = [s for s in ph.sems if s.name.endswith("normed_used")][0]
        blk = ph.block()

        @blk.sync
        def _(sp):
            for t in range(NT):
                sp.wait_ge(cp, 2 * t + 2)
                dst = io["y_sample"][0, t * P:(t + 1) * P, :] if t < 8 else io["y_prompt"][0]
                sp.dma_start(dst, y[:, t % 3, :]).then_inc(stored[t % 3], 16)
            for i in range(3):
                sp.wait_ge(stored[i], 48)

        @blk.scalar
        def _(act):
            on_act(lambda eng, k: None)
            for n in range(2 * NT):
                t = n // 2
                act.wait_ge(tr, n + 1)
                if t >= 3:
                    act.wait_ge(stored[t % 3], 16 * (t // 3))
                nc.scalar.activation(y[:, t % 3, 512 * (n % 2):512 * (n % 2) + 512], ps[:, n % 8, :], ACT.Copy).then_inc(cp, 1)

        @blk.tensor
        def _(pe):
            on_pe()
            pe.wait_ge(used, KD)
            for n in range(2 * NT):
                t, half = n // 2, n % 2
                if n >= 8:
                    pe.wait_ge(cp, n - 7)
                for j in range(4):
                    last = nc.tensor.transpose(ps[:, n % 8, j * P:(j + 1) * P], xn[:, 4 * half + j, t * P:(t + 1) * P], mem["ident"][:])
                last.then_inc(tr, 1)

        @blk.vector
        def _(dve):
            on_dve(lambda eng, k: None)


OUTS = [("y_prompt", (1, LP, D)), ("y_sample", (1, LS, D)), ("new_C", (1, 1, 2, HEADS, HD, HD)),
        ("new_n", (1, 1, 2, HEADS, HD)), ("new_m", (1, 1, 2, HEADS))]


def build(nc, io, stop=99):
    with ExitStack() as ctx:
        def sb(name, shape, dt=F32):
            return ctx.enter_context(nc.sbuf_tensor(name, shape, dt))

        mem = {"psum": ctx.enter_context(nc.psum_tensor("psum", [P, 8, 512], F32)),
               "par": sb("par", [P, NPAR]), "mod": sb("mod", [P, 48, 2]),
               "gain_mix": sb("gain_mix", [P, KD, 2]), "gain_ffn": sb("gain_ffn", [P, KD, 2]),
               "ident": sb("ident", [P, P]), "ones": sb("ones", [P, P]),
               "filter_gain": sb("filter_gain", [P, 2 * CH]),
               "w_raw": sb("w_raw", [P, 2, UNIT]), "w_hi": sb("w_hi", [P, 2, UNIT], F32R),
               "w_lo": sb("w_lo", [P, 2, UNIT], F32R)}
        dram = {n: nc.dram_tensor(f"scratch_{n}", shape, F32).ap() for n, shape in dict(
            xT=(KD, P, T), x0=(CH, P, T), hv=(CH, P, T), q=(CH, P, T), k=(CH, P, T),
            v=(NT, P, DH), o=(NT, P, DH), y=(KD, P, T),
            kt=(4, P, 4, DH), kt_row=(1, 2, DH), kt_prompt=(P, 2, DH),
            vt=(4, P, 4, DH), vt_row=(1, 2, DH), vt_prompt=(P, 2, DH)).items()}
        phases = [phase_modulation, phase_filters, phase_project, phase_hyena, phase_mlstm]
        with Phase(nc, "init") as ph:
            blk = ph.block()

            @blk.vector
            def _(dve):
                nc.vector.memset(mem["ones"][:], 1.0)
        with Phase(nc, "front") as front:
            mem.update(gates=front.sb("gates", [P, T]), mask=front.sb("mask", [P, 2, P]), sel=front.sb("sel", [ROWS, 8, P]))
            for f in phases[:min(stop, 5)]:
                f(nc, io, mem, dram)
        if stop > 5:
            phase_out(nc, io, mem, dram)
        return mem, dram


def kernel(**inputs):
    import concourse.bacc as bacc
    from concourse.bass_utils import run_bass_kernel_spmd

    nc = bacc.Bacc("TRN2", target_bir_lowering=False, num_devices=1)
    arrays = {n: np.ascontiguousarray(a) for n, a in inputs.items()}
    arrays.update(constants())
    io = {n: nc.dram_tensor(n, a.shape, F32, kind="ExternalInput").ap() for n, a in arrays.items()}
    for n, shape in OUTS:
        io[n] = nc.dram_tensor(n, shape, F32, kind="ExternalOutput").ap()
    build(nc, io)
    r = run_bass_kernel_spmd(nc, [arrays], core_ids=[0])
    return tuple(np.asarray(r.results[0][n]) for n, _ in OUTS)
```

```python
import math
from contextlib import ExitStack

import numpy as np

import concourse.bass as bass
from concourse import mybir

F32 = mybir.dt.float32
F32R = mybir.dt.float32r
ALU = mybir.AluOpType
ACT = mybir.ActivationFunctionType

P = 128
D = 1024
KD = D // P
LS, LP = 1024, 128
T = LS + LP
NB, BW = 3, 384
assert NB * BW == T
DH = 512
CH = DH // P
HEADS, HD = 4, 128
DFF = 2816
JF = DFF // P
NIN = 3 * DH + 4 * DH + 16
QOFF, KOFF, VOFF, OOFF, GOFF = 3 * DH, 4 * DH, 5 * DH, 6 * DH, 7 * DH
W_IN_UNITS = [QOFF + 256 * i for i in range(8)] + [256 * i for i in range(6)]
EPS = 1e-6
UNIT = 2048
NT = T // P
ROWS = 64

PA = {}
at = 0
for name, n in (("ada_b", 48), ("norm_mix_w", 8), ("norm_ffn_w", 8), ("final_norm_w", 8),
                ("hy_conv_b", 12), ("hy_bias", 4), ("ml_conv_b", 8), ("ml_norm_w", 4)):
    PA[name] = at
    at += n
NROW1 = at
PA["hy_conv_w"] = 128
PA["ml_conv_w"] = 128 + 36
PA["cond"] = 128 + 60
PA["filter_vec"] = 128 + 76
PA["ffn_conv_w"] = 256
PA["ffn_conv_b"] = 256 + 9 * 44
NPAR = 256 + 440
FROWS = 110


def lin(start, stop, n):
    step = np.arange(n, dtype=np.float32) / np.float32(n - 1)
    out = np.float32(start) * (np.float32(1) - step) + np.float32(stop) * step
    out[-1] = np.float32(stop)
    return out.astype(np.float32)


def positions(L):
    t = lin(0.0, 1.0, L)[:, None]
    wpos = np.float32(2.0 * math.pi / L) * np.arange(L, dtype=np.float32)[:, None]
    arg = (lin(1e-4, 15, 16)[None, :] * wpos).astype(np.float32).astype(np.float64)
    z = np.concatenate([t, np.cos(arg), -np.sin(arg)], axis=1).astype(np.float32)
    dmin, dmax = math.log(1e-2) / 1.5, math.log(1e-2) / 0.3
    deltas = np.abs(lin(dmin, dmax, DH))
    decay = np.exp((-t * deltas[None, :]).astype(np.float64)).astype(np.float32)
    return z, decay


def constants():
    zs, ds = positions(LS)
    zp, dp = positions(LP)
    zT = np.concatenate([zs, zp], 0).T.copy()
    decay = np.stack([ds[p + 256 * b:p + 256 * (b + 1):2] for p in (0, 1) for b in range(4)] + [dp])
    k = np.arange(512)[None, :]
    s = np.arange(512)[:, None]
    fwd = []
    for p in (0, 1):
        fwd.append(np.cos(2 * np.pi * ((k * (2 * s + p)) % 2048) / 2048))
    for p in (0, 1):
        m = np.sin(2 * np.pi * ((k * (2 * s + p)) % 2048) / 2048)
        m[:, 0] = (-1.0) ** s[:, 0]
        fwd.append(m)
    weight = np.full((512, 1), 2.0 / 2048)
    weight[0] = 1.0 / 2048
    inv = [fwd[0].T * weight, None, fwd[1].T * weight, None]
    for p in (0, 1):
        m = fwd[2 + p].T * (2.0 / 2048)
        inv[2 * p + 1] = m
    f = np.stack(fwd).reshape(4, 4, P, 4, P)
    fwd_units = f.transpose(3, 2, 0, 1, 4).reshape(4, P, UNIT)
    inv_units = np.stack(inv).reshape(4, 4, P, 512).transpose(0, 2, 1, 3).reshape(4, P, UNIT)
    tt = np.arange(P)[:, None]
    kk = np.arange(P)[None, :]
    c = np.cos(2 * np.pi * (tt * kk % 256) / 256)
    sn = np.sin(2 * np.pi * (tt * kk % 256) / 256)
    sn[:, 0] = (-1.0) ** tt[:, 0]
    wc = np.full((P, 1), 2.0 / 256)
    wc[0] = 1.0 / 256
    prompt = np.stack([c, sn, c.T * wc, sn.T * wc], 1).reshape(P, 4 * P)
    ident = np.eye(P)
    i = np.arange(P)
    mask = np.stack([np.where(i[:, None] <= i[None, :], 0.0, 1e30),
                     np.where(i[:, None] >= i[None, :], 0.0, 1e30)], 1)
    sel = np.zeros((ROWS, 8, P))
    for d in range(2):
        for h in range(HEADS):
            sel[32 * d + h, 4 * d + h] = 1.0
    reset = np.ones((ROWS, T))
    reset[0:32, 0::P] = 0.0
    reset[32:64, P - 1::P] = 0.0
    return {n: np.ascontiguousarray(a, dtype=np.float32) for n, a in dict(
        k_z=zT, k_decay=decay, k_fwd=fwd_units, k_inv=inv_units, k_prompt=prompt,
        k_ident=ident, k_mask=mask, k_sel=sel, k_reset=reset).items()}


class Chain:

    def __init__(self, eng, sem):
        self.eng, self.sem, self.n = eng, sem, 0

    def do(self, ins):
        self.n += 1
        ins.then_inc(self.sem, 1)
        self.eng.wait_ge(self.sem, self.n)


class WeightRing:

    def __init__(self, nc, ph, mem, used_at, ahead=0, first=0):
        self.nc, self.mem, self.ahead, self.first = nc, mem, ahead, first
        self.raw_in = [ph.sem(f"weights_loaded{i}") for i in range(2)]
        self.hi_done = ph.sem("weights_hi")
        self.lo_done = ph.sem("weights_lo")
        self.used_at = used_at

    def slot(self, u):
        return (u + self.first) % 2

    def raw(self, u):
        return self.mem["w_raw"][:, self.slot(u), :]

    def hi(self, u):
        return self.mem["w_hi"][:, self.slot(u), :]

    def lo(self, u):
        return self.mem["w_lo"][:, self.slot(u), :]

    def load(self, sp, u, src, view=None):
        if u - 1 > self.ahead:
            sp.wait_ge(self.lo_done, u - 1 - self.ahead)
        dst = self.raw(u) if view is None else view(self.raw(u))
        sp.dma_start(dst, src).then_inc(self.raw_in[self.slot(u)], 16)

    def split_hi(self, act, u, n=UNIT):
        act.wait_ge(self.raw_in[self.slot(u)], 16 * ((u - self.ahead) // 2 + 1))
        if u >= 2:
            act.wait_ge(*self.used_at(u - 2))
        self.nc.scalar.activation(self.hi(u)[:, 0:n], self.raw(u)[:, 0:n], ACT.Copy).then_inc(self.hi_done, 1)

    def split_lo(self, pool, u, n=UNIT):
        pool.wait_ge(self.hi_done, u + 1 - self.ahead)
        self.nc.gpsimd.tensor_tensor(self.lo(u)[:, 0:n], self.raw(u)[:, 0:n], self.hi(u)[:, 0:n].bitcast(F32),
                                     ALU.subtract).then_inc(self.lo_done, 1)

    def ready(self, pe, u):
        if u >= self.ahead:
            pe.wait_ge(self.lo_done, u + 1 - self.ahead)


def load_w_in(sp, ring, io, u):
    c0 = W_IN_UNITS[u]
    ring.load(sp, u, io["w_in"][0, :, c0:c0 + 256].rearrange("(k p) c -> p k c", p=P), lambda r: cols(r, 256))


def load_forward(sp, ring, io, u, at=0):
    if u == 0:
        ring.load(sp, at, io["k_prompt"], lambda r: r[:, 0:4 * P])
    else:
        ring.load(sp, at + u, io["k_fwd"][u - 1])


def forward_width(u):
    return 4 * P if u == 0 else UNIT


def load_w_out(sp, ring, io, u, at=0):
    ring.load(sp, at + u, io["w_out"][0, :, 256 * u:256 * u + 256].rearrange("(k p) c -> p k c", p=P), lambda r: cols(r, 256))


def cols(u, width):
    return u.rearrange("p (k c) -> p k c", c=width)


def product(nc, banks, w_hi, w_lo, x_hi, x_lo, chunks, first=True, last=True):
    ins = None
    for n, k in enumerate(chunks):
        wh, wl = w_hi(k), w_lo(k)
        begin, end = first and n == 0, last and n == len(chunks) - 1
        for i, out in enumerate(banks):
            ins = nc.tensor.matmul(out, wh, x_hi(k, i), start=begin, stop=False)
        for i, out in enumerate(banks):
            ins = nc.tensor.matmul(out, wh, x_lo(k, i), start=False, stop=False)
        for i, out in enumerate(banks):
            ins = nc.tensor.matmul(out, wl, x_hi(k, i), start=False, stop=end)
    return ins


class Phase:
    def __init__(self, nc, name):
        self.nc, self.name, self.ctx, self.sems = nc, name, ExitStack(), []

    def __enter__(self):
        self.in_block = None
        self.ctx.__enter__()
        return self

    def __exit__(self, *a):
        if self.in_block:
            self.in_block.close()
        if self.sems:
            for s in self.sems:
                self.nc.gpsimd.sem_clear(s)
            self.nc.all_engine_barrier()
        return self.ctx.__exit__(*a)

    def sb(self, name, shape, dt=F32):
        return self.ctx.enter_context(self.nc.sbuf_tensor(f"{self.name}_{name}", shape, dt))

    def sem(self, name):
        self.sems.append(self.ctx.enter_context(self.nc.semaphore(f"{self.name}_{name}")))
        return self.sems[-1]

    def block(self):
        self.in_block = ExitStack()
        return self.in_block.enter_context(self.nc.Block())


def norm_steps(nc, ph, mem, x, n_out, square_ring, finish):
    sq_ready = ph.sem("squares_ready")
    sq_used = ph.sem("squares_used")
    sum_done = ph.sem("sum_done")
    ms_done = ph.sem("mean_square_done")
    root_done = ph.sem("root_done")
    rstd_done = ph.sem("rstd_done")
    normed = ph.sem("normed")
    normed_used = ph.sem("normed_used")
    ms = ph.sb("ms", [P, T])
    rstd = ph.sb("rstd", [P, T])
    norm_t = ph.sb("norm_t", [P, 2, T])
    ps = mem["psum"]

    def on_act(x_ready):
        act = nc.scalar
        for k in range(KD):
            x_ready(act, k)
            if k >= 2:
                act.wait_ge(sq_used, k - 1)
            act.activation(square_ring[:, k % 2, :], x[:, k, :], ACT.Square).then_inc(sq_ready, 1)
        act.wait_ge(ms_done, 1)
        act.activation(ms[:], ms[:], ACT.Sqrt).then_inc(root_done, 1)
        for k in range(KD):
            act.wait_ge(normed, k + 1)
            finish(act, k, norm_t[:, k % 2, :], normed_used)

    def on_pe():
        pe = nc.tensor
        for k in range(KD):
            pe.wait_ge(sq_ready, k + 1)
            for b in range(NB):
                last = nc.tensor.matmul(ps[:, b, 0:BW], mem["ones"][:], square_ring[:, k % 2, b * BW:(b + 1) * BW],
                                        start=(k == 0), stop=(k == KD - 1))
            last.then_inc(sq_used, 1)
        last_sem = sq_used
        return last_sem

    def on_dve(x_ready):
        dve = nc.vector
        dve.wait_ge(sq_used, KD)
        nc.vector.tensor_scalar(ms[:].rearrange("p (b c) -> p b c", c=BW), ps[:, 0:NB, 0:BW], 1.0 / D, EPS,
                                ALU.mult, ALU.add).then_inc(ms_done, 1)
        dve.wait_ge(root_done, 1)
        nc.vector.reciprocal(rstd[:], ms[:]).then_inc(rstd_done, 1)
        dve.wait_ge(rstd_done, 1)
        for k in range(KD):
            x_ready(dve, k)
            if k >= 2:
                dve.wait_ge(normed_used, k - 1)
            nc.vector.tensor_tensor(norm_t[:, k % 2, :], x[:, k, :], rstd[:], ALU.mult).then_inc(normed, 1)

    return on_act, on_pe, on_dve


def modulated_norm(nc, ph, mem, x, h_hi, h_lo, gain, shift_block):
    square_ring = ph.sb("squares", [P, 2, T])
    full = ph.sb("h_full", [P, 2, T])
    full_done = ph.sem("h_full_done")
    hi_done = ph.sem("h_hi_done")
    lo_done = ph.sem("h_lo_done")

    def finish(act, k, t, used):
        if k >= 2:
            act.wait_ge(lo_done, k - 1)
        for j, (a, b) in enumerate(((0, LS), (LS, T))):
            ins = act.activation(full[:, k % 2, a:b], t[:, a:b], ACT.Identity,
                                 scale=mem[gain][:, k, j:j + 1], bias=mem["mod"][:, shift_block + k, j:j + 1])
            if j == 1:
                ins.then_inc(used, 1)
            else:
                ins.then_inc(full_done, 1)
        act.wait_ge(full_done, k + 1)
        act.wait_ge(used, k + 1)
        act.activation(h_hi[:, k, :], full[:, k % 2, :], ACT.Copy).then_inc(hi_done, 1)

    def on_pool():
        for k in range(KD):
            nc.gpsimd.wait_ge(hi_done, k + 1)
            nc.gpsimd.tensor_tensor(h_lo[:, k, :], full[:, k % 2, :], h_hi[:, k, :].bitcast(F32),
                                    ALU.subtract).then_inc(lo_done, 1)

    return norm_steps(nc, ph, mem, x, None, square_ring, finish) + (on_pool, lo_done)


def mixing_norm(nc, io, mem, h_hi, h_lo):
    G = NT // 3
    with Phase(nc, "norm1") as ph:
        x = ph.sb("x", [P, NT, D])
        square = ph.sb("square", [P, D])
        sum_sq = ph.sb("sum_sq", [P, NT])
        mean_sq = ph.sb("mean_sq", [P, NT])
        root = ph.sb("root", [P, NT])
        rstd = ph.sb("rstd", [P, NT])
        full = ph.sb("h_full", [P, 4, BW])
        x_in = [ph.sem(f"x_in{t}") for t in range(NT)]
        summed = ph.sem("squares_summed")
        means = ph.sem("mean_squares")
        roots = ph.sem("roots")
        rstds = ph.sem("rstds")
        scaled = ph.sem("rows_scaled")
        turned = ph.sem("chunk_transposed")
        full_done = ph.sem("h_full_done")
        hi_done = ph.sem("h_hi_done")
        lo_done = ph.sem("h_lo_done")
        ps = mem["psum"]
        ring = WeightRing(nc, ph, mem, None)
        blk = ph.block()

        @blk.sync
        def _(sp):
            for t in range(NT):
                sp.dma_start(x[:, t, :], io["x_sample"][0, t * P:(t + 1) * P, :] if t < 8 else io["x_prompt"][0])\
                  .then_inc(x_in[t], 16)
            for u in range(2):
                load_w_in(sp, ring, io, u)

        @blk.scalar
        def _(act):
            for t in range(NT):
                act.wait_ge(x_in[t], 16)
                if t:
                    act.wait_ge(summed, t)
                nc.scalar.activation(square[:], x[:, t, :], ACT.Square, accum_out=sum_sq[:, t:t + 1]).then_inc(summed, 1)
                if t % 3 == 2:
                    g = t // 3
                    act.wait_ge(means, g + 1)
                    nc.scalar.activation(root[:, 3 * g:3 * g + 3], mean_sq[:, 3 * g:3 * g + 3], ACT.Sqrt).then_inc(roots, 1)
            for n in range(G * KD):
                g, k = n // KD, n % KD
                if n in (4, 12):
                    ring.split_hi(act, n // 8)
                act.wait_ge(full_done, n + 1)
                nc.scalar.activation(h_hi[:, k, g * BW:(g + 1) * BW], full[:, n % 4, :], ACT.Copy).then_inc(hi_done, 1)

        def affine(dve, g):
            for k in range(KD):
                n = g * KD + k
                dve.wait_ge(turned, n + 1)
                if n >= 4:
                    dve.wait_ge(lo_done, n - 3)
                parts = ((0, BW, 0),) if g < G - 1 else ((0, BW - LP, 0), (BW - LP, BW, 1))
                for a, b, j in parts:
                    ins = nc.vector.tensor_scalar(full[:, n % 4, a:b], ps[:, n % 8, a:b], mem["gain_mix"][:, k, j:j + 1],
                                                  mem["mod"][:, k, j:j + 1], ALU.mult, ALU.add)
                ins.then_inc(full_done, 1)

        @blk.vector
        def _(dve):
            for g in range(G):
                s = slice(3 * g, 3 * g + 3)
                dve.wait_ge(summed, 3 * g + 3)
                nc.vector.tensor_scalar(mean_sq[:, s], sum_sq[:, s], 1.0 / D, EPS, ALU.mult, ALU.add).then_inc(means, 1)
                dve.wait_ge(roots, g + 1)
                nc.vector.reciprocal(rstd[:, s], root[:, s]).then_inc(rstds, 1)
                dve.wait_ge(rstds, g + 1)
                for t in range(3 * g, 3 * g + 3):
                    nc.vector.tensor_scalar_mul(x[:, t, :], x[:, t, :], rstd[:, t:t + 1]).then_inc(scaled, 1)
            for g in range(G):
                affine(dve, g)

        @blk.tensor
        def _(pe):
            for n in range(G * KD):
                g, k = n // KD, n % KD
                if k == 0:
                    pe.wait_ge(scaled, 3 * g + 3)
                if n >= 8:
                    pe.wait_ge(full_done, n - 7)
                for i in range(3):
                    last = nc.tensor.transpose(ps[:, n % 8, i * P:(i + 1) * P], x[:, 3 * g + i, k * P:(k + 1) * P],
                                               mem["ident"][:])
                last.then_inc(turned, 1)

        @blk.gpsimd
        def _(pool):
            for n in range(G * KD):
                g, k = n // KD, n % KD
                if n in (4, 12):
                    ring.split_lo(pool, n // 8)
                pool.wait_ge(hi_done, n + 1)
                nc.gpsimd.tensor_tensor(h_lo[:, k, g * BW:(g + 1) * BW], full[:, n % 4, :],
                                        h_hi[:, k, g * BW:(g + 1) * BW].bitcast(F32), ALU.subtract).then_inc(lo_done, 1)


def phase_project(nc, io, mem, dram):
    with Phase(nc, "proj") as ph:
        h_hi = ph.sb("h_hi", [P, KD, T], F32R)
        h_lo = ph.sb("h_lo", [P, KD, T], F32R)
        ps = mem["psum"]
        mixing_norm(nc, io, mem, h_hi, h_lo)

        gw = ph.sb("gate_w", [P, KD, P])
        gh = ph.sb("gate_w_hi", [P, KD, P], F32R)
        gl = ph.sb("gate_w_lo", [P, KD, P], F32R)
        gb = ph.sb("gate_bias", [P, 1])
        pad = ph.sb("pad", [P, 2, T + 4])
        taps = ph.sb("taps", [P, T])
        x1 = ph.sb("x1", [P, CH, T])
        silu = ph.sb("silu", [P, 2, T])
        stage = ph.sb("stage", [P, 2, T])
        gw_zero = ph.sem("gate_w_zero")
        gw_in = ph.sem("gate_w_in")
        gw_hi = ph.sem("gate_w_hi_done")
        gw_lo = ph.sem("gate_w_lo_done")
        gates_done = ph.sem("gates_done")
        full = ph.sem("product_done")
        evac = ph.sem("product_copied")
        conved = ph.sem("conv_done")
        silued = ph.sem("silu_done")
        staged = [ph.sem(f"staged{i}") for i in range(2)]
        stored = [ph.sem(f"stored{i}") for i in range(2)]
        step_sem = ph.sem("dve_step")
        pads_zero = ph.sem("pads_zero")

        G = io["w_in"][0, :, GOFF:GOFF + 16].rearrange("(k p) c -> p k c", p=P)
        gate_at = ((0, 0), (8, 32), (4, 64), (12, 96))
        units = W_IN_UNITS
        AFTER = len(units)
        items = [("gates", 0, -1)]
        for u, c0 in enumerate(units):
            if VOFF <= c0 < GOFF:
                items += [("tokens", g, u) for g in range(3)]
            else:
                items += [("block", c0 // P + b, u) for b in range(2)]
        NQ = QOFF // P
        ring = WeightRing(nc, ph, mem, lambda u: (full, 1 + max(n for n, item in enumerate(items) if item[2] == u)), ahead=2)

        def kinds():
            conv = ml = st = 0
            for n, (what, b, u) in enumerate(items):
                yield n, what, b, u, conv, ml, st
                if what == "block":
                    conv += 1
                    ml += b >= NQ
                    st += not (CH <= b < 2 * CH)
                elif what == "tokens":
                    st += 1
        blk = ph.block()

        @blk.sync
        def _(sp):
            sp.wait_ge(gw_zero, 2)
            for c, p in gate_at:
                with nc.allow_non_contiguous_dma(reason="16 gate columns"):
                    sp.dma_start(gw[:, :, p:p + 4], G[:, :, c:c + 4]).then_inc(gw_in, 16)
                    sp.dma_start(gb[p:p + 4, :], io["b_gate"][0, c:c + 4].rearrange("(c o) -> c o", o=1)).then_inc(gw_in, 16)
            done = -1
            for n, what, b, u, conv, ml, st in kinds():
                if u > done:
                    if u + 2 < AFTER:
                        load_w_in(sp, ring, io, u + 2)
                    else:
                        load_forward(sp, ring, io, u + 2 - AFTER, AFTER)
                    done = u
                if what == "gates":
                    continue
                if what == "block" and CH <= b < 2 * CH:
                    continue
                sp.wait_ge(staged[st % 2], st // 2 + 1)
                src = stage[:, st % 2, :]
                if what == "tokens":
                    c0 = units[u]
                    name, off = ("v", c0 - VOFF) if c0 < OOFF else ("o", c0 - OOFF)
                    sp.dma_start(dram[name][3 * b:3 * b + 3, :, off:off + 256].rearrange("t p c -> p t c"),
                                 src[:, 0:768].rearrange("p (t c) -> p t c", c=256)).then_inc(stored[st % 2], 16)
                else:
                    name, j = (("x0", b) if b < CH else ("hv", b - 2 * CH) if b < NQ else
                               ("q", b - NQ) if b < NQ + 4 else ("k", b - NQ - 4))
                    sp.dma_start(dram[name][j], src).then_inc(stored[st % 2], 16)
            n_st = st + 1
            sp.wait_ge(stored[0], 16 * ((n_st + 1) // 2))
            sp.wait_ge(stored[1], 16 * (n_st // 2))

        @blk.gpsimd
        def _(pool):
            nc.gpsimd.memset(gw[:], 0.0).then_inc(gw_zero, 1)
            nc.gpsimd.memset(gb[:], 0.0).then_inc(gw_zero, 1)
            nc.gpsimd.memset(pad[:], 0.0).then_inc(pads_zero, 1)
            pool.wait_ge(gw_hi, 1)
            nc.gpsimd.tensor_tensor(gl[:], gw[:], gh[:].bitcast(F32), ALU.subtract).then_inc(gw_lo, 1)
            done = -1
            for n, what, b, u, conv, ml, st in kinds():
                if u > done and 2 <= u + 1:
                    ring.split_lo(pool, u + 1, UNIT if u + 1 < AFTER else forward_width(0))
                done = u
                if what == "block" and b >= NQ:
                    pool.wait_ge(silued, ml + 1)
                    if st >= 2:
                        pool.wait_ge(stored[st % 2], 16 * (st // 2))
                    scale = 1.0 if b < NQ + 4 else HD ** -0.5
                    nc.gpsimd.tensor_scalar(stage[:, st % 2, :], silu[:, ml % 2, :], scale, 0.0, ALU.mult, ALU.add)\
                      .then_inc(staged[st % 2], 1)
            ring.split_lo(pool, AFTER + 1, forward_width(1))

        @blk.scalar
        def _(act):
            act.wait_ge(gw_in, 16 * 8)
            nc.scalar.activation(gh[:], gw[:], ACT.Copy).then_inc(gw_hi, 1)
            done = -1

            def silu_step(b, conv, ml, st):
                act.wait_ge(conved, conv + 1)
                if ml >= 2:
                    act.wait_ge(staged[st % 2], st // 2)
                nc.scalar.activation(silu[:, ml % 2, :], taps[:], ACT.Silu).then_inc(silued, 1)

            for n, what, b, u, conv, ml, st in kinds():
                if u > done and 2 <= u + 1:
                    ring.split_hi(act, u + 1, UNIT if u + 1 < AFTER else forward_width(0))
                done = u
                act.wait_ge(full, n + 1)
                slot = ps[:, 3 * (n % 2):3 * (n % 2) + 3, :]
                if what == "gates":
                    nc.scalar.activation(mem["gates"][:].rearrange("p (b c) -> p b c", c=BW), slot[:, :, 0:BW],
                                         ACT.Identity, bias=gb[:, 0:1]).then_inc(evac, 1)
                elif what == "tokens":
                    if st >= 2:
                        act.wait_ge(stored[st % 2], 16 * (st // 2))
                    func = ACT.Copy if units[u] < OOFF else ACT.Sigmoid
                    nc.scalar.activation(stage[:, st % 2, 0:768].rearrange("p (t c) -> p t c", c=256),
                                         slot[:, :, 0:256], func).then_inc(evac, 1)
                    act.wait_ge(evac, n + 1)
                    act.sem_inc(staged[st % 2], 1)
                else:
                    if conv >= 2:
                        act.wait_ge(conved, conv - 1)
                    else:
                        act.wait_ge(pads_zero, 1)
                    pd = pad[:, conv % 2, :]
                    nc.scalar.activation(pd[:, 1:769].rearrange("p (b c) -> p b c", c=BW), slot[:, 0:2, 0:BW], ACT.Copy)
                    nc.scalar.activation(pd[:, 769:1025], slot[:, 2, 0:256], ACT.Copy)
                    nc.scalar.activation(pd[:, 1027:1155], slot[:, 2, 256:384], ACT.Copy).then_inc(evac, 1)
                    if b >= NQ:
                        silu_step(b, conv, ml, st)
            ring.split_hi(act, AFTER + 1, forward_width(1))

        @blk.vector
        def _(dve):
            step = Chain(dve, step_sem)
            for n, what, b, u, conv, ml, st in kinds():
                if what != "block":
                    continue
                dve.wait_ge(evac, n + 1)
                pd = pad[:, conv % 2, :]
                hy = b < NQ
                if hy:
                    wt, bt, width = PA["hy_conv_w"], PA["hy_conv_b"], 12
                    j = b
                else:
                    wt, bt, width = PA["ml_conv_w"], PA["ml_conv_b"], 8
                    j = b - NQ
                par = mem["par"]
                if hy and b < CH:
                    out, final = stage[:, st % 2, :], staged
                    if st >= 2:
                        dve.wait_ge(stored[st % 2], 16 * (st // 2))
                elif hy and b < 2 * CH:
                    out, final = x1[:, b - CH, :], None
                elif hy:
                    out, final = taps[:], None
                else:
                    out, final = taps[:], None
                    if ml >= 1:
                        dve.wait_ge(silued, ml)
                for k in range(3):
                    wk = par[:, wt + k * width + j:wt + k * width + j + 1]
                    for (a, z, o) in ((0, LS, 0), (LS, T, 2)):
                        src = pd[:, a + o + k:z + o + k]
                        if k == 0:
                            ins = nc.vector.tensor_scalar(out[:, a:z], src, wk, par[:, bt + j:bt + j + 1], ALU.mult, ALU.add)
                        else:
                            ins = nc.vector.scalar_tensor_tensor(out=out[:, a:z], in0=src, scalar=wk, in1=out[:, a:z],
                                                                 op0=ALU.mult, op1=ALU.add)
                        if k == 2 and a:
                            ins.then_inc(conved, 1)
                        else:
                            step.n += 1
                            ins.then_inc(step_sem, 1)
                    if k < 2:
                        dve.wait_ge(step_sem, step.n)
                dve.wait_ge(conved, conv + 1)
                dve.wait_ge(step_sem, step.n)
                if hy and b < CH:
                    dve.sem_inc(staged[st % 2], 1)
                elif hy and b >= 2 * CH:
                    if st >= 2:
                        dve.wait_ge(stored[st % 2], 16 * (st // 2))
                    nc.vector.tensor_tensor(stage[:, st % 2, :], taps[:], x1[:, b - 2 * CH, :], ALU.mult).then_inc(staged[st % 2], 1)
                    dve.wait_ge(staged[st % 2], st // 2 + 1)

        @blk.tensor
        def _(pe):
            for n, what, b, u, conv, ml, st in kinds():
                if n >= 2:
                    pe.wait_ge(evac, n - 1)
                slot = ps[:, 3 * (n % 2):3 * (n % 2) + 3, :]
                if what == "gates":
                    pe.wait_ge(gw_lo, 1)
                    product(nc, [slot[:, i, 0:BW] for i in range(NB)], lambda k: gh[:, k, :], lambda k: gl[:, k, :],
                            lambda k, i: h_hi[:, k, i * BW:(i + 1) * BW], lambda k, i: h_lo[:, k, i * BW:(i + 1) * BW],
                            range(KD)).then_inc(full, 1)
                    continue
                ring.ready(pe, u)
                wh, wl = cols(ring.hi(u), 256), cols(ring.lo(u), 256)
                if what == "tokens":
                    for i in range(3):
                        t = 3 * b + i
                        ins = product(nc, [slot[:, i, 0:256]], lambda k: h_hi[:, k, t * P:(t + 1) * P],
                                      lambda k: h_lo[:, k, t * P:(t + 1) * P], lambda k, i: wh[:, k, :], lambda k, i: wl[:, k, :],
                                      range(KD))
                else:
                    c = (b % 2) * P
                    ins = product(nc, [slot[:, i, 0:BW] for i in range(NB)], lambda k: wh[:, k, c:c + P], lambda k: wl[:, k, c:c + P],
                                  lambda k, i: h_hi[:, k, i * BW:(i + 1) * BW], lambda k, i: h_lo[:, k, i * BW:(i + 1) * BW],
                                  range(KD))
                ins.then_inc(full, 1)


TWO_PI_PARTS = (6.28125, 0.0019350051879882812, 3.019916050561733e-07)
ROUND = 12582912.0


def phase_filters(nc, io, mem, dram):
    with Phase(nc, "spec") as outer:
        k_hi = outer.sb("k_hi", [P, 2, NT, DH], F32R)
        k_lo = outer.sb("k_lo", [P, 2, NT, DH], F32R)
        modulation_and_taps(nc, io, mem, k_hi, k_lo)
        filter_spectra(nc, io, mem, dram, k_hi, k_lo)


def modulation_and_taps(nc, io, mem, k_hi, k_lo):
    PARTS, AW, RING = 24, 512, 3
    HK = KD // 2
    BLOCKS = 6 * KD
    SHARED = 6
    SHARE = 1216
    with Phase(nc, "filt") as ph:
        rows = ph.sb("rows", [P, 6, P])
        cond_silu = ph.sb("cond_silu", [P, KD, 2])
        cond_hi = ph.sb("cond_hi", [P, KD, 2], F32R)
        cond_wide = ph.sb("cond_wide", [P, KD, P])
        cond = ph.sb("cond", [P, KD, P], F32R)
        ada_more = ph.sb("ada_more", [P, RING - 2, UNIT])
        part_rows = ph.sb("part_rows", [4, 2, AW])
        mod_rows = ph.sb("mod_rows", [BLOCKS, 4, P])
        w1 = ph.sb("w1", [33, 64])
        w2 = ph.sb("w2", [64, 64])
        w3 = ph.sb("w3", [64, 64])
        w4 = ph.sb("w4", [64, 2 * DH])
        vec = mem["par"][0:64, PA["filter_vec"]:PA["filter_vec"] + 4]
        h = ph.sb("h", [64, T])
        z = h[0:33, :]
        h_hi = ph.sb("h_hi", [64, T], F32R)
        h_lo = ph.sb("h_lo", [64, T], F32R)
        w4_hi, w4_lo = k_hi[0:64, :, NT - 1, :], k_lo[0:64, :, NT - 1, :]
        scratch = ph.sb("scratch", [P, 2, T])
        arg, turns = scratch[0:64, 0, :], scratch[0:64, 1, :]
        summed = scratch[:, :, 0:2 * DH].rearrange("p r (i c) -> p r i c", i=2)
        decay = ph.sb("decay", [P, 2, DH])
        taps = ph.sb("taps", [P, 2, 2, DH])
        size = ph.sb("size", [P, 2, 2, DH])
        absum = ph.sb("absum", [P, 2, 2, DH])
        norm = ph.sb("norm", [P, 2 * CH])
        zeroed = ph.sem("zeroed")
        ident_in = ph.sem("ident_in")
        rows_in = ph.sem("rows_in")
        rows1_in = ph.sem("rows1_in")
        mlp_in = ph.sem("mlp_inputs_in")
        decay_in = [ph.sem(f"decay_in{i}") for i in range(2)]
        ada_in = [ph.sem(f"ada_in{i}") for i in range(RING)]
        par_t = ph.sem("params_transposed")
        par_c = ph.sem("params_copied")
        silu_done = ph.sem("silu_done")
        cond_zero = ph.sem("conditions_zeroed")
        cond_hi_done = ph.sem("conditions_hi")
        cond_placed = ph.sem("conditions_placed")
        cond_ready = ph.sem("conditions_ready")
        part_copied = ph.sem("part_copied")
        part_moved = [ph.sem(f"part_moved{i}") for i in range(2)]
        mod_turned = ph.sem("mod_transposed")
        ada_hi = ph.sem("ada_hi")
        ada_lo = ph.sem("ada_lo")
        ada_lo_share = ph.sem("ada_lo_share")
        part_done = ph.sem("part_done")
        mm = ph.sem("mlp_product")
        arg_done = ph.sem("arg_done")
        sin_done = ph.sem("sin_done")
        w4_split = ph.sem("w4_split")
        h_split = ph.sem("h_split")
        w4_done = ph.sem("w4_product")
        tapped = ph.sem("taps_done")
        edge = ph.sem("edge_cleared")
        sums = ph.sem("sums")
        k_hi_done = ph.sem("k_hi_done")
        k_lo_done = ph.sem("k_lo_done")
        sized = ph.sem("sizes_done")
        absum_zero = ph.sem("absum_zero")
        accumulated = ph.sem("sizes_accumulated")
        norm_mm = ph.sem("norm_product")
        step_sem = ph.sem("dve_step")
        ps, par = mem["psum"], mem["par"]
        ADA_BANK = 6
        row_place = {1: (4, 0), 0: (5, 0), 2: (5, 1), 3: (5, 2), 4: (5, 3), 5: (3, 0)}
        raw = [mem["w_raw"][:, i, :] for i in range(2)] + [ada_more[:, i, :] for i in range(RING - 2)]

        small = [(io["ada_b"].rearrange("l (b p) -> (l b) p", p=P), PA["ada_b"], 48)]
        for n in ("norm_mix_w", "norm_ffn_w", "hy_conv_b", "hy_bias", "ml_conv_b", "ml_norm_w"):
            small.append((io[n].rearrange("l (b p) -> (l b) p", p=P), PA[n], io[n].shape[1] // P))
        small.append((io["final_norm_w"].rearrange("(b p) -> b p", p=P), PA["final_norm_w"], 8))
        conv = [(io["hy_conv_w"].rearrange("l j (b p) -> (l j b) p", p=P), 0, 36),
                (io["ml_conv_w"].rearrange("l j (b p) -> (l j b) p", p=P), 36, 24)]
        conv += [(io["c"][0].rearrange("(b p) -> b p", p=P), 60, 8), (io["c_ctx"].rearrange("(b p) -> b p", p=P), 68, 8)]
        ffn_taps = io["ffn_conv_w"].rearrange("l y x (b p) -> (l y x b) p", p=P)
        ffn_bias = io["ffn_conv_b"].rearrange("l (b p) -> (l b) p", p=P)
        filt = [(io[n], 76 + i) for i, n in enumerate(("hy_filt_b1", "hy_filt_b2", "hy_filt_b3", "hy_freq"))]
        n_rows = len(small) + 5

        sizes = [2, 2, 2] + [2] * NT
        part_at = [range(sum(sizes[:i]), sum(sizes[:i + 1])) for i in range(len(sizes))]
        assert sum(sizes) == PARTS

        def split_ada_hi(act, p):
            act.wait_ge(ada_in[p % RING], 16 * (p // RING + 1))
            if p >= 2:
                act.wait_ge(part_done, p - 1)
            nc.scalar.activation(mem["w_hi"][:, p % 2, :], raw[p % RING], ACT.Copy).then_inc(ada_hi, 1)

        def split_ada_lo(eng, p, a, b, done):
            eng.wait_ge(ada_hi, p + 1)
            eng.tensor_tensor(mem["w_lo"][:, p % 2, a:b], raw[p % RING][:, a:b], mem["w_hi"][:, p % 2, a:b].bitcast(F32),
                              ALU.subtract).then_inc(done, 1)

        blk = ph.block()

        @blk.sync
        def _(sp):
            sp.dma_start(mem["ident"][:], io["k_ident"]).then_inc(ident_in, 16)
            for dst, src in ((z, io["k_z"]), (w1[:], io["hy_filt_w1"][0]), (w2[:], io["hy_filt_w2"][0]),
                             (w3[:], io["hy_filt_w3"][0]), (w4[:], io["hy_filt_w4"][0])):
                sp.dma_start(dst, src).then_inc(mlp_in, 16)
            for p in range(PARTS):
                if p >= RING:
                    sp.wait_ge(ada_lo, p - RING + 1)
                if p - RING >= SHARED:
                    sp.wait_ge(ada_lo_share, p - RING - SHARED + 1)
                r0, c0 = HK * P * (p % 2), AW * (p // 2)
                sp.dma_start(cols(raw[p % RING], AW), io["ada_w"][0, r0:r0 + HK * P, c0:c0 + AW]
                             .rearrange("(k p) c -> p k c", p=P)).then_inc(ada_in[p % RING], 16)

        @blk.gpsimd
        def _(pool):
            nc.gpsimd.memset(rows[:], 0.0).then_inc(zeroed, 1)
            nc.gpsimd.memset(cond_wide[:], 0.0).then_inc(cond_zero, 1)
            pool.wait_ge(cond_zero, 1)
            nc.gpsimd.memset(absum[:], 0.0).then_inc(absum_zero, 1)
            pool.wait_ge(cond_hi_done, 1)
            nc.gpsimd.tensor_copy(cond_wide[:, :, 0:2], cond_hi[:].bitcast(F32)).then_inc(cond_placed, 1)
            nc.gpsimd.tensor_tensor(cond_wide[:, :, 2:4], cond_silu[:], cond_hi[:].bitcast(F32), ALU.subtract)\
              .then_inc(cond_placed, 1)
            for group, parts in enumerate(part_at):
                j = group - 3
                if j == 0:
                    pool.wait_ge(w4_split, 1)
                    nc.gpsimd.tensor_tensor(w4_lo, w4[:].rearrange("p (i c) -> p i c", i=2), w4_hi.bitcast(F32),
                                            ALU.subtract).then_inc(w4_split, 1)
                for p in parts:
                    split_ada_lo(nc.gpsimd, p, 0, UNIT if p < SHARED else SHARE, ada_lo)
                if j >= 0:
                    pool.wait_ge(k_hi_done, j + 1)
                    nc.gpsimd.tensor_tensor(k_lo[:, :, j, :], summed[:, j % 2, :, :], k_hi[:, :, j, :].bitcast(F32),
                                            ALU.subtract).then_inc(k_lo_done, 1)

        @blk.tensor
        def _(pe):
            def mlp_layer(layer):
                x = z if layer == 0 else h
                for b in range(NB):
                    last = nc.tensor.matmul(ps[0:64, b, 0:BW], (w1, w2, w3)[layer][:], x[:, b * BW:(b + 1) * BW],
                                            start=True, stop=True)
                last.then_inc(mm, 1)

            def ada_parts(group):
                for p in part_at[group]:
                    pe.wait_ge(ada_lo, p + 1)
                    if p >= SHARED:
                        pe.wait_ge(ada_lo_share, p - SHARED + 1)
                    q = p // 2
                    if p % 2 == 0 and q >= 2:
                        pe.wait_ge(part_copied, q - 1)
                    for k in range(HK * (p % 2), HK * (p % 2) + HK):
                        for n, w in enumerate((mem["w_hi"], mem["w_lo"])):
                            last = nc.tensor.matmul(ps[:, ADA_BANK + q % 2, :], cond[:, k, :], cols(w[:, p % 2, :], AW)[:, k % HK, :],
                                                    start=(k + n == 0), stop=(k + n == KD))
                    last.then_inc(part_done, 1)

            pe.wait_ge(ident_in, 16)
            pe.wait_ge(rows1_in, 16 * 8)
            for i in (1, 0, 2, 3, 4, 5):
                if i == 0:
                    pe.wait_ge(rows_in, 16 * n_rows)
                bank, at_ = row_place[i]
                nc.tensor.transpose(ps[:, bank, at_ * P:(at_ + 1) * P], rows[:, i, :], mem["ident"][:]).then_inc(par_t, 1)
                if i == 1:
                    pe.wait_ge(mlp_in, 80)
                    mlp_layer(0)
            pe.wait_ge(cond_ready, 1)
            ada_parts(0)
            for layer in range(1, 3):
                pe.wait_ge(sin_done, layer)
                mlp_layer(layer)
                ada_parts(layer)
            pe.wait_ge(h_split, 2)
            pe.wait_ge(w4_split, 2)
            pe.wait_ge(par_c, 4)
            for j in range(NT):
                if j >= 2:
                    pe.wait_ge(tapped, 2 * (j - 1))
                s0 = (j // 4) + 256 * (j % 4) if j < 8 else LS
                at_ = slice(s0, s0 + 255, 2) if j < 8 else slice(LS, T)
                last = product(nc, [ps[:, 2 * (j % 2) + half, :] for half in range(2)], lambda k: h_hi[:, at_], lambda k: h_lo[:, at_],
                               lambda k, i: w4_hi[:, i, :], lambda k, i: w4_lo[:, i, :], range(1))
                last.then_inc(w4_done, 1)
                if j >= 1:
                    ada_parts(2 + j)
            ada_parts(2 + NT)
            pe.wait_ge(accumulated, NT)
            for j in range(2):
                for c in range(CH):
                    for half in range(2):
                        last = nc.tensor.matmul(ps[:, 4, CH * j + c:CH * j + c + 1], absum[:, j, half, c * P:(c + 1) * P],
                                                mem["ones"][:, 0:1], start=(half == 0), stop=(half == 1))
            last.then_inc(norm_mm, 1)
            for i in range(2):
                pe.wait_ge(part_moved[i], 16 * PARTS)
            for j in range(4):
                last = nc.tensor.transpose(ps[:, 5, BLOCKS * j:BLOCKS * (j + 1)], mod_rows[:, j, :],
                                           mem["ident"][0:BLOCKS, 0:BLOCKS])
            last.then_inc(mod_turned, 1)

        @blk.scalar
        def _(act):
            act.wait_ge(zeroed, 1)
            first = [(rows[r:r + n, 1, :], src) for src, r, n in conv]
            first += [(rows[r:r + 1, 1, 0:64], src) for src, r in filt]
            for dst, src in first:
                act.dma_start(dst, src).then_inc(rows1_in, 16)
            loads = [(rows[r:r + n, 0, :], src) for src, r, n in small]
            for i in range(4):
                n = FROWS if i < 3 else 66
                loads.append((rows[0:n, 2 + i, :], ffn_taps[FROWS * i:FROWS * i + n, :]))
            loads.append((rows[66:110, 5, :], ffn_bias))
            for dst, src in loads:
                act.dma_start(dst, src).then_inc(rows_in, 16)
            for j in range(2):
                act.dma_start(decay[:, j, :], io["k_decay"][j]).then_inc(decay_in[j], 16)
            split_ada_hi(act, 0)
            act.wait_ge(par_c, 1)
            c0 = PA["cond"]
            nc.scalar.activation(cond_silu[:], par[:, c0:c0 + 16].rearrange("p (j k) -> p k j", j=2), ACT.Silu)\
              .then_inc(silu_done, 1)
            act.wait_ge(silu_done, 1)
            nc.scalar.activation(cond_hi[:], cond_silu[:], ACT.Copy).then_inc(cond_hi_done, 1)
            split_ada_hi(act, 1)
            act.wait_ge(mlp_in, 80)
            nc.scalar.activation(w4_hi, w4[:].rearrange("p (i c) -> p i c", i=2), ACT.Copy).then_inc(w4_split, 1)
            act.wait_ge(cond_placed, 2)
            nc.scalar.activation(cond[:], cond_wide[:], ACT.Copy).then_inc(cond_ready, 1)

            def move_part(q):
                act.wait_ge(part_done, 2 * q + 2)
                if q >= 2:
                    act.wait_ge(part_moved[q % 2], 64 * (q // 2))
                nc.scalar.activation(part_rows[:, q % 2, :], ps[0:4, ADA_BANK + q % 2, :], ACT.Copy).then_inc(part_copied, 1)
                act.wait_ge(part_copied, q + 1)
                for b in range(4):
                    act.dma_start(mod_rows[4 * q + b:4 * q + b + 1, :, :], part_rows[:, q % 2, b * P:(b + 1) * P])\
                      .then_inc(part_moved[q % 2], 16)

            for layer in range(3):
                for p in part_at[layer]:
                    if p >= 2:
                        split_ada_hi(act, p)
                    if p >= 2 and p % 2:
                        move_part((p - 3) // 2)
                act.wait_ge(arg_done, layer + 1)
                nc.scalar.activation(h[:], arg, ACT.Sin).then_inc(sin_done, 1)
            act.wait_ge(sin_done, 3)
            nc.scalar.activation(h_hi[:], h[:], ACT.Copy).then_inc(h_split, 1)
            for j in range(NT):
                for p in part_at[3 + j]:
                    split_ada_hi(act, p)
                    if p % 2:
                        move_part((p - 3) // 2)
                act.wait_ge(tapped, 2 * j + 2)
                act.wait_ge(edge, 1 + j // 8)
                if j >= 2:
                    act.wait_ge(accumulated, j - 1)
                nc.scalar.activation(size[:, j % 2], taps[:, j % 2], ACT.Abs).then_inc(sized, 1)
                act.wait_ge(sums, 2 * j + 2)
                nc.scalar.activation(k_hi[:, :, j, :], summed[:, j % 2, :, :], ACT.Copy).then_inc(k_hi_done, 1)
                if j + 2 < NT:
                    act.dma_start(decay[:, j % 2, :], io["k_decay"][j + 2]).then_inc(decay_in[j % 2], 16)
            move_part(PARTS // 2 - 1)

        def mlp_argument(dve, step, layer):
            dve.wait_ge(mm, layer + 1)
            step.do(nc.vector.tensor_scalar(arg.rearrange("p (b c) -> p b c", c=BW), ps[0:64, 0:NB, 0:BW],
                                            vec[:, layer:layer + 1], vec[:, 3:4], ALU.add, ALU.mult))
            step.do(nc.vector.tensor_scalar(turns, arg, 1.0 / (2 * math.pi), ROUND, ALU.mult, ALU.add))
            step.do(nc.vector.tensor_scalar_add(turns, turns, -ROUND))
            for part in TWO_PI_PARTS:
                step.do(nc.vector.scalar_tensor_tensor(out=arg, in0=turns, scalar=-part, in1=arg,
                                                       op0=ALU.mult, op1=ALU.add))
            nc.vector.tensor_scalar(arg, arg, 3.1415925, -3.1415925, ALU.min, ALU.max).then_inc(arg_done, 1)

        @blk.vector
        def _(dve):
            step = Chain(dve, step_sem)
            dve.wait_ge(par_t, 1)
            nc.vector.tensor_copy(par[:, 128:256], ps[:, 4, 0:P]).then_inc(par_c, 1)
            dve.wait_ge(par_c, 1)
            mlp_argument(dve, step, 0)
            dve.wait_ge(par_t, 6)
            nc.vector.tensor_copy(par[:, 0:P], ps[:, 5, 0:P]).then_inc(par_c, 1)
            fp = par[:, 256:256 + 4 * FROWS].rearrange("p (i r) -> p i r", r=FROWS)
            nc.vector.tensor_copy(fp[:, 0:3], ps[:, 5, P:4 * P].rearrange("p (i r) -> p i r", r=P)[:, :, 0:FROWS])\
              .then_inc(par_c, 1)
            nc.vector.tensor_copy(fp[:, 3], ps[:, 3, 0:FROWS]).then_inc(par_c, 1)
            dve.wait_ge(par_c, 4)
            for layer in range(1, 3):
                mlp_argument(dve, step, layer)

            dve.wait_ge(h_split, 1)
            nc.vector.tensor_tensor(h_lo[:], h[:], h_hi[:].bitcast(F32), ALU.subtract).then_inc(h_split, 1)

            def accumulate(j):
                dve.wait_ge(sized, j + 1)
                dve.wait_ge(accumulated, j) if j else dve.wait_ge(absum_zero, 1)
                nc.vector.tensor_tensor(absum[:, j // 8], absum[:, j // 8], size[:, j % 2], ALU.add).then_inc(accumulated, 1)

            for j in range(NT):
                i, bank = j % 2, 2 * (j % 2)
                dve.wait_ge(w4_done, j + 1)
                dve.wait_ge(decay_in[i], 16 * (j // 2 + 1))
                if j >= 2:
                    dve.wait_ge(sized, j - 1)
                for half in range(2):
                    nc.vector.tensor_tensor(taps[:, i, half], ps[:, bank + half, :], decay[:, i, :], ALU.mult)\
                      .then_inc(tapped, 1)
                dve.wait_ge(tapped, 2 * j + 2)
                if j in (0, 8):
                    nc.vector.memset(taps[0:1, i, 1, :], 0.0).then_inc(edge, 1)
                    dve.wait_ge(edge, 1 + j // 8)
                if j >= 2:
                    dve.wait_ge(k_lo_done, j - 1)
                nc.vector.tensor_tensor(summed[:, i, 0, :], taps[:, i, 0], taps[:, i, 1], ALU.add).then_inc(sums, 1)
                nc.vector.tensor_tensor(summed[:, i, 1, :], taps[:, i, 0], taps[:, i, 1], ALU.subtract).then_inc(sums, 1)
                if j >= 1:
                    accumulate(j - 1)
                for p in part_at[3 + j]:
                    if p >= SHARED:
                        split_ada_lo(nc.vector, p, SHARE, UNIT, ada_lo_share)
            accumulate(NT - 1)
            dve.wait_ge(norm_mm, 1)
            step.do(nc.vector.tensor_copy(norm[:], ps[:, 4, 0:2 * CH]))
            step.do(nc.vector.reciprocal(mem["filter_gain"][:], norm[:]))
            dve.wait_ge(mod_turned, 1)
            mod = mem["mod"]
            W = BLOCKS
            for j in range(2):
                step.do(nc.vector.tensor_copy(mod[:, :, j], ps[:, 5, (2 + j) * W:(3 + j) * W]))
                step.do(nc.vector.tensor_tensor(mod[:, :, j], ps[:, 5, j * W:(j + 1) * W], mod[:, :, j], ALU.add))
                step.do(nc.vector.tensor_tensor(mod[:, :, j], mod[:, :, j], par[:, PA["ada_b"]:PA["ada_b"] + W], ALU.add))
            for dst, w, blk_at in (("gain_mix", "norm_mix_w", 8), ("gain_ffn", "norm_ffn_w", 32)):
                for j in range(2):
                    step.do(nc.vector.scalar_tensor_tensor(
                        out=mem[dst][:, :, j], in0=mod[:, blk_at:blk_at + 8, j], scalar=1.0,
                        in1=par[:, PA[w]:PA[w] + 8], op0=ALU.add, op1=ALU.mult))


def transform_products(nc, pe, mem, ring, x_hi, x_lo, two, full, prompt_read, row_done, banks_read):
    ps = mem["psum"]

    def sums(bank, w, blocks, i, tokens):
        pairs = list(zip(blocks, tokens))
        return product(nc, [ps[:, bank, :]], lambda a: w[0][:, a[0], :], lambda a: w[1][:, a[0], :],
                       lambda a, _: x_hi[:, i, a[1], :], lambda a, _: x_lo[:, i, a[1], :], pairs)

    for u in range(5):
        ring.ready(pe, u)
        w = [half.rearrange("p (b k) -> p b k", k=P) for half in (ring.hi(u), ring.lo(u))]
        if u == 0:
            sums(4, w, [0], 0, [NT - 1])
            last = sums(5, w, [1], 1 if two else 0, [NT - 1])
            if two:
                last = sums(6, w, [1], 0, [NT - 1])
            last.then_inc(full, 1)
            continue
        kt = u - 1
        if kt == 1:
            pe.wait_ge(prompt_read, 1)
            if two:
                pe.wait_ge(row_done, 2)
        if kt >= 2:
            pe.wait_ge(banks_read, 4 * (kt - 1))
        for t in range(4):
            last = sums(4 * (kt % 2) + t, w, range(4 * t, 4 * t + 4), t // 2 if two else 0, range(4 * (t % 2), 4 * (t % 2) + 4))
        if two and kt == 0:
            last = sums(7, w, range(8, 12), 0, range(4))
        last.then_inc(full, 1)


def filter_spectra(nc, io, mem, dram, x_hi, x_lo):
    with Phase(nc, "kt") as ph:
        full = ph.sem("sums_done")
        odd = ph.sem("odd_copied")
        spec_done = ph.sem("spectrum_done")
        row_done = ph.sem("row_done")
        spec_out = [ph.sem(f"spectrum_out{i}") for i in range(2)]
        prompt_copied = ph.sem("prompt_copied")
        prompt_read = ph.sem("prompt_read")
        prompt_out = ph.sem("prompt_out")
        ring = WeightRing(nc, ph, mem, lambda u: (full, u + 1))
        spec = ph.sb("spec", [P, 2, 4, DH])
        prompt = ph.sb("prompt", [P, 2, DH])
        ps = mem["psum"]
        blk = ph.block()

        @blk.sync
        def _(sp):
            for u in range(5):
                load_forward(sp, ring, io, u)
            sp.wait_ge(prompt_read, 1)
            sp.dma_start(dram["kt_prompt"], prompt[:]).then_inc(prompt_out, 16)
            for kt in range(4):
                sp.wait_ge(spec_done, 4 * (kt + 1))
                if kt == 0:
                    sp.wait_ge(row_done, 2)
                sp.dma_start(dram["kt"][kt], spec[:, kt % 2]).then_inc(spec_out[kt % 2], 16)
            sp.wait_ge(prompt_out, 16)
            sp.wait_ge(spec_out[0], 32)
            sp.wait_ge(spec_out[1], 32)

        @blk.gpsimd
        def _(pool):
            for u in range(5):
                ring.split_lo(pool, u, forward_width(u))

        @blk.tensor
        def _(pe):
            transform_products(nc, pe, mem, ring, x_hi, x_lo, True, full, prompt_read, row_done, spec_done)

        @blk.scalar
        def _(act):
            ring.split_hi(act, 0, forward_width(0))
            ring.split_hi(act, 1, forward_width(1))
            for kt in range(4):
                if kt < 3:
                    ring.split_hi(act, kt + 2)
                act.wait_ge(full, kt + 2)
                b = 4 * (kt % 2)
                if kt >= 2:
                    act.wait_ge(spec_out[kt % 2], 16)
                nc.scalar.activation(spec[:, kt % 2, 1:4:2, :], ps[:, b + 1:b + 4:2, :], ACT.Copy).then_inc(odd, 1)

        @blk.vector
        def _(dve):
            dve.wait_ge(full, 1)
            nc.vector.tensor_copy(prompt[:], ps[:, 4:6, :]).then_inc(prompt_copied, 1)
            dve.wait_ge(prompt_copied, 1)
            nc.vector.tensor_copy(prompt[0:1, 1, :], ps[0:1, 6, :]).then_inc(prompt_read, 1)
            for kt in range(4):
                dve.wait_ge(odd, kt + 1)
                combine(nc, ps, 4 * (kt % 2), spec[:, kt % 2], spec_done)
                if kt == 0:
                    dve.wait_ge(spec_done, 4)
                    for i, bank in ((2, 7), (3, 3)):
                        nc.vector.tensor_copy(spec[0:1, 0, i, :], ps[0:1, bank, :]).then_inc(row_done, 1)


def combine(nc, ps, b, spec, done):
    tt = nc.vector.tensor_tensor
    tt(spec[:, 0, :], ps[:, b, :], spec[:, 1, :], ALU.add).then_inc(done, 1)
    tt(spec[:, 1, :], ps[:, b, :], spec[:, 1, :], ALU.subtract).then_inc(done, 1)
    tt(spec[:, 2, :], ps[:, b + 2, :], spec[:, 3, :], ALU.add).then_inc(done, 1)
    nc.vector.scalar_tensor_tensor(out=spec[:, 3, :], in0=ps[:, b + 2, :], scalar=-1.0, in1=spec[:, 3, :],
                                   op0=ALU.mult, op1=ALU.add).then_inc(done, 1)


def phase_hyena(nc, io, mem, dram):
    with Phase(nc, "conv") as outer:
        y_hi = outer.sb("y_hi", [P, 4, 4, DH], F32R)
        y_lo = outer.sb("y_lo", [P, 4, 4, DH], F32R)
        yp_hi = outer.sb("yp_hi", [P, 2, DH], F32R)
        yp_lo = outer.sb("yp_lo", [P, 2, DH], F32R)
        spectra(nc, io, mem, dram, y_hi, y_lo, yp_hi, yp_lo)
        inverse_transform(nc, io, mem, dram, y_hi, y_lo, yp_hi, yp_lo)


def spectra(nc, io, mem, dram, y_hi, y_lo, yp_hi, yp_lo):
    ps = mem["psum"]
    with Phase(nc, "vspec") as outer:
        v_hi = outer.sb("v_hi", [P, 1, NT, DH], F32R)
        v_lo = outer.sb("v_lo", [P, 1, NT, DH], F32R)
        with Phase(nc, "vtok") as ph:
            v = ph.sb("v", [P, CH, T])
            v_in = [ph.sem(f"v_in{c}") for c in range(CH)]
            tr = ph.sem("transposed")
            hi = ph.sem("hi")
            lo = ph.sem("lo")
            blk = ph.block()

            @blk.sync
            def _(sp):
                for c in range(CH):
                    sp.dma_start(v[:, c, :], dram["hv"][c]).then_inc(v_in[c], 16)

            @blk.tensor
            def _(pe):
                for j in range(NT):
                    if j >= 4:
                        pe.wait_ge(lo, j - 3)
                    for c in range(CH):
                        if j == 0:
                            pe.wait_ge(v_in[c], 16)
                        s0 = (j // 4) + 256 * (j % 4)
                        src = v[:, c, s0:s0 + 255:2] if j < 8 else v[:, c, LS:T]
                        last = nc.tensor.transpose(ps[:, j % 4, c * P:(c + 1) * P], src, mem["ident"][:])
                    last.then_inc(tr, 1)

            @blk.scalar
            def _(act):
                for j in range(NT):
                    act.wait_ge(tr, j + 1)
                    nc.scalar.activation(v_hi[:, 0, j, :], ps[:, j % 4, :], ACT.Copy).then_inc(hi, 1)

            @blk.vector
            def _(dve):
                for j in range(NT):
                    dve.wait_ge(hi, j + 1)
                    nc.vector.tensor_tensor(v_lo[:, 0, j, :], ps[:, j % 4, :], v_hi[:, 0, j, :].bitcast(F32),
                                            ALU.subtract).then_inc(lo, 1)
        transform_and_multiply(nc, io, mem, dram, v_hi, v_lo, y_hi, y_lo, yp_hi, yp_lo)


def transform_and_multiply(nc, io, mem, dram, v_hi, v_lo, y_hi, y_lo, yp_hi, yp_lo):
    ps = mem["psum"]
    with Phase(nc, "vt") as ph:
        ks = ph.sb("k_spectrum", [P, 2, 4, DH])
        vs = ph.sb("v_spectrum", [P, 4, DH])
        t = ph.sb("cross", [P, 2, 2, DH])
        out = ph.sb("folded", [P, 4, DH])
        k_in = [ph.sem(f"k_in{i}") for i in range(2)]
        full = ph.sem("sums_done")
        prompt_read = ph.sem("prompt_read")
        row_read = ph.sem("row_read")
        odd = ph.sem("odd_copied")
        read = ph.sem("sums_read")
        used = ph.sem("spectra_used")
        folded_done = ph.sem("folded")
        hi = ph.sem("hi")
        lo = ph.sem("lo")
        step_sem = ph.sem("dve_step")
        ring = WeightRing(nc, ph, mem, lambda u: (full, u + 1), ahead=2)
        blk = ph.block()

        @blk.sync
        def _(sp):
            sp.dma_start(ks[:, 1, 0:2], dram["kt_prompt"]).then_inc(k_in[1], 16)
            load_forward(sp, ring, io, 2)
            sp.dma_start(ks[:, 0], dram["kt"][0]).then_inc(k_in[0], 16)
            load_forward(sp, ring, io, 3)
            for kt in range(1, 4):
                sp.wait_ge(used, kt)
                sp.dma_start(ks[:, kt % 2], dram["kt"][kt]).then_inc(k_in[kt % 2], 16)
                if kt == 1:
                    load_forward(sp, ring, io, 4)
                else:
                    ring.load(sp, kt + 3, io["k_inv"][kt - 2])

        @blk.tensor
        def _(pe):
            transform_products(nc, pe, mem, ring, v_hi, v_lo, False, full, prompt_read, None, read)

        def coefficients(n):
            return (y_hi[:, :, n - 1, :], y_lo[:, :, n - 1, :], out[:]) if n else (yp_hi[:], yp_lo[:], out[:, 0:2])

        @blk.scalar
        def _(act):
            def to_hi(n):
                act.wait_ge(folded_done, n + 1)
                nc.scalar.activation(coefficients(n)[0], coefficients(n)[2], ACT.Copy).then_inc(hi, 1)

            for kt in range(4):
                if kt < 3:
                    ring.split_hi(act, kt + 2)
                act.wait_ge(full, kt + 2)
                if kt == 0:
                    act.wait_ge(row_read, 1)
                else:
                    act.wait_ge(used, kt + 1)
                b = 4 * (kt % 2)
                nc.scalar.activation(vs[:, 1:4:2, :], ps[:, b + 1:b + 4:2, :], ACT.Copy).then_inc(odd, 1)
                to_hi(kt)
            for u in range(5, 7):
                ring.split_hi(act, u)
            to_hi(4)

        @blk.gpsimd
        def _(pool):
            def to_lo(n):
                pool.wait_ge(hi, n + 1)
                h, l, src = coefficients(n)
                nc.gpsimd.tensor_tensor(l, src, h.bitcast(F32), ALU.subtract).then_inc(lo, 1)

            for kt in range(4):
                if kt < 3:
                    ring.split_lo(pool, kt + 2)
                to_lo(kt)
            for u in range(5, 7):
                ring.split_lo(pool, u)
            to_lo(4)

        @blk.vector
        def _(dve):
            step = Chain(dve, step_sem)
            tt = nc.vector.tensor_tensor
            dve.wait_ge(full, 1)
            dve.wait_ge(k_in[1], 16)
            ka, kb = ks[:, 1, 0], ks[:, 1, 1]
            step.do(tt(t[:, 0, 0], ps[:, 4, :], ka, ALU.mult))
            step.do(tt(t[:, 0, 1], ps[:, 5, :], kb, ALU.mult))
            step.do(tt(t[:, 1, 0], ps[:, 4, :], kb, ALU.mult))
            step.do(tt(t[:, 1, 1], ps[:, 5, :], ka, ALU.mult))
            dve.sem_inc(prompt_read, 1)
            dve.sem_inc(used, 1)
            step.do(tt(out[:, 0, :], t[:, 0, 0], t[:, 0, 1], ALU.subtract))
            step.do(tt(out[:, 1, :], t[:, 1, 0], t[:, 1, 1], ALU.add))
            step.do(nc.vector.tensor_copy(out[0:1, 0:2, :], t[0:1, 0, :, :]))
            dve.sem_inc(folded_done, 1)
            dve.wait_ge(full, 2)
            dve.wait_ge(k_in[0], 16)
            row = ks[0:1, 0, 2:4]
            r = t[0:1].rearrange("p a b c -> p (a b) c")
            step.do(tt(r[:, 0, :], ps[0:1, 2, :], row[:, 0], ALU.mult))
            step.do(tt(r[:, 1, :], ps[0:1, 3, :], row[:, 1], ALU.mult))
            step.do(tt(r[:, 2, :], ps[0:1, 2, :], row[:, 1], ALU.mult))
            step.do(tt(r[:, 3, :], ps[0:1, 3, :], row[:, 0], ALU.mult))
            dve.sem_inc(row_read, 1)
            step.do(tt(row[:, 0], r[:, 0], r[:, 1], ALU.subtract))
            step.do(tt(row[:, 1], r[:, 2], r[:, 3], ALU.add))
            for kt in range(4):
                dve.wait_ge(odd, kt + 1)
                combine(nc, ps, 4 * (kt % 2), vs, read)
                dve.wait_ge(read, 4 * (kt + 1))
                dve.wait_ge(k_in[kt % 2], 16 * (kt // 2 + 1 + kt % 2))
                ka, kb = ks[:, kt % 2, 0:2], ks[:, kt % 2, 2:4]
                va, vb = vs[:, 0:2], vs[:, 2:4]
                step.do(tt(t[:, 0], vb, kb, ALU.mult))
                step.do(tt(t[:, 1], va, kb, ALU.mult))
                step.do(tt(va, va, ka, ALU.mult))
                step.do(tt(vb, vb, ka, ALU.mult))
                if kt == 0:
                    step.do(nc.vector.memset(t[0:1, 0], 0.0))
                step.do(tt(t[:, 0], va, t[:, 0], ALU.subtract))
                step.do(tt(t[:, 1], vb, t[:, 1], ALU.add))
                if kt >= 1:
                    dve.sem_inc(used, 1)
                dve.wait_ge(lo, kt + 1)
                step.do(tt(out[:, 0, :], t[:, 0, 0], t[:, 0, 1], ALU.add))
                step.do(tt(out[:, 2, :], t[:, 0, 0], t[:, 0, 1], ALU.subtract))
                step.do(tt(out[:, 1, :], t[:, 1, 0], t[:, 1, 1], ALU.subtract))
                step.do(tt(out[:, 3, :], t[:, 1, 0], t[:, 1, 1], ALU.add))
                if kt == 0:
                    step.do(nc.vector.tensor_copy(out[0:1, 1:4:2, :], row))
                    dve.sem_inc(used, 1)
                dve.sem_inc(folded_done, 1)


def inverse_transform(nc, io, mem, dram, y_hi, y_lo, yp_hi, yp_lo):
    ps = mem["psum"]
    with Phase(nc, "inv") as ph:
        full = ph.sem("product_done")
        unit_used = ph.sem("unit_used")
        ring = WeightRing(nc, ph, mem, lambda u: (unit_used, u + 1), ahead=2, first=1)
        v = ph.sb("v", [P, CH, T])
        x0 = ph.sb("x0", [P, CH, T])
        v_in = [ph.sem(f"v_in{c}") for c in range(CH)]
        bias_done = ph.sem("bias_done")
        summed = ph.sem("summed")
        gated = ph.sem("gated")
        y_out = ph.sem("y_out")
        blk = ph.block()

        @blk.sync
        def _(sp):
            ring.load(sp, 2, io["k_inv"][2])
            ring.load(sp, 3, io["k_inv"][3])
            for c in range(CH):
                sp.dma_start(v[:, c, :], dram["hv"][c]).then_inc(v_in[c], 16)
                sp.dma_start(x0[:, c, :], dram["x0"][c]).then_inc(v_in[c], 16)
            load_forward(sp, ring, io, 0, 4)
            for u in range(2):
                load_w_out(sp, ring, io, u, 5)
            sp.wait_ge(gated, 12)
            sp.dma_start(dram["y"].rearrange("k p t -> p k t")[:, 0:CH, :], x0[:]).then_inc(y_out, 16)
            sp.wait_ge(y_out, 16)

        @blk.gpsimd
        def _(pool):
            for u in range(2, 7):
                ring.split_lo(pool, u, 4 * P if u == 4 else UNIT)

        @blk.tensor
        def _(pe):
            for u in range(4):
                ring.ready(pe, u)
                xh, xl = cols(ring.hi(u), 512), cols(ring.lo(u), 512)
                for c in range(CH):
                    last = product(nc, [ps[:, 4 * (u // 2) + c, :]], lambda k: y_hi[:, u, k, c * P:(c + 1) * P],
                                   lambda k: y_lo[:, u, k, c * P:(c + 1) * P],
                                   lambda k, _: xh[:, k, :], lambda k, _: xl[:, k, :], range(4),
                                   first=u % 2 == 0, last=u % 2 == 1)
                    if u % 2:
                        last.then_inc(full, 1)
                    if c == CH - 1 and u % 2 == 0:
                        last.then_inc(unit_used, 1)
                if u % 2:
                    pe.wait_ge(full, 4 * (u // 2 + 1))
                    pe.sem_inc(unit_used, 1)
            ring.ready(pe, 4)
            pe.wait_ge(summed, 1)
            xh = ring.hi(4)[:, 0:4 * P].rearrange("p (t k) -> p t k", t=4)
            xl = ring.lo(4)[:, 0:4 * P].rearrange("p (t k) -> p t k", t=4)
            for c in range(CH):
                last = product(nc, [ps[:, 0, c * P:(c + 1) * P]], lambda t: yp_hi[:, t, c * P:(c + 1) * P],
                               lambda t: yp_lo[:, t, c * P:(c + 1) * P], lambda t, _: xh[:, 2 + t, :],
                               lambda t, _: xl[:, 2 + t, :], range(2))
            last.then_inc(full, 1)
            pe.wait_ge(full, 9)
            pe.sem_inc(unit_used, 1)

        @blk.scalar
        def _(act):
            for u in range(2, 7):
                ring.split_hi(act, u, 4 * P if u == 4 else UNIT)

        @blk.vector
        def _(dve):
            par = mem["par"]
            for c in range(CH):
                dve.wait_ge(v_in[c], 32)
                nc.vector.tensor_scalar_mul(v[:, c, :], v[:, c, :], par[:, PA["hy_bias"] + c:PA["hy_bias"] + c + 1])\
                  .then_inc(bias_done, 1)
            dve.wait_ge(bias_done, CH)
            for n in range(12):
                c = n % 4
                dve.wait_ge(full, n + 1 if n < 8 else 9)
                if n < 8:
                    seg = slice(n // 4, LS, 2)
                    src, gain = ps[:, n, :], mem["filter_gain"][:, c:c + 1]
                else:
                    seg = slice(LS, T)
                    src, gain = ps[:, 0, c * P:(c + 1) * P], mem["filter_gain"][:, CH + c:CH + c + 1]
                nc.vector.scalar_tensor_tensor(out=v[:, c, seg], in0=src, scalar=gain, in1=v[:, c, seg],
                                               op0=ALU.mult, op1=ALU.add).then_inc(summed, 1)
                dve.wait_ge(summed, n + 1)
                nc.vector.tensor_tensor(x0[:, c, seg], v[:, c, seg], x0[:, c, seg], ALU.mult).then_inc(gated, 1)


G_SRC, G_INTER, G_FLOOR, G_STATE = range(4)


def gate_rows(nc, io, mem, dram, col, wcb, mrow, q, k, kn, v, work, C):
    ps = mem["psum"]
    gates = mem["gates"]
    with Phase(nc, "rows") as ph:
        f, e, u, lnu = (work[0:ROWS].rearrange("p a b c -> p (a b c)")[:, i * T:(i + 1) * T] for i in range(4))
        reset = ph.sb("reset", [ROWS, T])
        b = ph.sb("b", [ROWS, T])
        jump = ph.sb("jump", [ROWS, T])
        r1 = ph.sb("r1", [P, T])
        r2 = ph.sb("r2", [P, T])
        m0 = ph.sb("m0", [ROWS, 1])
        m_in = ph.sb("m_in", [ROWS, NT])
        m_end = ph.sb("m_end", [ROWS, NT])
        wc = ph.sb("wc", [ROWS, NT])
        m_new = ph.sb("m_new", [ROWS, 1])
        ins_in = ph.sem("inputs_in")
        zeroed = ph.sem("zeroed")
        act_step = ph.sem("act_step")
        dve_sem = ph.sem("dve_step")
        lin = ph.sem("log_parts")
        ready = ph.sem("exponents_ready")
        tr = ph.sem("transposed")
        stored = ph.sem("stored")
        c_rows = ph.sb("c_rows", [P, 8, HD])
        n_rows = ph.sb("n_rows", [8, HD])
        q_in = ph.sem("q_in")
        v_in = ph.sem("v_in")
        k_in = ph.sem("k_in")
        c_in = ph.sem("c_in")
        turned = ph.sem("keys_transposed")
        copied = ph.sem("keys_copied")
        g, M = r1[0:ROWS, :], mrow
        blk = ph.block()

        @blk.gpsimd
        def _(pool):
            nc.gpsimd.memset(m0[:], 0.0).then_inc(zeroed, 1)
            nc.gpsimd.memset(C[:, 0], 0.0)
            nc.gpsimd.memset(v[:, :, :, HD:HD + 1], 1.0)

        @blk.sync
        def _(sp):
            sp.wait_ge(zeroed, 1)
            for dst, src in ((reset, "k_reset"), (mem["sel"], "k_sel"), (mem["mask"], "k_mask")):
                sp.dma_start(dst[:], io[src]).then_inc(ins_in, 16)
            for d in range(2):
                sp.dma_start(m0[32 * d:32 * d + HEADS, :], io["state_mlstm_m"][0, 0, d].rearrange("(h o) -> h o", o=1))\
                  .then_inc(ins_in, 16)
            sp.dma_start(k[:], dram["k"].rearrange("h p t -> p h t")).then_inc(k_in, 16)
            sp.dma_start(c_rows[:], io["state_mlstm_C"][0, 0].rearrange("d h e k -> e (d h) k")).then_inc(c_in, 16)
            sp.dma_start(n_rows[:], io["state_mlstm_n"][0, 0].rearrange("d h k -> (d h) k")).then_inc(c_in, 16)
            sp.dma_start(q[:], dram["q"].rearrange("h p t -> p h t")).then_inc(q_in, 16)
            for t in range(NT):
                sp.dma_start(v[:, t, :, 0:HD], dram["v"][t].rearrange("p (h d) -> p h d", h=HEADS)).then_inc(v_in, 16)
            sp.wait_ge(act_step, 5)
            for d in range(2):
                for i, rows in enumerate((mrow, r1)):
                    p0 = 32 * d + ROWS * i
                    sp.dma_start(dram["scan_rows"][i, HEADS * d:HEADS * d + HEADS, :], rows[p0:p0 + HEADS, :]).then_inc(stored, 16)
            sp.wait_ge(ready, 5)
            for d in range(2):
                sp.dma_start(io["new_m"][0, 0, d].rearrange("(h o) -> h o", o=1), m_new[32 * d:32 * d + HEADS, :])\
                  .then_inc(stored, 16)
            sp.wait_ge(q_in, 16)
            sp.wait_ge(v_in, 16 * NT)
            sp.wait_ge(stored, 96)

        @blk.scalar
        def _(act):
            step = Chain(act, act_step)
            step.do(nc.scalar.activation(f, gates[ROWS:P, :], ACT.Copy))
            step.do(nc.scalar.activation(e, gates[ROWS:P, :], ACT.Abs))
            step.do(nc.scalar.activation(e, e, ACT.Exp, scale=-1.0))
            act.wait_ge(lin, 1)
            step.do(nc.scalar.activation(lnu, u, ACT.Ln))
            for c in range(NT + 3):
                act.wait_ge(turned, c + 1)
                src = ps[:, 6 + c % 2, :].rearrange("p (h d) -> p h d", h=HEADS)
                if c < NT:
                    dst = kn[:, c]
                elif c < NT + 2:
                    dst = C[:, 1, 4 * (c - NT):4 * (c - NT) + 4, 0:HD]
                else:
                    dst, src = C[:, 1, :, HD], ps[:, 6 + c % 2, 0:8]
                nc.scalar.activation(dst, src, ACT.Copy).then_inc(copied, 1)
            act.wait_ge(ready, 1)
            step.do(nc.scalar.activation(r1[ROWS:P, :], r1[ROWS:P, :], ACT.Exp))
            act.wait_ge(ready, 2)
            step.do(nc.scalar.activation(r2[0:ROWS, :], r2[0:ROWS, :], ACT.Exp, scale=-1.0))
            act.wait_ge(ready, 3)
            step.do(nc.scalar.activation(r2[ROWS:P, :], r2[ROWS:P, :], ACT.Exp))
            act.wait_ge(ready, 4)
            step.do(nc.scalar.activation(wc[:], wc[:], ACT.Exp))

        @blk.vector
        def _(dve):
            step = Chain(dve, dve_sem)
            tt, ts, scan = nc.vector.tensor_tensor, nc.vector.tensor_scalar, nc.vector.tensor_tensor_scan
            step.do(nc.vector.memset(jump[:], 0.0))
            dve.wait_ge(act_step, 3)
            nc.vector.tensor_scalar_add(u, e, 1.0).then_inc(lin, 1)
            dve.wait_ge(lin, 1)
            step.do(nc.vector.reciprocal(b[:], u))
            step.do(nc.vector.scalar_tensor_tensor(out=e, in0=u, scalar=1.0, in1=e, op0=ALU.subtract, op1=ALU.subtract))
            step.do(tt(e, e, b[:], ALU.mult))
            dve.wait_ge(act_step, 4)
            step.do(tt(lnu, lnu, e, ALU.subtract))
            step.do(nc.vector.scalar_tensor_tensor(out=f, in0=f, scalar=0.0, in1=lnu, op0=ALU.min, op1=ALU.subtract))
            dve.wait_ge(ins_in, 80)
            F_, B_ = slice(0, 32), slice(32, 64)
            step.do(scan(out=b[F_, :], data0=reset[F_, :], data1=f[F_, :], initial=0.0, op0=ALU.mult, op1=ALU.add))
            step.do(scan(out=b[B_, ::-1], data0=reset[B_, ::-1], data1=f[B_, ::-1], initial=0.0, op0=ALU.mult, op1=ALU.add))
            step.do(tt(g, gates[0:ROWS, :], b[:], ALU.subtract))
            step.do(nc.vector.tensor_copy(jump[F_, P:LS:P], b[F_, P - 1:LS - 1:P]))
            step.do(nc.vector.tensor_copy(jump[B_, P - 1:LS - 1:P], b[B_, P:LS:P]))
            for rows, init in ((slice(0, LS), True), (slice(LS, T), False)):
                a, z = rows.start, rows.stop
                step.do(scan(out=M[F_, a:z], data0=jump[F_, a:z], data1=g[F_, a:z],
                             initial=m0[F_, :] if init else 0.0, op0=ALU.add, op1=ALU.max))
                step.do(scan(out=M[B_, a:z][:, ::-1], data0=jump[B_, a:z][:, ::-1], data1=g[B_, a:z][:, ::-1],
                             initial=m0[B_, :] if init else 0.0, op0=ALU.add, op1=ALU.max))
            step.do(nc.vector.memset(m_in[:], 0.0))
            step.do(nc.vector.tensor_copy(m_in[F_, 0:1], m0[F_, :]))
            step.do(nc.vector.tensor_copy(m_in[B_, 7:8], m0[B_, :]))
            step.do(tt(m_in[F_, 1:8], M[F_, P - 1:LS - 1:P], b[F_, P - 1:LS - 1:P], ALU.add))
            step.do(tt(m_in[B_, 0:7], M[B_, P:LS:P], b[B_, P:LS:P], ALU.add))
            step.do(nc.vector.tensor_copy(m_end[F_, :], M[F_, P - 1:T:P]))
            step.do(nc.vector.tensor_copy(m_end[B_, :], M[B_, 0:T:P]))

            def chunked(a):
                return a.rearrange("p (c t) -> p c t", t=P)

            def spread(a):
                return a.unsqueeze(2).broadcast_to([ROWS, NT, P])

            nc.vector.tensor_tensor(chunked(r1[ROWS:P, :]), spread(m_in[:]), chunked(M[:]), ALU.subtract).then_inc(ready, 1)
            tt(r2[0:ROWS, :], b[:], M[:], ALU.add).then_inc(ready, 1)
            tt(chunked(r2[ROWS:P, :]), chunked(g), spread(m_end[:]), ALU.subtract).then_inc(ready, 1)
            tt(wc[:], m_in[:], m_end[:], ALU.subtract).then_inc(ready, 1)
            step.do(tt(m_new[F_, :], m_end[F_, 8:9], b[F_, T - 1:T], ALU.add))
            step.do(tt(m_new[B_, :], m_end[B_, 8:9], b[B_, LS:LS + 1], ALU.add))
            dve.sem_inc(ready, 1)
            for i in range(5):
                dve.wait_ge(tr, i + 1)
                c0, n = 2 * i, min(4, 18 - 4 * i)
                step.do(nc.vector.tensor_copy(col[:, c0:c0 + n // 2, :, :].rearrange("p c g r -> p (c g r)"), ps[:, i, 0:n * P]))
            dve.wait_ge(tr, 6)
            step.do(nc.vector.tensor_copy(wcb[:].rearrange("p r c -> p (r c)"), ps[:, 5, 0:8 * NT]))

        @blk.tensor
        def _(pe):
            pe.wait_ge(k_in, 16)
            for c in range(NT + 3):
                if c == NT:
                    pe.wait_ge(c_in, 32)
                if c >= 2:
                    pe.wait_ge(copied, c - 1)
                if c == NT + 2:
                    nc.tensor.transpose(ps[:, 6 + c % 2, 0:8], n_rows[:], mem["ident"][0:8, 0:8]).then_inc(turned, 1)
                    continue
                for h in range(HEADS):
                    src = k[:, h, c * P:(c + 1) * P] if c < NT else c_rows[:, 4 * (c - NT) + h, :]
                    ins = nc.tensor.transpose(ps[:, 6 + c % 2, h * P:(h + 1) * P], src, mem["ident"][:])
                ins.then_inc(turned, 1)
            pe.wait_ge(act_step, 8)
            for c in range(NT):
                for j, r in enumerate((r1, r2)):
                    n = 2 * c + j
                    ins = nc.tensor.transpose(ps[:, n // 4, (n % 4) * P:(n % 4 + 1) * P], r[:, c * P:(c + 1) * P], mem["ident"][:])
                    if n % 4 == 3 or n == 17:
                        ins.then_inc(tr, 1)
            for r in range(8):
                ins = nc.tensor.matmul(ps[:, 5, r * NT:(r + 1) * NT], mem["sel"][:, r, :], wc[:], start=True, stop=True)
            ins.then_inc(tr, 1)


def chunk_units():
    units = [(0, 8, 0, True), (1, 8, 0, True)]
    for j in range(8):
        units += [(0, j, 1, j < 7), (1, 7 - j, 1, j < 7)]
    return units


def phase_mlstm(nc, io, mem, dram):
    ps = mem["psum"]
    HC = HEADS
    with Phase(nc, "mlstm") as outer:
        col = outer.sb("col", [P, NT, 4, ROWS])
        wcb = outer.sb("wcb", [P, 8, NT])
        mrow = outer.sb("M", [ROWS, T])
        mem.update(mask=outer.sb("mask", [P, 2, P]), sel=outer.sb("sel", [ROWS, 8, P]))
        q = outer.sb("q", [P, HC, T])
        k = outer.sb("k", [P, HC, T])
        kn = outer.sb("k_tok", [P, NT, HC, HD])
        v = outer.sb("v", [P, NT, HC, HD + 1])
        hacc = outer.sb("h", [P, NT, HC, HD])
        C = outer.sb("C", [P, 2, 8, HD + 1])
        gate_rows(nc, io, mem, dram, col, wcb, mrow, q, k, kn, v, hacc, C)
        chunk_scan(nc, mem, dram, q, k, kn, v, hacc, C, col, wcb)
        mlstm_output(nc, io, mem, dram, hacc, C, q)


def chunk_scan(nc, mem, dram, q, k, kn, v, hacc, C, col, wcb):
    ps = mem["psum"]
    units = chunk_units()
    N = len(units)
    ups = [n for n, un in enumerate(units) if un[3]]
    HC = HEADS
    E = HD + 1
    RB = 3

    def updates_before(n):
        return sum(1 for i in ups if i < n)

    def updates_upto_same(n):
        d, c, s, _ = units[n]
        last = [i for i in ups if i < n and units[i][0] == d and units[i][2] == s]
        return updates_before(last[-1]) + 1 if last else 0

    with Phase(nc, "scan") as ph:
        spread = ph.sb("rows_spread", [P, RB, 2, HC, P])
        dist = ph.sb("dist", [P, 2, HC, P])
        dec = ph.sb("decay", [P, 2, HC, P])
        prob = ph.sb("prob", [P, 2, HC, P])
        qw = ph.sb("weighted_q", [P, 2, HC, P])
        wv = ph.sb("weighted_v", [P, 2, HC, E])
        den = ph.sb("den", [P, 2, HC])
        cleared = ph.sem("h_cleared")
        rows_in = [ph.sem(f"rows_in{i}") for i in range(RB)]
        score = ph.sem("scores_done")
        dist_done = ph.sem("dist_done")
        dec_done = ph.sem("decay_done")
        prob_done = ph.sem("prob_done")
        qw_done = ph.sem("weighted_q_done")
        wv_done = ph.sem("weighted_v_done")
        num_done = ph.sem("numerators_done")
        state_mm = ph.sem("state_product_done")
        state_done = ph.sem("state_updated")
        out_done = ph.sem("h_added")
        step_sem = ph.sem("dve_step")
        B_S, B_N, B_C = 0, 2, 6
        blk = ph.block()

        def heads(bank):
            return ps[:, bank, :].rearrange("p (h d) -> p h d", h=HC)

        def wide(bank, h):
            return ps[:, bank + h // 2, (h % 2) * E:(h % 2) * E + E]

        @blk.sync
        def _(sp):
            for n in range(N):
                d, c, s, up = units[n]
                if n >= RB:
                    sp.wait_ge(dist_done, n - RB + 1)
                    sp.wait_ge(qw_done, n - RB + 1)
                for i in range(2):
                    src = dram["scan_rows"][i:i + 1, HC * d:HC * d + HC, c * P:(c + 1) * P]
                    sp.dma_start(spread[:, n % RB, i], src.broadcast_to([P, HC, P])).then_inc(rows_in[n % RB], 16)

        @blk.tensor
        def _(pe):
            def scores(n):
                d, c, s, up = units[n]
                tok = slice(c * P, (c + 1) * P)
                if n >= 2:
                    pe.wait_ge(prob_done, n - 1)
                for h in range(HC):
                    ins = nc.tensor.matmul(heads(B_S + n % 2)[:, h, :], k[:, h, tok], q[:, h, tok], start=True, stop=True)
                ins.then_inc(score, 1)

            scores(0)
            for n in range(N):
                d, c, s, up = units[n]
                num = B_N + 2 * (n % 2)
                if n + 1 < N:
                    scores(n + 1)
                pe.wait_ge(prob_done, n + 1)
                if n >= 2:
                    pe.wait_ge(out_done, n - 1)
                pe.wait_ge(qw_done, n + 1)
                pe.wait_ge(state_done, updates_upto_same(n)) if updates_upto_same(n) else None
                for h in range(HC):
                    nc.tensor.matmul(wide(num, h), prob[:, n % 2, h, :], v[:, c, h, :], start=True, stop=False)
                    ins = nc.tensor.matmul(wide(num, h), qw[:, n % 2, h, :], C[:, s, 4 * d + h, :], start=False, stop=True)
                ins.then_inc(num_done, 1)
                if up:
                    j = updates_before(n)
                    pe.wait_ge(wv_done, j + 1)
                    if j >= 1:
                        pe.wait_ge(state_done, j)
                    for h in range(HC):
                        ins = nc.tensor.matmul(wide(B_C, h), kn[:, c, h, :], wv[:, j % 2, h, :], start=True, stop=True)
                    ins.then_inc(state_mm, 1)

        @blk.gpsimd
        def _(pool):
            nc.gpsimd.memset(hacc[:], 0.0).then_inc(cleared, 1)
            for n in range(N):
                d, c, s, up = units[n]
                pool.wait_ge(rows_in[n % RB], 32 * (n // RB + 1))
                if n >= 2:
                    pool.wait_ge(num_done, n - 1)
                nc.gpsimd.tensor_tensor(qw[:, n % 2], q[:, :, c * P:(c + 1) * P], spread[:, n % RB, 1], ALU.mult)\
                  .then_inc(qw_done, 1)
                if up:
                    j = updates_before(n)
                    if j >= 2:
                        pool.wait_ge(state_mm, j - 1)
                    w = col[:, c, G_STATE, 32 * d:32 * d + HC].unsqueeze(2).broadcast_to([P, HC, E])
                    nc.gpsimd.tensor_tensor(wv[:, j % 2], v[:, c], w, ALU.mult).then_inc(wv_done, 1)

        @blk.scalar
        def _(act):
            for n in range(N):
                act.wait_ge(dist_done, n + 1)
                if n >= 2:
                    act.wait_ge(prob_done, n - 1)
                nc.scalar.activation(dec[:, n % 2], dist[:, n % 2], ACT.Exp, scale=-1.0).then_inc(dec_done, 1)

        @blk.vector
        def _(dve):
            step = Chain(dve, step_sem)
            tt, stt = nc.vector.tensor_tensor, nc.vector.scalar_tensor_tensor

            def distance(n):
                d, c, s, up = units[n]
                dve.wait_ge(rows_in[n % RB], 32 * (n // RB + 1))
                if n >= 2:
                    dve.wait_ge(dec_done, n - 1)
                for h in range(HC):
                    r = 32 * d + h
                    ins = stt(out=dist[:, n % 2, h, :], in0=spread[:, n % RB, 0, h, :], scalar=col[:, c, G_SRC, r:r + 1],
                              in1=mem["mask"][:, d, :], op0=ALU.subtract, op1=ALU.max)
                ins.then_inc(dist_done, 1)

            def probabilities(n):
                dve.wait_ge(dec_done, n + 1)
                dve.wait_ge(score, n + 1)
                if n >= 2:
                    dve.wait_ge(num_done, n - 1)
                tt(prob[:, n % 2], heads(B_S + n % 2), dec[:, n % 2], ALU.mult).then_inc(prob_done, 1)

            distance(0)
            distance(1)
            probabilities(0)
            dve.wait_ge(cleared, 1)
            for n in range(N):
                d, c, s, up = units[n]
                rows = slice(32 * d, 32 * d + HC)
                num = B_N + 2 * (n % 2)
                if n + 2 < N:
                    distance(n + 2)
                if n + 1 < N:
                    probabilities(n + 1)
                if up:
                    j, r0 = updates_before(n), 4 * d
                    dve.wait_ge(state_mm, j + 1)
                    for h in range(HC):
                        ins = stt(out=C[:, s, r0 + h, :], in0=C[:, s, r0 + h, :], scalar=wcb[:, r0 + h, c:c + 1],
                                  in1=wide(B_C, h), op0=ALU.mult, op1=ALU.add)
                    ins.then_inc(state_done, 1)
                dve.wait_ge(num_done, n + 1)
                sums = ps[:, num:num + 2, 0:2 * E].rearrange("p b (h e) -> p b h e", h=2)[:, :, :, HD]
                dn = den[:, n % 2]
                step.do(nc.vector.tensor_copy(dn.rearrange("p (b h) -> p b h", b=2), sums))
                step.do(stt(out=dn, in0=dn, scalar=-1.0, in1=dn, op0=ALU.mult, op1=ALU.max))
                step.do(tt(dn, dn, col[:, c, G_FLOOR, rows], ALU.max))
                step.do(nc.vector.reciprocal(dn, dn))
                for h in range(HC):
                    ins = stt(out=hacc[:, c, h, :], in0=wide(num, h)[:, 0:HD], scalar=dn[:, h:h + 1], in1=hacc[:, c, h, :],
                              op0=ALU.mult, op1=ALU.add)
                ins.then_inc(out_done, 1)
                dve.wait_ge(out_done, n + 1)


def mlstm_output(nc, io, mem, dram, hacc, C, stage):
    ps = mem["psum"]
    HC = HEADS
    with Phase(nc, "mout") as ph:
        sq = ph.sb("sq", [P, HC, HD])
        ss = ph.sb("ss", [P, NT, HC])
        o = ph.sb("o", [P, NT, HC, HD])
        c_out = ph.sb("c_out", [P, 8, HD])
        n_out = ph.sb("n_out", [8, HD])
        o_in = ph.sem("o_in")
        c_tr = ph.sem("state_transposed")
        c_cp = ph.sem("state_copied")
        squares = ph.sem("squares")
        mean = ph.sem("mean_square")
        root = ph.sem("root")
        gated = ph.sem("gated")
        tr = ph.sem("transposed")
        cp = ph.sem("copied")
        step_sem = ph.sem("dve_step")
        stored = ph.sem("stored")
        blk = ph.block()

        @blk.sync
        def _(sp):
            sp.dma_start(o[:], dram["o"].rearrange("t p c -> p t c")).then_inc(o_in, 16)
            sp.wait_ge(c_cp, 3)
            sp.dma_start(io["new_C"][0, 0].rearrange("d h e k -> e (d h) k"), c_out[:]).then_inc(stored, 16)
            sp.dma_start(io["new_n"][0, 0].rearrange("d h k -> (d h) k"), n_out[:]).then_inc(stored, 16)
            sp.wait_ge(cp, NT)
            sp.dma_start(dram["y"].rearrange("k p t -> p k t")[:, CH:KD, :], stage[:]).then_inc(stored, 16)
            sp.wait_ge(stored, 48)

        @blk.tensor
        def _(pe):
            for i in range(2):
                for h in range(HC):
                    ins = nc.tensor.transpose(ps[:, 4 + i, h * P:(h + 1) * P], C[:, 0, 4 * i + h, 0:HD], mem["ident"][:])
            nc.tensor.transpose(ps[0:8, 6, 0:P], C[:, 0, :, HD], mem["ident"][:]).then_inc(c_tr, 1)
            for t in range(NT):
                pe.wait_ge(gated, t + 1)
                if t >= 4:
                    pe.wait_ge(cp, t - 3)
                for h in range(HC):
                    ins = nc.tensor.transpose(ps[:, t % 4, h * P:(h + 1) * P], hacc[:, t, h, :], mem["ident"][:])
                ins.then_inc(tr, 1)

        @blk.scalar
        def _(act):
            act.wait_ge(c_tr, 1)
            for i in range(2):
                nc.scalar.activation(c_out[:, 4 * i:4 * i + 4, :].rearrange("p h d -> p (h d)"), ps[:, 4 + i, :], ACT.Copy)\
                  .then_inc(c_cp, 1)
            nc.scalar.activation(n_out[:], ps[0:8, 6, 0:P], ACT.Copy).then_inc(c_cp, 1)
            act.wait_ge(mean, 1)
            nc.scalar.activation(ss[:], ss[:], ACT.Sqrt).then_inc(root, 1)
            w0 = PA["ml_norm_w"]
            for t in range(NT):
                act.wait_ge(tr, t + 1)
                for h in range(HC):
                    ins = nc.scalar.activation(stage[:, h, t * P:(t + 1) * P], ps[:, t % 4, h * P:(h + 1) * P], ACT.Copy,
                                               scale=mem["par"][:, w0 + h:w0 + h + 1])
                ins.then_inc(cp, 1)

        @blk.vector
        def _(dve):
            step = Chain(dve, step_sem)
            tt = nc.vector.tensor_tensor
            for t in range(NT):
                step.do(tt(sq[:], hacc[:, t], hacc[:, t], ALU.mult))
                step.do(nc.vector.tensor_reduce(out=ss[:, t, :], in_=sq[:], op=ALU.add, axis=mybir.AxisListType.X))
            nc.vector.tensor_scalar(ss[:], ss[:], 1.0 / HD, EPS, ALU.mult, ALU.add).then_inc(mean, 1)
            dve.wait_ge(root, 1)
            step.do(nc.vector.reciprocal(ss[:], ss[:]))
            dve.wait_ge(o_in, 16)
            for t in range(NT):
                step.do(tt(hacc[:, t], hacc[:, t], ss[:, t, :].unsqueeze(2).broadcast_to([P, HC, HD]), ALU.mult))
                tt(hacc[:, t], hacc[:, t], o[:, t], ALU.mult).then_inc(gated, 1)


GRID_W = 64
GRID_H = LS // GRID_W
PADW = GRID_W + 2
GRID = (GRID_H + 2) * PADW
PADT = GRID + LP + 2
STEPS = JF // 2
TAPS = 9


def slot_banks(ps, n):
    return ps[:, 3 * (n % 2):3 * (n % 2) + 3, :]


def add_gated(nc, ps_slot, x, gate):
    stt = nc.vector.scalar_tensor_tensor
    a = x[:, 0:768].rearrange("p (b c) -> p b c", c=BW)
    stt(out=a, in0=ps_slot[:, 0:2, 0:BW], scalar=gate[:, 0:1], in1=a, op0=ALU.mult, op1=ALU.add)
    stt(out=x[:, 768:LS], in0=ps_slot[:, 2, 0:256], scalar=gate[:, 0:1], in1=x[:, 768:LS], op0=ALU.mult, op1=ALU.add)
    return stt(out=x[:, LS:T], in0=ps_slot[:, 2, 256:BW], scalar=gate[:, 1:2], in1=x[:, LS:T], op0=ALU.mult, op1=ALU.add)


def phase_out(nc, io, mem, dram):
    with Phase(nc, "tail") as outer:
        x = outer.sb("x", [P, KD, T])
        output_projection(nc, io, mem, dram, x)
        with Phase(nc, "ffn") as mid:
            h_hi = mid.sb("h_hi", [P, KD, T], F32R)
            h_lo = mid.sb("h_lo", [P, KD, T], F32R)
            with Phase(nc, "norm2") as nh:
                on_act, on_pe, on_dve, on_pool, _ = modulated_norm(nc, nh, mem, x, h_hi, h_lo, "gain_ffn", 24)
                blk = nh.block()

                @blk.scalar
                def _(act):
                    on_act(lambda eng, k: None)

                @blk.tensor
                def _(pe):
                    on_pe()

                @blk.vector
                def _(dve):
                    on_dve(lambda eng, k: None)

                @blk.gpsimd
                def _(pool):
                    on_pool()
            feed_forward(nc, io, mem, x, h_hi, h_lo)
        final_norm(nc, io, mem, x)


def output_projection(nc, io, mem, dram, x):
    ps = mem["psum"]
    with Phase(nc, "oproj") as ph:
        full = ph.sem("product_done")
        ring = WeightRing(nc, ph, mem, lambda u: (full, 2 * (u + 1)), ahead=2)
        y = ph.sb("y", [P, 2, T])
        y_hi = ph.sb("y_hi", [P, KD, T], F32R)
        y_lo = ph.sb("y_lo", [P, KD, T], F32R)
        y_in = [ph.sem(f"y_in{i}") for i in range(2)]
        x_rows = ph.sb("x_rows", [P, 3, D])
        x_in = [ph.sem(f"x_in{i}") for i in range(3)]
        x_turned = ph.sem("x_transposed")
        x_done = ph.sem("x_copied")
        hi = ph.sem("y_hi_done")
        lo = ph.sem("y_lo_done")
        added = ph.sem("added")
        blk = ph.block()

        @blk.sync
        def _(sp):
            for k in range(KD):
                if k >= 2:
                    sp.wait_ge(lo, k - 1)
                sp.dma_start(y[:, k % 2, :], dram["y"][k]).then_inc(y_in[k % 2], 16)
            for t in range(NT):
                if t >= 3:
                    sp.wait_ge(x_turned, 2 * (t - 2))
                sp.dma_start(x_rows[:, t % 3, :], io["x_sample"][0, t * P:(t + 1) * P, :] if t < 8 else io["x_prompt"][0])\
                  .then_inc(x_in[t % 3], 16)
            for u in range(2, 4):
                load_w_out(sp, ring, io, u)

        @blk.scalar
        def _(act):
            for k in range(KD):
                act.wait_ge(y_in[k % 2], 16 * (k // 2 + 1))
                nc.scalar.activation(y_hi[:, k, :], y[:, k % 2, :], ACT.Copy).then_inc(hi, 1)
            for n in range(2 * NT):
                t, half = n // 2, n % 2
                act.wait_ge(x_turned, n + 1)
                nc.scalar.activation(x[:, 4 * half:4 * half + 4, t * P:(t + 1) * P],
                                     ps[:, 6 + half, :].rearrange("p (k t) -> p k t", t=P), ACT.Copy).then_inc(x_done, 1)
            ring.split_hi(act, 2)
            ring.split_hi(act, 3)

        @blk.gpsimd
        def _(pool):
            for u in range(2, 4):
                ring.split_lo(pool, u)

        @blk.vector
        def _(dve):
            for k in range(KD):
                dve.wait_ge(hi, k + 1)
                nc.vector.tensor_tensor(y_lo[:, k, :], y[:, k % 2, :], y_hi[:, k, :].bitcast(F32), ALU.subtract).then_inc(lo, 1)
            dve.wait_ge(x_done, 2 * NT)
            for n in range(KD):
                dve.wait_ge(full, n + 1)
                add_gated(nc, slot_banks(ps, n), x[:, n, :], mem["mod"][:, 16 + n, :]).then_inc(added, 1)

        @blk.tensor
        def _(pe):
            for n in range(2 * NT):
                t, half = n // 2, n % 2
                if half == 0:
                    pe.wait_ge(x_in[t % 3], 16 * (t // 3 + 1))
                if n >= 2:
                    pe.wait_ge(x_done, n - 1)
                for j in range(4):
                    last = nc.tensor.transpose(ps[:, 6 + half, j * P:(j + 1) * P],
                                               x_rows[:, t % 3, (4 * half + j) * P:(4 * half + j + 1) * P], mem["ident"][:])
                last.then_inc(x_turned, 1)
            for n in range(KD):
                ring.ready(pe, n // 2)
                if n == 0:
                    pe.wait_ge(lo, KD)
                if n >= 2:
                    pe.wait_ge(added, n - 1)
                wh, wl = cols(ring.hi(n // 2), 256), cols(ring.lo(n // 2), 256)
                c = (n % 2) * P
                slot = slot_banks(ps, n)
                product(nc, [slot[:, i, 0:BW] for i in range(NB)], lambda k: wh[:, k, c:c + P], lambda k: wl[:, k, c:c + P],
                        lambda k, i: y_hi[:, k, i * BW:(i + 1) * BW], lambda k, i: y_lo[:, k, i * BW:(i + 1) * BW],
                        range(KD)).then_inc(full, 1)


def feed_forward(nc, io, mem, x, h_hi, h_lo):
    ps, par = mem["psum"], mem["par"]
    up, down = io["ffn_w_up"][0], io["ffn_w_down"][0]
    with Phase(nc, "mlp") as ph:
        pad = ph.sb("pad", [P, 2, PADT])
        acc_a = ph.sb("acc_a", [P, 2, T])
        acc_v = ph.sb("acc_v", [P, 2, T])
        g_hi = ph.sb("g_hi", [P, 2, T], F32R)
        g_lo = ph.sb("g_lo", [P, 2, T], F32R)
        taps = ph.sb("taps", [P, 2, 2, TAPS + 1, 2])
        pads_zero = ph.sem("pads_zero")
        raw_in = [ph.sem(f"weights_loaded{i}") for i in range(2)]
        w_hi_done = ph.sem("weights_hi")
        w_lo_done = ph.sem("weights_lo")
        taps_ready = ph.sem("taps_ready")
        full = ph.sem("product_done")
        evac = ph.sem("product_copied")
        tap0_done = ph.sem("first_tap_done")
        conv_done = ph.sem("conv_done")
        silu_done = ph.sem("silu_done")
        gated = ph.sem("gated")
        g_hi_done = ph.sem("gated_hi")
        g_lo_done = ph.sem("gated_lo")
        added = ph.sem("down_added")
        step_sem = ph.sem("dve_step")
        row_sem = ph.sem("row_step")
        blk = ph.block()

        w_raw, w_hi, w_lo = mem["w_raw"], mem["w_hi"], mem["w_lo"]

        def products(i):
            return 12 * i - 8 if not (isinstance(i, int) and i == 0) else 0

        class Unit:

            def __init__(self, i, odd, kind):
                k = {"a": -1, "d": 0, "v": 1}[kind]
                if isinstance(i, int) and i == 0:
                    self.u, self.slot = {"a": 0, "v": 1}[kind], {"a": 0, "v": 1}[kind]
                else:
                    self.u = 3 * i + k
                    self.slot = (3 * odd + k) % 2
                self.i, self.kind = i, kind
                self.u_even = self.u - self.slot

            def loads(self):
                return 8 * self.u_even + 16

        def load(sp, un):
            if not isinstance(un.u, int) or un.u >= 2:
                sp.wait_ge(w_lo_done, un.u - 1)
            dst = w_raw[:, un.slot, :]
            if un.kind == "d":
                src = down[bass.ds(256 * (un.i - 1), 256), :].rearrange("(j p) c -> p j c", p=P)
                dst = dst.rearrange("p (j c) -> p j c", j=2)
            else:
                src = up[:, bass.ds(256 * un.i + (DFF if un.kind == "v" else 0), 256)].rearrange("(k p) c -> p k c", p=P)
                dst = cols(dst, 256)
            sp.dma_start(dst, src).then_inc(raw_in[un.slot], 16)

        def split_hi(act, un, used):
            act.wait_ge(raw_in[un.slot], un.loads())
            if used is not None:
                act.wait_ge(full, used)
            nc.scalar.activation(w_hi[:, un.slot, :], w_raw[:, un.slot, :], ACT.Copy).then_inc(w_hi_done, 1)

        def split_lo(pool, un):
            pool.wait_ge(w_hi_done, un.u + 1)
            nc.gpsimd.tensor_tensor(w_lo[:, un.slot, :], w_raw[:, un.slot, :], w_hi[:, un.slot, :].bitcast(F32),
                                    ALU.subtract).then_inc(w_lo_done, 1)

        def grid(j, dy, dx):
            return pad[:, j, 0:GRID].rearrange("p (r c) -> p r c", c=PADW)[:, dy:dy + GRID_H, dx:dx + GRID_W]

        def row(j, dx):
            return pad[:, j, GRID + dx:GRID + dx + LP]

        def image(a):
            return a[:, 0:LS].rearrange("p (r c) -> p r c", c=GRID_W)

        def steps(eng, body, last):
            body(0, 0)
            with eng.Fori(0, (STEPS - 1) // 2) as turn:
                body(2 * turn + 1, 1)
                body(2 * turn + 2, 0)
            last(STEPS, 1)

        @blk.sync
        def _(sp):
            def body(i, odd):
                if not isinstance(i, int):
                    load(sp, Unit(i, odd, "a"))
                    load(sp, Unit(i, odd, "d"))
                    load(sp, Unit(i, odd, "v"))
                else:
                    load(sp, Unit(0, 0, "a"))
                    load(sp, Unit(0, 0, "v"))

            def last(i, odd):
                un = Unit(i, odd, "a")
                un.kind = "d"
                load(sp, un)
            steps(sp, body, last)

        @blk.gpsimd
        def _(pool):
            nc.gpsimd.memset(pad[:], 0.0).then_inc(pads_zero, 1)
            view = par[:, PA["ffn_conv_w"]:PA["ffn_conv_w"] + (TAPS + 1) * 2 * JF].rearrange("p (t b) -> p t b", b=2 * JF)

            def fetch_taps(i, odd):
                if not (isinstance(i, int) and i < 2):
                    pool.wait_ge(conv_done, 4 * i - 3)
                for half in range(2):
                    nc.gpsimd.tensor_copy(taps[:, odd, half], view[:, :, bass.ds(2 * i + JF * half, 2)]).then_inc(taps_ready, 1)

            def gated_lo(i, j):
                pool.wait_ge(g_hi_done, 2 * i + j + 1)
                nc.gpsimd.tensor_tensor(g_lo[:, j, :], acc_a[:, j, :], g_hi[:, j, :].bitcast(F32), ALU.subtract)\
                  .then_inc(g_lo_done, 1)

            def body(i, odd):
                if isinstance(i, int):
                    split_lo(pool, Unit(0, 0, "a"))
                    split_lo(pool, Unit(0, 0, "v"))
                    fetch_taps(0, 0)
                else:
                    split_lo(pool, Unit(i, odd, "d"))
                    fetch_taps(i, odd)
                    gated_lo(i - 1, 0)
                    gated_lo(i - 1, 1)
                    split_lo(pool, Unit(i, odd, "v"))
                split_lo(pool, Unit(i + 1, 1 - odd, "a"))

            def last(i, odd):
                gated_lo(i - 1, 0)
                gated_lo(i - 1, 1)
            steps(pool, body, last)

        @blk.scalar
        def _(act):
            def copy_out(i, loc, odd):
                first = isinstance(i, int)
                n = products(i) + (loc if first else (0, 1, 6, 11)[loc])
                slot = ps[:, 3 * (loc % 2):3 * (loc % 2) + 3, :]
                j = loc % 2
                act.wait_ge(full, n + 1)
                if first and loc < 2:
                    act.wait_ge(pads_zero, 1)
                else:
                    act.wait_ge(conv_done, 4 * i + loc - 1)
                g = pad[:, j, 0:GRID].rearrange("p (r c) -> p r c", c=PADW)
                nc.scalar.activation(g[:, 1:13, 1:65].rearrange("p (b r) c -> p b r c", b=2),
                                     slot[:, 0:2, 0:BW].rearrange("p b (r c) -> p b r c", c=GRID_W), ACT.Copy)
                nc.scalar.activation(g[:, 13:17, 1:65], slot[:, 2, 0:256].rearrange("p (r c) -> p r c", c=GRID_W), ACT.Copy)
                nc.scalar.activation(pad[:, j, GRID + 1:GRID + 1 + LP], slot[:, 2, 256:BW], ACT.Copy).then_inc(evac, 1)
                if loc == 0:
                    act.wait_ge(taps_ready, 2 * i + 2)
                act.wait_ge(evac, 4 * i + loc + 1)
                half = loc // 2
                if half == 0:
                    if not first:
                        act.wait_ge(g_lo_done, 2 * i - 1 + j)
                    acc = acc_a[:, j, :]
                else:
                    if not first:
                        act.wait_ge(gated, 2 * i - 1 + j)
                    acc = acc_v[:, j, :]
                tp = taps[:, odd, half, :, j:j + 1]
                nc.scalar.activation(image(acc), grid(j, 0, 0), ACT.Identity, scale=tp[:, 0], bias=tp[:, TAPS])
                nc.scalar.activation(acc[:, LS:T], row(j, 0), ACT.Identity, scale=tp[:, 3], bias=tp[:, TAPS])\
                  .then_inc(tap0_done, 1)

            def silu(i, j):
                act.wait_ge(conv_done, 4 * i + j + 1)
                nc.scalar.activation(acc_a[:, j, :], acc_a[:, j, :], ACT.Silu).then_inc(silu_done, 1)

            def gated_hi(i, j):
                act.wait_ge(gated, 2 * i + j + 1)
                nc.scalar.activation(g_hi[:, j, :], acc_a[:, j, :], ACT.Copy).then_inc(g_hi_done, 1)

            def body(i, odd):
                if isinstance(i, int):
                    split_hi(act, Unit(0, 0, "a"), None)
                    split_hi(act, Unit(0, 0, "v"), None)
                else:
                    split_hi(act, Unit(i, odd, "d"), products(i))
                    gated_hi(i - 1, 0)
                copy_out(i, 0, odd)
                if not isinstance(i, int):
                    gated_hi(i - 1, 1)
                copy_out(i, 1, odd)
                if not isinstance(i, int):
                    split_hi(act, Unit(i, odd, "v"), products(i) + 2)
                silu(i, 0)
                silu(i, 1)
                copy_out(i, 2, odd)
                split_hi(act, Unit(i + 1, 1 - odd, "a"), 2 if isinstance(i, int) else products(i) + 11)
                copy_out(i, 3, odd)

            def last(i, odd):
                gated_hi(i - 1, 0)
                gated_hi(i - 1, 1)
            steps(act, body, last)

        @blk.vector
        def _(dve):
            OWN = 4 * 8

            def tap(i, loc, odd, acc, t):
                j, half = loc % 2, loc // 2
                tp = taps[:, odd, half, :, j:j + 1]
                if t == 1:
                    dve.wait_ge(tap0_done, 4 * i + loc + 1)
                else:
                    dve.wait_ge(step_sem, OWN * i + 8 * loc + t - 1)
                nc.vector.scalar_tensor_tensor(out=image(acc), in0=grid(j, t // 3, t % 3), scalar=tp[:, t], in1=image(acc),
                                               op0=ALU.mult, op1=ALU.add).then_inc(step_sem, 1)
                if t in (1, 2):
                    if t == 2:
                        dve.wait_ge(row_sem, 8 * i + 2 * loc + 1)
                    nc.vector.scalar_tensor_tensor(out=acc[:, LS:T], in0=row(j, t), scalar=tp[:, 3 + t], in1=acc[:, LS:T],
                                                   op0=ALU.mult, op1=ALU.add).then_inc(row_sem, 1)
                if t == TAPS - 1:
                    dve.wait_ge(row_sem, 8 * i + 2 * loc + 2)
                    dve.wait_ge(step_sem, OWN * i + 8 * loc + 8)
                    dve.sem_inc(conv_done, 1)

            def conv(i, loc, odd, acc):
                for t in range(1, TAPS):
                    tap(i, loc, odd, acc, t)

            def down_add(n, cb, slot):
                dve.wait_ge(full, n + 1)
                add_gated(nc, ps[:, 3 * slot:3 * slot + 3, :], x[:, cb, :], mem["mod"][:, 40 + cb, :]).then_inc(added, 1)

            def gate(i, j):
                dve.wait_ge(silu_done, 2 * i + j + 1)
                nc.vector.tensor_tensor(acc_a[:, j, :], acc_a[:, j, :], acc_v[:, j, :], ALU.mult).then_inc(gated, 1)

            def body(i, odd):
                conv(i, 0, odd, acc_a[:, 0, :])
                for loc, acc, cb0, at_ in ((1, acc_a[:, 1, :], 0, 2), (2, acc_v[:, 0, :], 4, 7)):
                    for t in range(1, TAPS):
                        if t <= 4 and not isinstance(i, int):
                            cb = cb0 + t - 1
                            down_add(products(i) + at_ + t - 1, cb, (at_ + t - 1) % 2)
                        tap(i, loc, odd, acc, t)
                gate(i, 0)
                conv(i, 3, odd, acc_v[:, 1, :])
                gate(i, 1)

            def last(i, odd):
                for cb in range(KD):
                    down_add(products(i) + cb, cb, cb % 2)
            dve.sem_inc(added, 1)
            steps(dve, body, last)

        @blk.tensor
        def _(pe):
            def up_product(un, i, loc):
                wh, wl = cols(w_hi[:, un.slot, :], 256), cols(w_lo[:, un.slot, :], 256)
                j = loc % 2
                if j == 0:
                    pe.wait_ge(w_lo_done, un.u + 1)
                slot = ps[:, 3 * j:3 * j + 3, :]
                c = j * P
                product(nc, [slot[:, b, 0:BW] for b in range(NB)], lambda k: wh[:, k, c:c + P], lambda k: wl[:, k, c:c + P],
                        lambda k, b: h_hi[:, k, b * BW:(b + 1) * BW], lambda k, b: h_lo[:, k, b * BW:(b + 1) * BW],
                        range(KD)).then_inc(full, 1)

            def down_product(un, cb, s):
                wh = w_hi[:, un.slot, :].rearrange("p (j c) -> p j c", j=2)
                wl = w_lo[:, un.slot, :].rearrange("p (j c) -> p j c", j=2)
                slot = ps[:, 3 * s:3 * s + 3, :]
                c = cb * P
                product(nc, [slot[:, b, 0:BW] for b in range(NB)], lambda k: wh[:, k, c:c + P], lambda k: wl[:, k, c:c + P],
                        lambda k, b: g_hi[:, k, b * BW:(b + 1) * BW], lambda k, b: g_lo[:, k, b * BW:(b + 1) * BW],
                        range(2)).then_inc(full, 1)

            def sums(i, n):
                pe.wait_ge(added, 8 * i - 8 + n + 1)

            def body(i, odd):
                a, v = Unit(i, odd, "a"), Unit(i, odd, "v")
                if isinstance(i, int):
                    for loc in range(4):
                        if loc >= 2:
                            pe.wait_ge(evac, loc - 1)
                        up_product(a if loc < 2 else v, i, loc)
                    return
                d = Unit(i, odd, "d")
                sums(i, 0)
                pe.wait_ge(evac, 4 * i - 1)
                up_product(a, i, 0)
                pe.wait_ge(evac, 4 * i)
                up_product(a, i, 1)
                pe.wait_ge(w_lo_done, d.u + 1)
                pe.wait_ge(g_lo_done, 2 * i)
                for cb in range(4):
                    if cb < 2:
                        pe.wait_ge(evac, 4 * i + 1 + cb)
                    else:
                        sums(i, cb - 1)
                    down_product(d, cb, cb % 2)
                sums(i, 3)
                up_product(v, i, 2)
                for cb in range(4, 8):
                    if cb == 5:
                        pe.wait_ge(evac, 4 * i + 3)
                    else:
                        sums(i, cb if cb == 4 else cb - 1)
                    down_product(d, cb, (cb + 1) % 2)
                sums(i, 7)
                up_product(v, i, 3)

            def last(i, odd):
                d = Unit(i, odd, "a")
                pe.wait_ge(w_lo_done, d.u + 1)
                pe.wait_ge(g_lo_done, 2 * i)
                pe.wait_ge(evac, 4 * i)
                for cb in range(KD):
                    sums(i, max(cb - 1, 0))
                    down_product(d, cb, cb % 2)
            steps(pe, body, last)


def final_norm(nc, io, mem, x):
    ps, par = mem["psum"], mem["par"]
    with Phase(nc, "final") as ph:
        square_ring = ph.sb("squares", [P, 2, T])
        xn = ph.sb("xn", [P, KD, T])
        y = ph.sb("y", [P, 3, D])
        xn_done = ph.sem("xn_done")
        tr = ph.sem("transposed")
        cp = ph.sem("copied")
        stored = [ph.sem(f"stored{i}") for i in range(3)]

        def finish(act, k, t, used):
            w0 = PA["final_norm_w"] + k
            act.activation(xn[:, k, :], t, ACT.Copy, scale=par[:, w0:w0 + 1]).then_inc(used, 1)

        on_act, on_pe, on_dve = norm_steps(nc, ph, mem, x, None, square_ring, finish)
        used = [s for s in ph.sems if s.name.endswith("normed_used")][0]
        blk = ph.block()

        @blk.sync
        def _(sp):
            for t in range(NT):
                sp.wait_ge(cp, 2 * t + 2)
                dst = io["y_sample"][0, t * P:(t + 1) * P, :] if t < 8 else io["y_prompt"][0]
                sp.dma_start(dst, y[:, t % 3, :]).then_inc(stored[t % 3], 16)
            for i in range(3):
                sp.wait_ge(stored[i], 48)

        @blk.scalar
        def _(act):
            on_act(lambda eng, k: None)
            for n in range(2 * NT):
                t = n // 2
                act.wait_ge(tr, n + 1)
                if t >= 3:
                    act.wait_ge(stored[t % 3], 16 * (t // 3))
                nc.scalar.activation(y[:, t % 3, 512 * (n % 2):512 * (n % 2) + 512], ps[:, n % 8, :], ACT.Copy).then_inc(cp, 1)

        @blk.tensor
        def _(pe):
            on_pe()
            pe.wait_ge(used, KD)
            for n in range(2 * NT):
                t, half = n // 2, n % 2
                if n >= 8:
                    pe.wait_ge(cp, n - 7)
                for j in range(4):
                    last = nc.tensor.transpose(ps[:, n % 8, j * P:(j + 1) * P], xn[:, 4 * half + j, t * P:(t + 1) * P], mem["ident"][:])
                last.then_inc(tr, 1)

        @blk.vector
        def _(dve):
            on_dve(lambda eng, k: None)


OUTS = [("y_prompt", (1, LP, D)), ("y_sample", (1, LS, D)), ("new_C", (1, 1, 2, HEADS, HD, HD)),
        ("new_n", (1, 1, 2, HEADS, HD)), ("new_m", (1, 1, 2, HEADS))]


def build(nc, io, stop=99):
    with ExitStack() as ctx:
        def sb(name, shape, dt=F32):
            return ctx.enter_context(nc.sbuf_tensor(name, shape, dt))

        mem = {"psum": ctx.enter_context(nc.psum_tensor("psum", [P, 8, 512], F32)),
               "par": sb("par", [P, NPAR]), "mod": sb("mod", [P, 48, 2]),
               "gain_mix": sb("gain_mix", [P, KD, 2]), "gain_ffn": sb("gain_ffn", [P, KD, 2]),
               "ident": sb("ident", [P, P]), "ones": sb("ones", [P, P]),
               "filter_gain": sb("filter_gain", [P, 2 * CH]),
               "w_raw": sb("w_raw", [P, 2, UNIT]), "w_hi": sb("w_hi", [P, 2, UNIT], F32R),
               "w_lo": sb("w_lo", [P, 2, UNIT], F32R)}
        dram = {n: nc.dram_tensor(f"scratch_{n}", shape, F32).ap() for n, shape in dict(
            x0=(CH, P, T), hv=(CH, P, T), q=(CH, P, T), k=(CH, P, T),
            v=(NT, P, DH), o=(NT, P, DH), y=(KD, P, T), scan_rows=(2, 2 * HEADS, T),
            kt=(4, P, 4, DH), kt_prompt=(P, 2, DH)).items()}
        
        with Phase(nc, "init") as ph:
            blk = ph.block()

            @blk.vector
            def _(dve):
                nc.vector.memset(mem["ones"][:], 1.0)
        phase_filters(nc, io, mem, dram)
        with Phase(nc, "front") as front:
            mem.update(gates=front.sb("gates", [P, T]))
            for f in (phase_project, phase_hyena, phase_mlstm)[:max(0, stop - 2)]:
                f(nc, io, mem, dram)
        if stop > 5:
            phase_out(nc, io, mem, dram)
        return mem, dram


def kernel(**inputs):
    import concourse.bacc as bacc
    from concourse.bass_utils import run_bass_kernel_spmd

    nc = bacc.Bacc("TRN2", target_bir_lowering=False, num_devices=1)
    arrays = {n: np.ascontiguousarray(a) for n, a in inputs.items()}
    arrays.update(constants())
    io = {n: nc.dram_tensor(n, a.shape, F32, kind="ExternalInput").ap() for n, a in arrays.items()}
    for n, shape in OUTS:
        io[n] = nc.dram_tensor(n, shape, F32, kind="ExternalOutput").ap()
    build(nc, io)
    r = run_bass_kernel_spmd(nc, [arrays], core_ids=[0])
    return tuple(np.asarray(r.results[0][n]) for n, _ in OUTS)
```

```python
import math
from contextlib import ExitStack

import numpy as np

import concourse.bass as bass
from concourse import mybir

F32 = mybir.dt.float32
F32R = mybir.dt.float32r
ALU = mybir.AluOpType
ACT = mybir.ActivationFunctionType

P = 128
D = 1024
KD = D // P
LS, LP = 1024, 128
T = LS + LP
NB, BW = 3, 384
assert NB * BW == T
DH = 512
CH = DH // P
HEADS, HD = 4, 128
DFF = 2816
JF = DFF // P
QOFF, KOFF, VOFF, OOFF, GOFF = 3 * DH, 4 * DH, 5 * DH, 6 * DH, 7 * DH
W_IN_UNITS = [256 * i for i in range(6)] + [QOFF + 256 * i for i in range(8)]
EPS = 1e-6
UNIT = 2048
NT = T // P
ROWS = 64

PA = {}
at = 0
for name, n in (("ada_b", 48), ("norm_mix_w", 8), ("norm_ffn_w", 8), ("final_norm_w", 8),
                ("hy_conv_b", 12), ("hy_bias", 4), ("ml_conv_b", 8), ("ml_norm_w", 4)):
    PA[name] = at
    at += n
PA["hy_conv_w"] = 128
PA["ml_conv_w"] = 128 + 36
PA["cond"] = 128 + 60
PA["filter_vec"] = 128 + 76
PA["ffn_conv_w"] = 256
PA["ffn_conv_b"] = 256 + 9 * 44
NPAR = 256 + 440
FROWS = 110


def lin(start, stop, n):
    step = np.arange(n, dtype=np.float32) / np.float32(n - 1)
    out = np.float32(start) * (np.float32(1) - step) + np.float32(stop) * step
    out[-1] = np.float32(stop)
    return out.astype(np.float32)


def positions(L):
    t = lin(0.0, 1.0, L)[:, None]
    wpos = np.float32(2.0 * math.pi / L) * np.arange(L, dtype=np.float32)[:, None]
    arg = (lin(1e-4, 15, 16)[None, :] * wpos).astype(np.float32).astype(np.float64)
    z = np.concatenate([t, np.cos(arg), -np.sin(arg)], axis=1).astype(np.float32)
    dmin, dmax = math.log(1e-2) / 1.5, math.log(1e-2) / 0.3
    deltas = np.abs(lin(dmin, dmax, DH))
    decay = np.exp((-t * deltas[None, :]).astype(np.float64)).astype(np.float32)
    return z, decay


def constants():
    zs, ds = positions(LS)
    zp, dp = positions(LP)
    zT = np.concatenate([zs, zp], 0).T.copy()
    decay = np.stack([ds[p + 256 * b:p + 256 * (b + 1):2] for p in (0, 1) for b in range(4)] + [dp])
    k = np.arange(512)[None, :]
    s = np.arange(512)[:, None]
    fwd = []
    for p in (0, 1):
        fwd.append(np.cos(2 * np.pi * ((k * (2 * s + p)) % 2048) / 2048))
    for p in (0, 1):
        m = np.sin(2 * np.pi * ((k * (2 * s + p)) % 2048) / 2048)
        m[:, 0] = (-1.0) ** s[:, 0]
        fwd.append(m)
    weight = np.full((512, 1), 2.0 / 2048)
    weight[0] = 1.0 / 2048
    inv = [fwd[0].T * weight, None, fwd[1].T * weight, None]
    for p in (0, 1):
        m = fwd[2 + p].T * (2.0 / 2048)
        inv[2 * p + 1] = m
    f = np.stack(fwd).reshape(4, 4, P, 4, P)
    fwd_units = f.transpose(3, 2, 0, 1, 4).reshape(4, P, UNIT)
    inv_units = np.stack(inv).reshape(4, 4, P, 512).transpose(0, 2, 1, 3).reshape(4, P, UNIT)
    tt = np.arange(P)[:, None]
    kk = np.arange(P)[None, :]
    c = np.cos(2 * np.pi * (tt * kk % 256) / 256)
    sn = np.sin(2 * np.pi * (tt * kk % 256) / 256)
    sn[:, 0] = (-1.0) ** tt[:, 0]
    wc = np.full((P, 1), 2.0 / 256)
    wc[0] = 1.0 / 256
    prompt = np.stack([c, sn, c.T * wc, sn.T * wc], 1).reshape(P, 4 * P)
    ident = np.eye(P)
    i = np.arange(P)
    mask = np.stack([np.where(i[:, None] <= i[None, :], 0.0, 1e30),
                     np.where(i[:, None] >= i[None, :], 0.0, 1e30)], 1)
    sel = np.zeros((ROWS, 8, P))
    for d in range(2):
        for h in range(HEADS):
            sel[32 * d + h, 4 * d + h] = 1.0
    reset = np.ones((ROWS, T))
    reset[0:32, 0::P] = 0.0
    reset[32:64, P - 1::P] = 0.0
    return {n: np.ascontiguousarray(a, dtype=np.float32) for n, a in dict(
        k_z=zT, k_decay=decay, k_fwd=fwd_units, k_inv=inv_units, k_prompt=prompt,
        k_ident=ident, k_mask=mask, k_sel=sel, k_reset=reset).items()}


class Chain:

    def __init__(self, eng, sem):
        self.eng, self.sem, self.n = eng, sem, 0

    def do(self, ins):
        self.n += 1
        ins.then_inc(self.sem, 1)
        self.eng.wait_ge(self.sem, self.n)


class WeightRing:

    def __init__(self, nc, ph, mem, used_at, ahead=0, first=0):
        self.nc, self.mem, self.ahead, self.first = nc, mem, ahead, first
        self.raw_in = [ph.sem(f"weights_loaded{i}") for i in range(2)]
        self.hi_done = ph.sem("weights_hi")
        self.lo_done = ph.sem("weights_lo")
        self.used_at = used_at

    def slot(self, u):
        return (u + self.first) % 2

    def raw(self, u):
        return self.mem["w_raw"][:, self.slot(u), :]

    def hi(self, u):
        return self.mem["w_hi"][:, self.slot(u), :]

    def lo(self, u):
        return self.mem["w_lo"][:, self.slot(u), :]

    def load(self, sp, u, src, view=None):
        if u - 1 > self.ahead:
            sp.wait_ge(self.lo_done, u - 1 - self.ahead)
        dst = self.raw(u) if view is None else view(self.raw(u))
        sp.dma_start(dst, src).then_inc(self.raw_in[self.slot(u)], 16)

    def split_hi(self, act, u, n=UNIT):
        act.wait_ge(self.raw_in[self.slot(u)], 16 * ((u - self.ahead) // 2 + 1))
        if u >= 2:
            act.wait_ge(*self.used_at(u - 2))
        self.nc.scalar.activation(self.hi(u)[:, 0:n], self.raw(u)[:, 0:n], ACT.Copy).then_inc(self.hi_done, 1)

    def split_lo(self, pool, u, n=UNIT):
        pool.wait_ge(self.hi_done, u + 1 - self.ahead)
        pool.tensor_tensor(self.lo(u)[:, 0:n], self.raw(u)[:, 0:n], self.hi(u)[:, 0:n].bitcast(F32),
                           ALU.subtract).then_inc(self.lo_done, 1)

    def ready(self, pe, u):
        if u >= self.ahead:
            pe.wait_ge(self.lo_done, u + 1 - self.ahead)


def load_w_in(sp, ring, io, u):
    c0 = W_IN_UNITS[u]
    ring.load(sp, u, io["w_in"][0, :, c0:c0 + 256].rearrange("(k p) c -> p k c", p=P), lambda r: cols(r, 256))


def load_forward(sp, ring, io, u, at=0):
    if u == 0:
        ring.load(sp, at, io["k_prompt"], lambda r: r[:, 0:4 * P])
    else:
        ring.load(sp, at + u, io["k_fwd"][u - 1])


def forward_width(u):
    return 4 * P if u == 0 else UNIT


def load_w_out(sp, ring, io, u, at=0):
    ring.load(sp, at + u, io["w_out"][0, :, 256 * u:256 * u + 256].rearrange("(k p) c -> p k c", p=P), lambda r: cols(r, 256))


def cols(u, width):
    return u.rearrange("p (k c) -> p k c", c=width)


def product(nc, banks, w_hi, w_lo, x_hi, x_lo, chunks, first=True, last=True):
    ins = None
    for n, k in enumerate(chunks):
        wh, wl = w_hi(k), w_lo(k)
        begin, end = first and n == 0, last and n == len(chunks) - 1
        for i, out in enumerate(banks):
            ins = nc.tensor.matmul(out, wh, x_hi(k, i), start=begin, stop=False)
        for i, out in enumerate(banks):
            ins = nc.tensor.matmul(out, wh, x_lo(k, i), start=False, stop=False)
        for i, out in enumerate(banks):
            ins = nc.tensor.matmul(out, wl, x_hi(k, i), start=False, stop=end)
    return ins


class Phase:

    cleared = None

    def __init__(self, nc, name):
        self.nc, self.name, self.ctx, self.sem_ctx, self.sems = nc, name, ExitStack(), ExitStack(), []

    def __enter__(self):
        self.in_block = None
        self.ctx.__enter__()
        self.sem_ctx.__enter__()
        return self

    def __exit__(self, *a):
        if self.in_block:
            self.in_block.close()
        if self.sems:
            for s in self.sems:
                self.nc.gpsimd.sem_clear(s)
            if Phase.cleared:
                Phase.cleared.close()
            Phase.cleared = self.sem_ctx
        return self.ctx.__exit__(*a)

    def sb(self, name, shape, dt=F32, side="left"):
        return self.ctx.enter_context(self.nc.sbuf_tensor(f"{self.name}_{name}", shape, dt, side=side))

    def sem(self, name):
        self.sems.append(self.sem_ctx.enter_context(self.nc.semaphore(f"{self.name}_{name}")))
        return self.sems[-1]

    def block(self):
        self.in_block = ExitStack()
        return self.in_block.enter_context(self.nc.Block())


class RowNorm:

    def __init__(self, nc, io, ph):
        self.nc, self.io = nc, io
        self.x = ph.sb("x", [P, NT, D])
        self.square = ph.sb("square", [P, D])
        self.sum_sq, self.mean_sq, self.root, self.rstd = (ph.sb(n, [P, NT]) for n in ("sum_sq", "mean_sq", "root", "rstd"))

    def semaphores(self, ph):
        self.x_in = [ph.sem(f"x_in{t}") for t in range(NT)]
        self.summed = ph.sem("squares_summed")
        self.means = ph.sem("mean_squares")
        self.roots = ph.sem("roots")
        self.rstds = ph.sem("rstds")

    def load(self, sp, g):
        for t in range(3 * g, 3 * g + 3):
            src = self.io["x_sample"][0, t * P:(t + 1) * P, :] if t < 8 else self.io["x_prompt"][0]
            sp.dma_start(self.x[:, t, :], src).then_inc(self.x_in[t], 16)

    def squares(self, act, g):
        for t in range(3 * g, 3 * g + 3):
            act.wait_ge(self.x_in[t], 16)
            if t:
                act.wait_ge(self.summed, t)
            self.nc.scalar.activation(self.square[:], self.x[:, t, :], ACT.Square, accum_out=self.sum_sq[:, t:t + 1])\
                .then_inc(self.summed, 1)

    def mean(self, dve, g):
        s = slice(3 * g, 3 * g + 3)
        dve.wait_ge(self.summed, 3 * g + 3)
        self.nc.vector.tensor_scalar(self.mean_sq[:, s], self.sum_sq[:, s], 1.0 / D, EPS, ALU.mult, ALU.add).then_inc(self.means, 1)

    def take_root(self, act, g):
        s = slice(3 * g, 3 * g + 3)
        act.wait_ge(self.means, g + 1)
        self.nc.scalar.activation(self.root[:, s], self.mean_sq[:, s], ACT.Sqrt).then_inc(self.roots, 1)

    def scale(self, dve, g):
        s = slice(3 * g, 3 * g + 3)
        dve.wait_ge(self.roots, g + 1)
        self.nc.vector.reciprocal(self.rstd[:, s], self.root[:, s]).then_inc(self.rstds, 1)
        dve.wait_ge(self.rstds, g + 1)
        for t in range(3 * g, 3 * g + 3):
            self.nc.vector.tensor_scalar_mul(self.x[:, t, :], self.x[:, t, :], self.rstd[:, t:t + 1])


def mixing_norm(nc, io, mem, x, h_hi, h_lo):
    G, FULL = NT // 3, 6
    with Phase(nc, "norm1") as ph:
        full = ph.sb("h_full", [P, FULL, BW])
        turned = ph.sem("chunk_transposed")
        full_done = ph.sem("h_full_done")
        hi_done = ph.sem("h_hi_done")
        lo_by = {"pool": ph.sem("lo_by_pool"), "dve": ph.sem("lo_by_dve")}
        ps = mem["psum"]
        ring = WeightRing(nc, ph, mem, None)
        blk = ph.block()

        def splitter(n):
            return "dve" if n % 3 == 2 else "pool"

        def wait_lo(eng, n):
            eng.wait_ge(lo_by[splitter(n)], sum(splitter(i) == splitter(n) for i in range(n + 1)))

        def split_lo(eng, n):
            g, k = n // KD, n % KD
            eng.wait_ge(hi_done, n + 1)
            eng.tensor_tensor(h_lo[:, k, g * BW:(g + 1) * BW], full[:, n % FULL, :],
                              h_hi[:, k, g * BW:(g + 1) * BW].bitcast(F32), ALU.subtract).then_inc(lo_by[splitter(n)], 1)

        @blk.sync
        def _(sp):
            for u in range(2):
                load_w_in(sp, ring, io, u)

        @blk.tensor
        def _(pe):
            for n in range(G * KD):
                g, k = n // KD, n % KD
                if n >= 8:
                    pe.wait_ge(full_done, n - 7)
                for i in range(3):
                    last = nc.tensor.transpose(ps[:, n % 8, i * P:(i + 1) * P], x[:, 3 * g + i, k * P:(k + 1) * P],
                                               mem["ident"][:])
                last.then_inc(turned, 1)

        @blk.vector
        def _(dve):
            for n in range(G * KD):
                g, k = n // KD, n % KD
                dve.wait_ge(turned, n + 1)
                if n >= FULL:
                    wait_lo(dve, n - FULL)
                parts = ((0, BW, 0),) if g < G - 1 else ((0, BW - LP, 0), (BW - LP, BW, 1))
                for a, b, j in parts:
                    ins = nc.vector.tensor_scalar(full[:, n % FULL, a:b], ps[:, n % 8, a:b], mem["gain_mix"][:, k, j:j + 1],
                                                  mem["mod"][:, k, j:j + 1], ALU.mult, ALU.add)
                ins.then_inc(full_done, 1)
                if n >= 2 and splitter(n - 2) == "dve":
                    split_lo(nc.vector, n - 2)
                if n == 9:
                    ring.split_lo(nc.vector, 0)
            split_lo(nc.vector, G * KD - 1)

        @blk.scalar
        def _(act):
            for n in range(G * KD):
                g, k = n // KD, n % KD
                if n in (4, 12):
                    ring.split_hi(act, n // 8)
                act.wait_ge(full_done, n + 1)
                nc.scalar.activation(h_hi[:, k, g * BW:(g + 1) * BW], full[:, n % FULL, :], ACT.Copy).then_inc(hi_done, 1)

        @blk.gpsimd
        def _(pool):
            for n in range(G * KD):
                if splitter(n) == "pool":
                    split_lo(nc.gpsimd, n)
            ring.split_lo(pool, 1)


def phase_project(nc, io, mem, dram, h_hi, h_lo):
    with Phase(nc, "proj") as ph:
        ps = mem["psum"]
        gw = ph.sb("gate_w", [P, KD, P])
        gh = ph.sb("gate_w_hi", [P, KD, P], F32R)
        gl = ph.sb("gate_w_lo", [P, KD, P], F32R)
        gb = ph.sb("gate_bias", [P, 1])
        pad = ph.sb("pad", [P, 2, T + 4])
        taps = ph.sb("taps", [P, T])
        x1 = ph.sb("x1", [P, CH, T])
        silu = ph.sb("silu", [P, 2, T])
        stage = ph.sb("stage", [P, 2, T])
        gw_zero = ph.sem("gate_w_zero")
        gw_in = ph.sem("gate_w_in")
        gw_hi = ph.sem("gate_w_hi_done")
        gw_lo = ph.sem("gate_w_lo_done")
        full = ph.sem("product_done")
        evac = ph.sem("product_copied")
        conved = ph.sem("conv_done")
        silued = ph.sem("silu_done")
        staged = [ph.sem(f"staged{i}") for i in range(2)]
        stored = [ph.sem(f"stored{i}") for i in range(2)]
        step_sem = ph.sem("dve_step")
        pads_zero = ph.sem("pads_zero")

        G = io["w_in"][0, :, GOFF:GOFF + 16].rearrange("(k p) c -> p k c", p=P)
        gate_at = ((0, 0), (8, 32), (4, 64), (12, 96))
        units = W_IN_UNITS
        AFTER = len(units)
        items = []
        for u, c0 in enumerate(units):
            if VOFF <= c0 < GOFF:
                items += [("tokens", g, u) for g in range(3)]
            else:
                items += [("block", c0 // P + b, u) for b in range(2)]
            if u == 0:
                items.append(("gates", 0, 0))
        NQ = QOFF // P
        ring = WeightRing(nc, ph, mem, lambda u: (full, 1 + max(n for n, item in enumerate(items) if item[2] == u)), ahead=2)

        def kinds():
            conv = ml = st = 0
            for n, (what, b, u) in enumerate(items):
                yield n, what, b, u, conv, ml, st
                if what == "block":
                    conv += 1
                    ml += b >= NQ
                    st += not (CH <= b < 2 * CH)
                elif what == "tokens":
                    st += 1
        blk = ph.block()

        @blk.sync
        def _(sp):
            sp.wait_ge(gw_zero, 2)
            for c, p in gate_at:
                with nc.allow_non_contiguous_dma(reason="16 gate columns"):
                    sp.dma_start(gw[:, :, p:p + 4], G[:, :, c:c + 4]).then_inc(gw_in, 16)
                    sp.dma_start(gb[p:p + 4, :], io["b_gate"][0, c:c + 4].rearrange("(c o) -> c o", o=1)).then_inc(gw_in, 16)
            done = -1
            for n, what, b, u, conv, ml, st in kinds():
                if u > done:
                    if u + 2 < AFTER:
                        load_w_in(sp, ring, io, u + 2)
                    else:
                        load_forward(sp, ring, io, u + 2 - AFTER, AFTER)
                    done = u
                if what == "gates":
                    continue
                if what == "block" and CH <= b < 2 * CH:
                    continue
                sp.wait_ge(staged[st % 2], st // 2 + 1)
                src = stage[:, st % 2, :]
                if what == "tokens":
                    c0 = units[u]
                    name, off = ("v", c0 - VOFF) if c0 < OOFF else ("o", c0 - OOFF)
                    sp.dma_start(dram[name][3 * b:3 * b + 3, :, off:off + 256].rearrange("t p c -> p t c"),
                                 src[:, 0:768].rearrange("p (t c) -> p t c", c=256)).then_inc(stored[st % 2], 16)
                else:
                    name, j = (("x0", b) if b < CH else ("hv", b - 2 * CH) if b < NQ else
                               ("q", b - NQ) if b < NQ + 4 else ("k", b - NQ - 4))
                    sp.dma_start(dram[name][j], src).then_inc(stored[st % 2], 16)
            sp.wait_ge(ring.raw_in[ring.slot(AFTER + 1)], 16 * (AFTER // 2))
            n_st = st + 1
            sp.wait_ge(stored[0], 16 * ((n_st + 1) // 2))
            sp.wait_ge(stored[1], 16 * (n_st // 2))

        @blk.gpsimd
        def _(pool):
            nc.gpsimd.memset(gw[:], 0.0).then_inc(gw_zero, 1)
            nc.gpsimd.memset(gb[:], 0.0).then_inc(gw_zero, 1)
            nc.gpsimd.memset(pad[:], 0.0).then_inc(pads_zero, 1)
            pool.wait_ge(gw_hi, 1)
            nc.gpsimd.tensor_tensor(gl[:], gw[:], gh[:].bitcast(F32), ALU.subtract).then_inc(gw_lo, 1)
            done = -1
            for n, what, b, u, conv, ml, st in kinds():
                if u > done and 2 <= u + 1:
                    ring.split_lo(pool, u + 1, UNIT if u + 1 < AFTER else forward_width(0))
                done = u
                if what == "block" and b >= NQ:
                    pool.wait_ge(silued, ml + 1)
                    if st >= 2:
                        pool.wait_ge(stored[st % 2], 16 * (st // 2))
                    scale = 1.0 if b < NQ + 4 else HD ** -0.5
                    nc.gpsimd.tensor_scalar(stage[:, st % 2, :], silu[:, ml % 2, :], scale, 0.0, ALU.mult, ALU.add)\
                      .then_inc(staged[st % 2], 1)

        @blk.scalar
        def _(act):
            act.wait_ge(gw_in, 16 * 8)
            nc.scalar.activation(gh[:], gw[:], ACT.Copy).then_inc(gw_hi, 1)
            done = -1

            def silu_step(conv, ml, st):
                act.wait_ge(conved, conv + 1)
                if ml >= 2:
                    act.wait_ge(staged[st % 2], st // 2)
                nc.scalar.activation(silu[:, ml % 2, :], taps[:], ACT.Silu).then_inc(silued, 1)

            for n, what, b, u, conv, ml, st in kinds():
                if u > done and 2 <= u + 1:
                    ring.split_hi(act, u + 1, UNIT if u + 1 < AFTER else forward_width(0))
                done = u
                act.wait_ge(full, n + 1)
                slot = ps[:, 3 * (n % 2):3 * (n % 2) + 3, :]
                if what == "gates":
                    nc.scalar.activation(mem["gates"][:].rearrange("p (b c) -> p b c", c=BW), slot[:, :, 0:BW],
                                         ACT.Identity, bias=gb[:, 0:1]).then_inc(evac, 1)
                elif what == "tokens":
                    if st >= 2:
                        act.wait_ge(stored[st % 2], 16 * (st // 2))
                    func = ACT.Copy if units[u] < OOFF else ACT.Sigmoid
                    nc.scalar.activation(stage[:, st % 2, 0:768].rearrange("p (t c) -> p t c", c=256),
                                         slot[:, :, 0:256], func).then_inc(evac, 1)
                    act.wait_ge(evac, n + 1)
                    act.sem_inc(staged[st % 2], 1)
                else:
                    if conv >= 2:
                        act.wait_ge(conved, conv - 1)
                    else:
                        act.wait_ge(pads_zero, 1)
                    pd = pad[:, conv % 2, :]
                    nc.scalar.activation(pd[:, 1:769].rearrange("p (b c) -> p b c", c=BW), slot[:, 0:2, 0:BW], ACT.Copy)
                    nc.scalar.activation(pd[:, 769:1025], slot[:, 2, 0:256], ACT.Copy)
                    nc.scalar.activation(pd[:, 1027:1155], slot[:, 2, 256:384], ACT.Copy).then_inc(evac, 1)
                    if b >= NQ:
                        silu_step(conv, ml, st)

        @blk.vector
        def _(dve):
            step = Chain(dve, step_sem)
            for n, what, b, u, conv, ml, st in kinds():
                if what != "block":
                    continue
                dve.wait_ge(evac, n + 1)
                pd = pad[:, conv % 2, :]
                hy = b < NQ
                if hy:
                    wt, bt, width = PA["hy_conv_w"], PA["hy_conv_b"], 12
                    j = b
                else:
                    wt, bt, width = PA["ml_conv_w"], PA["ml_conv_b"], 8
                    j = b - NQ
                par = mem["par"]
                if hy and b < CH:
                    out = stage[:, st % 2, :]
                    if st >= 2:
                        dve.wait_ge(stored[st % 2], 16 * (st // 2))
                elif hy and b < 2 * CH:
                    out = x1[:, b - CH, :]
                elif hy:
                    out = taps[:]
                else:
                    out = taps[:]
                    if ml >= 1:
                        dve.wait_ge(silued, ml)
                for k in range(3):
                    wk = par[:, wt + k * width + j:wt + k * width + j + 1]
                    for (a, z, o) in ((0, LS, 0), (LS, T, 2)):
                        src = pd[:, a + o + k:z + o + k]
                        if k == 0:
                            ins = nc.vector.tensor_scalar(out[:, a:z], src, wk, par[:, bt + j:bt + j + 1], ALU.mult, ALU.add)
                        else:
                            ins = nc.vector.scalar_tensor_tensor(out=out[:, a:z], in0=src, scalar=wk, in1=out[:, a:z],
                                                                 op0=ALU.mult, op1=ALU.add)
                        if k == 2 and a:
                            ins.then_inc(conved, 1)
                        else:
                            step.n += 1
                            ins.then_inc(step_sem, 1)
                    if k < 2:
                        dve.wait_ge(step_sem, step.n)
                dve.wait_ge(conved, conv + 1)
                dve.wait_ge(step_sem, step.n)
                if hy and b < CH:
                    dve.sem_inc(staged[st % 2], 1)
                elif hy and b >= 2 * CH:
                    if st >= 2:
                        dve.wait_ge(stored[st % 2], 16 * (st // 2))
                    nc.vector.tensor_tensor(stage[:, st % 2, :], taps[:], x1[:, b - 2 * CH, :], ALU.mult).then_inc(staged[st % 2], 1)
                    dve.wait_ge(staged[st % 2], st // 2 + 1)

        @blk.tensor
        def _(pe):
            for n, what, b, u, conv, ml, st in kinds():
                if n >= 2:
                    pe.wait_ge(evac, n - 1)
                slot = ps[:, 3 * (n % 2):3 * (n % 2) + 3, :]
                if what == "gates":
                    pe.wait_ge(gw_lo, 1)
                    product(nc, [slot[:, i, 0:BW] for i in range(NB)], lambda k: gh[:, k, :], lambda k: gl[:, k, :],
                            lambda k, i: h_hi[:, k, i * BW:(i + 1) * BW], lambda k, i: h_lo[:, k, i * BW:(i + 1) * BW],
                            range(KD)).then_inc(full, 1)
                    continue
                ring.ready(pe, u)
                wh, wl = cols(ring.hi(u), 256), cols(ring.lo(u), 256)
                if what == "tokens":
                    for i in range(3):
                        t = 3 * b + i
                        ins = product(nc, [slot[:, i, 0:256]], lambda k: h_hi[:, k, t * P:(t + 1) * P],
                                      lambda k: h_lo[:, k, t * P:(t + 1) * P], lambda k, i: wh[:, k, :], lambda k, i: wl[:, k, :],
                                      range(KD))
                else:
                    c = (b % 2) * P
                    ins = product(nc, [slot[:, i, 0:BW] for i in range(NB)], lambda k: wh[:, k, c:c + P], lambda k: wl[:, k, c:c + P],
                                  lambda k, i: h_hi[:, k, i * BW:(i + 1) * BW], lambda k, i: h_lo[:, k, i * BW:(i + 1) * BW],
                                  range(KD))
                ins.then_inc(full, 1)


TWO_PI_PARTS = (6.28125, 0.0019350051879882812, 3.019916050561733e-07)
ROUND = 12582912.0


def modulation_and_taps(nc, io, mem, k_hi, k_lo):
    PARTS, AW, RING = 24, 512, 3
    HK = KD // 2
    BLOCKS = 6 * KD
    PIECES = ((0, 2), (2, 3))
    SHARED = 6
    SHARE = 1216
    with Phase(nc, "filt") as ph:
        rows = ph.sb("rows", [P, 6, P])
        cond_silu = ph.sb("cond_silu", [P, KD, 2])
        cond_hi = ph.sb("cond_hi", [P, KD, 2], F32R)
        cond_wide = ph.sb("cond_wide", [P, KD, P])
        cond = ph.sb("cond", [P, KD, P], F32R)
        ada_more = ph.sb("ada_more", [P, RING - 2, UNIT])
        part_rows = ph.sb("part_rows", [4, 2, AW])
        mod_rows = ph.sb("mod_rows", [BLOCKS, 4, P])
        w1 = ph.sb("w1", [33, 64])
        w2 = ph.sb("w2", [64, 64])
        w3 = ph.sb("w3", [64, 64])
        w4 = ph.sb("w4", [64, 2 * DH])
        vec = mem["par"][0:64, PA["filter_vec"]:PA["filter_vec"] + 4]
        h = ph.sb("h", [64, T])
        z = h[0:33, :]
        h_hi = ph.sb("h_hi", [64, T], F32R)
        h_lo = ph.sb("h_lo", [64, T], F32R)
        w4_hi, w4_lo = k_hi[0:64, :, NT - 1, :], k_lo[0:64, :, NT - 1, :]
        scratch = ph.sb("scratch", [P, 2, T])
        arg, turns = scratch[0:64, 0, :], scratch[0:64, 1, :]
        summed = scratch[:, :, 0:2 * DH].rearrange("p r (i c) -> p r i c", i=2)
        decay = ph.sb("decay", [P, 2, DH])
        taps = ph.sb("taps", [P, 2, 2, DH])
        size = ph.sb("size", [P, 2, 2, DH])
        absum = ph.sb("absum", [P, 2, 2, DH])
        norm = ph.sb("norm", [P, 2 * CH])
        zeroed = ph.sem("zeroed")
        ident_in = ph.sem("ident_in")
        rows_in = ph.sem("rows_in")
        rows1_in = ph.sem("rows1_in")
        mlp_in = ph.sem("mlp_inputs_in")
        decay_in = [ph.sem(f"decay_in{i}") for i in range(2)]
        ada_in = [ph.sem(f"ada_in{i}") for i in range(RING)]
        par_t = ph.sem("params_transposed")
        par_c = ph.sem("params_copied")
        silu_done = ph.sem("silu_done")
        cond_zero = ph.sem("conditions_zeroed")
        cond_hi_done = ph.sem("conditions_hi")
        cond_placed = ph.sem("conditions_placed")
        cond_ready = ph.sem("conditions_ready")
        part_copied = ph.sem("part_copied")
        part_moved = [ph.sem(f"part_moved{i}") for i in range(2)]
        mod_turned = ph.sem("mod_transposed")
        ada_hi = ph.sem("ada_hi")
        ada_lo = ph.sem("ada_lo")
        ada_lo_share = ph.sem("ada_lo_share")
        part_done = ph.sem("part_done")
        mm = ph.sem("mlp_product")
        arg_done = ph.sem("arg_done")
        sin_done = ph.sem("sin_done")
        w4_split = ph.sem("w4_split")
        h_split = ph.sem("h_split")
        w4_done = ph.sem("w4_product")
        tapped = ph.sem("taps_done")
        edge = ph.sem("edge_cleared")
        sums = ph.sem("sums")
        k_hi_done = ph.sem("k_hi_done")
        k_lo_done = ph.sem("k_lo_done")
        sized = ph.sem("sizes_done")
        absum_zero = ph.sem("absum_zero")
        accumulated = ph.sem("sizes_accumulated")
        norm_mm = ph.sem("norm_product")
        step_sem = ph.sem("dve_step")
        ps, par = mem["psum"], mem["par"]
        ADA_BANK = 6
        row_place = {1: (4, 0), 0: (5, 0), 2: (5, 1), 3: (5, 2), 4: (5, 3), 5: (3, 0)}
        raw = [mem["w_raw"][:, i, :] for i in range(2)] + [ada_more[:, i, :] for i in range(RING - 2)]

        small = [(io["ada_b"].rearrange("l (b p) -> (l b) p", p=P), PA["ada_b"], 48)]
        for n in ("norm_mix_w", "norm_ffn_w", "hy_conv_b", "hy_bias", "ml_conv_b", "ml_norm_w"):
            small.append((io[n].rearrange("l (b p) -> (l b) p", p=P), PA[n], io[n].shape[1] // P))
        small.append((io["final_norm_w"].rearrange("(b p) -> b p", p=P), PA["final_norm_w"], 8))
        conv = [(io["hy_conv_w"].rearrange("l j (b p) -> (l j b) p", p=P), 0, 36),
                (io["ml_conv_w"].rearrange("l j (b p) -> (l j b) p", p=P), 36, 24)]
        conv += [(io["c"][0].rearrange("(b p) -> b p", p=P), 60, 8), (io["c_ctx"].rearrange("(b p) -> b p", p=P), 68, 8)]
        ffn_taps = io["ffn_conv_w"].rearrange("l y x (b p) -> (l y x b) p", p=P)
        ffn_bias = io["ffn_conv_b"].rearrange("l (b p) -> (l b) p", p=P)
        filt = [(io[n], 76 + i) for i, n in enumerate(("hy_filt_b1", "hy_filt_b2", "hy_filt_b3", "hy_freq"))]
        n_rows = len(small) + 5

        sizes = [1, 2, 2] + [2] * (NT - 1) + [3]
        part_at = [range(sum(sizes[:i]), sum(sizes[:i + 1])) for i in range(len(sizes))]
        assert sum(sizes) == PARTS

        def split_ada_hi(act, p):
            act.wait_ge(ada_in[p % RING], 16 * (p // RING + 1))
            if p >= 2:
                act.wait_ge(part_done, p - 1)
            nc.scalar.activation(mem["w_hi"][:, p % 2, :], raw[p % RING], ACT.Copy).then_inc(ada_hi, 1)

        def split_ada_lo(eng, p, a, b, done):
            eng.wait_ge(ada_hi, p + 1)
            eng.tensor_tensor(mem["w_lo"][:, p % 2, a:b], raw[p % RING][:, a:b], mem["w_hi"][:, p % 2, a:b].bitcast(F32),
                              ALU.subtract).then_inc(done, 1)

        blk = ph.block()

        @blk.sync
        def _(sp):
            sp.dma_start(mem["ident"][:], io["k_ident"]).then_inc(ident_in, 16)
            for dst, src in ((z, io["k_z"]), (w1[:], io["hy_filt_w1"][0]), (w2[:], io["hy_filt_w2"][0]),
                             (w3[:], io["hy_filt_w3"][0]), (w4[:], io["hy_filt_w4"][0])):
                sp.dma_start(dst, src).then_inc(mlp_in, 16)
            sp.wait_ge(rows1_in, 16 * 8)
            loads = [(rows[r:r + n, 0, :], src) for src, r, n in small]
            for i in range(4):
                n = FROWS if i < 3 else 66
                loads.append((rows[0:n, 2 + i, :], ffn_taps[FROWS * i:FROWS * i + n, :]))
            loads.append((rows[66:110, 5, :], ffn_bias))
            for p in range(PARTS):
                if p >= RING:
                    sp.wait_ge(ada_lo, p - RING + 1)
                if p - RING >= SHARED:
                    sp.wait_ge(ada_lo_share, p - RING - SHARED + 1)
                r0, c0 = HK * P * (p % 2), AW * (p // 2)
                sp.dma_start(cols(raw[p % RING], AW), io["ada_w"][0, r0:r0 + HK * P, c0:c0 + AW]
                             .rearrange("(k p) c -> p k c", p=P)).then_inc(ada_in[p % RING], 16)
                if p == 0:
                    for dst, src in loads:
                        sp.dma_start(dst, src).then_inc(rows_in, 16)

        @blk.gpsimd
        def _(pool):
            nc.gpsimd.memset(rows[:], 0.0).then_inc(zeroed, 1)
            nc.gpsimd.memset(cond_wide[:], 0.0).then_inc(cond_zero, 1)
            pool.wait_ge(cond_zero, 1)
            nc.gpsimd.memset(absum[:], 0.0).then_inc(absum_zero, 1)
            pool.wait_ge(cond_hi_done, 1)
            nc.gpsimd.tensor_copy(cond_wide[:, :, 0:2], cond_hi[:].bitcast(F32)).then_inc(cond_placed, 1)
            nc.gpsimd.tensor_tensor(cond_wide[:, :, 2:4], cond_silu[:], cond_hi[:].bitcast(F32), ALU.subtract)\
              .then_inc(cond_placed, 1)
            for group, parts in enumerate(part_at):
                j = group - 3
                if j == 0:
                    pool.wait_ge(w4_split, 1)
                    nc.gpsimd.tensor_tensor(w4_lo, w4[:].rearrange("p (i c) -> p i c", i=2), w4_hi.bitcast(F32),
                                            ALU.subtract).then_inc(w4_split, 1)
                for p in parts:
                    split_ada_lo(nc.gpsimd, p, 0, UNIT if p < SHARED else SHARE, ada_lo)
                if j >= 0:
                    pool.wait_ge(k_hi_done, j + 1)
                    nc.gpsimd.tensor_tensor(k_lo[:, :, j, :], summed[:, j % 2, :, :], k_hi[:, :, j, :].bitcast(F32),
                                            ALU.subtract).then_inc(k_lo_done, 1)

        @blk.tensor
        def _(pe):
            def mlp_layer(layer):
                x = z if layer == 0 else h
                for i, (b0, b1) in enumerate(PIECES):
                    if layer:
                        pe.wait_ge(sin_done, 2 * layer - 1 + i)
                    for b in range(b0, b1):
                        last = nc.tensor.matmul(ps[0:64, b, 0:BW], (w1, w2, w3)[layer][:], x[:, b * BW:(b + 1) * BW],
                                                start=True, stop=True)
                    last.then_inc(mm, 1)

            def turn_rows(i):
                bank, at_ = row_place[i]
                nc.tensor.transpose(ps[:, bank, at_ * P:(at_ + 1) * P], rows[:, i, :], mem["ident"][:]).then_inc(par_t, 1)

            def ada_parts(group):
                for p in part_at[group]:
                    pe.wait_ge(ada_lo, p + 1)
                    if p >= SHARED:
                        pe.wait_ge(ada_lo_share, p - SHARED + 1)
                    q = p // 2
                    if p % 2 == 0 and q >= 2:
                        pe.wait_ge(part_copied, q - 1)
                    for k in range(HK * (p % 2), HK * (p % 2) + HK):
                        for n, w in enumerate((mem["w_hi"], mem["w_lo"])):
                            last = nc.tensor.matmul(ps[:, ADA_BANK + q % 2, :], cond[:, k, :], cols(w[:, p % 2, :], AW)[:, k % HK, :],
                                                    start=(k + n == 0), stop=(k + n == KD))
                    last.then_inc(part_done, 1)

            pe.wait_ge(ident_in, 16)
            pe.wait_ge(rows1_in, 16 * 8)
            turn_rows(1)
            pe.wait_ge(mlp_in, 80)
            mlp_layer(0)
            pe.wait_ge(cond_ready, 1)
            ada_parts(0)
            for layer in range(1, 3):
                mlp_layer(layer)
                if layer == 2:
                    pe.wait_ge(rows_in, 16 * n_rows)
                    for i in (0, 2, 3, 4, 5):
                        turn_rows(i)
                ada_parts(layer)
            pe.wait_ge(h_split, 2)
            pe.wait_ge(w4_split, 2)
            pe.wait_ge(par_c, 4)
            for j in range(NT):
                if j >= 2:
                    pe.wait_ge(tapped, 2 * (j - 1))
                s0 = (j // 4) + 256 * (j % 4) if j < 8 else LS
                at_ = slice(s0, s0 + 255, 2) if j < 8 else slice(LS, T)
                last = product(nc, [ps[:, 2 * (j % 2) + half, :] for half in range(2)], lambda k: h_hi[:, at_], lambda k: h_lo[:, at_],
                               lambda k, i: w4_hi[:, i, :], lambda k, i: w4_lo[:, i, :], range(1))
                last.then_inc(w4_done, 1)
                if j >= 1:
                    ada_parts(2 + j)
            ada_parts(2 + NT)
            pe.wait_ge(accumulated, NT)
            for j in range(2):
                for c in range(CH):
                    for half in range(2):
                        last = nc.tensor.matmul(ps[:, 4, CH * j + c:CH * j + c + 1], absum[:, j, half, c * P:(c + 1) * P],
                                                mem["ones"][:, 0:1], start=(half == 0), stop=(half == 1))
            last.then_inc(norm_mm, 1)
            for i in range(2):
                pe.wait_ge(part_moved[i], 16 * PARTS)
            for j in range(4):
                last = nc.tensor.transpose(ps[:, 5, BLOCKS * j:BLOCKS * (j + 1)], mod_rows[:, j, :],
                                           mem["ident"][0:BLOCKS, 0:BLOCKS])
            last.then_inc(mod_turned, 1)

        @blk.scalar
        def _(act):
            act.wait_ge(zeroed, 1)
            first = [(rows[r:r + n, 1, :], src) for src, r, n in conv]
            first += [(rows[r:r + 1, 1, 0:64], src) for src, r in filt]
            for dst, src in first:
                act.dma_start(dst, src).then_inc(rows1_in, 16)
            act.wait_ge(par_c, 1)
            c0 = PA["cond"]
            nc.scalar.activation(cond_silu[:], par[:, c0:c0 + 16].rearrange("p (j k) -> p k j", j=2), ACT.Silu)\
              .then_inc(silu_done, 1)
            act.wait_ge(silu_done, 1)
            nc.scalar.activation(cond_hi[:], cond_silu[:], ACT.Copy).then_inc(cond_hi_done, 1)
            split_ada_hi(act, 0)
            act.wait_ge(mlp_in, 80)
            nc.scalar.activation(w4_hi, w4[:].rearrange("p (i c) -> p i c", i=2), ACT.Copy).then_inc(w4_split, 1)
            act.wait_ge(cond_placed, 2)
            nc.scalar.activation(cond[:], cond_wide[:], ACT.Copy).then_inc(cond_ready, 1)
            split_ada_hi(act, 1)
            for j in range(2):
                act.dma_start(decay[:, j, :], io["k_decay"][j]).then_inc(decay_in[j], 16)

            def move_part(q):
                act.wait_ge(part_done, 2 * q + 2)
                if q >= 2:
                    act.wait_ge(part_moved[q % 2], 64 * (q // 2))
                nc.scalar.activation(part_rows[:, q % 2, :], ps[0:4, ADA_BANK + q % 2, :], ACT.Copy).then_inc(part_copied, 1)
                act.wait_ge(part_copied, q + 1)
                for b in range(4):
                    act.dma_start(mod_rows[4 * q + b:4 * q + b + 1, :, :], part_rows[:, q % 2, b * P:(b + 1) * P])\
                      .then_inc(part_moved[q % 2], 16)

            for layer in range(3):
                for p in part_at[layer]:
                    if p >= 2:
                        split_ada_hi(act, p)
                    if p >= 2 and p % 2:
                        move_part((p - 3) // 2)
                for i, (b0, b1) in enumerate(PIECES):
                    at_ = slice(b0 * BW, b1 * BW)
                    act.wait_ge(arg_done, 2 * layer + i + 1)
                    nc.scalar.activation(h[:, at_], arg[:, at_], ACT.Sin).then_inc(sin_done, 1)
            act.wait_ge(sin_done, 6)
            nc.scalar.activation(h_hi[:], h[:], ACT.Copy).then_inc(h_split, 1)
            for j in range(NT):
                for p in part_at[3 + j]:
                    split_ada_hi(act, p)
                    if p % 2:
                        move_part((p - 3) // 2)
                act.wait_ge(tapped, 2 * j + 2)
                act.wait_ge(edge, 1 + j // 8)
                if j >= 2:
                    act.wait_ge(accumulated, j - 1)
                nc.scalar.activation(size[:, j % 2], taps[:, j % 2], ACT.Abs).then_inc(sized, 1)
                act.wait_ge(sums, 2 * j + 2)
                nc.scalar.activation(k_hi[:, :, j, :], summed[:, j % 2, :, :], ACT.Copy).then_inc(k_hi_done, 1)
                if j + 2 < NT:
                    act.dma_start(decay[:, j % 2, :], io["k_decay"][j + 2]).then_inc(decay_in[j % 2], 16)
            move_part(PARTS // 2 - 1)

        def mlp_argument(dve, step, layer):
            for i, (b0, b1) in enumerate(PIECES):
                a, n = arg[:, b0 * BW:b1 * BW], turns[:, b0 * BW:b1 * BW]
                dve.wait_ge(mm, 2 * layer + i + 1)
                step.do(nc.vector.tensor_scalar(a.rearrange("p (b c) -> p b c", c=BW), ps[0:64, b0:b1, 0:BW],
                                                vec[:, layer:layer + 1], vec[:, 3:4], ALU.add, ALU.mult))
                step.do(nc.vector.tensor_scalar(n, a, 1.0 / (2 * math.pi), ROUND, ALU.mult, ALU.add))
                step.do(nc.vector.tensor_scalar_add(n, n, -ROUND))
                for part in TWO_PI_PARTS:
                    step.do(nc.vector.scalar_tensor_tensor(out=a, in0=n, scalar=-part, in1=a, op0=ALU.mult, op1=ALU.add))
                nc.vector.tensor_scalar(a, a, 3.1415925, -3.1415925, ALU.min, ALU.max).then_inc(arg_done, 1)

        @blk.vector
        def _(dve):
            step = Chain(dve, step_sem)
            dve.wait_ge(par_t, 1)
            nc.vector.tensor_copy(par[:, 128:256], ps[:, 4, 0:P]).then_inc(par_c, 1)
            dve.wait_ge(par_c, 1)
            mlp_argument(dve, step, 0)
            for layer in range(1, 3):
                mlp_argument(dve, step, layer)
            dve.wait_ge(par_t, 6)
            nc.vector.tensor_copy(par[:, 0:P], ps[:, 5, 0:P]).then_inc(par_c, 1)
            fp = par[:, 256:256 + 4 * FROWS].rearrange("p (i r) -> p i r", r=FROWS)
            nc.vector.tensor_copy(fp[:, 0:3], ps[:, 5, P:4 * P].rearrange("p (i r) -> p i r", r=P)[:, :, 0:FROWS])\
              .then_inc(par_c, 1)
            nc.vector.tensor_copy(fp[:, 3], ps[:, 3, 0:FROWS]).then_inc(par_c, 1)
            dve.wait_ge(par_c, 4)
            dve.wait_ge(h_split, 1)
            nc.vector.tensor_tensor(h_lo[:], h[:], h_hi[:].bitcast(F32), ALU.subtract).then_inc(h_split, 1)

            def accumulate(j):
                dve.wait_ge(sized, j + 1)
                if j:
                    dve.wait_ge(accumulated, j)
                else:
                    dve.wait_ge(absum_zero, 1)
                nc.vector.tensor_tensor(absum[:, j // 8], absum[:, j // 8], size[:, j % 2], ALU.add).then_inc(accumulated, 1)

            for j in range(NT):
                i, bank = j % 2, 2 * (j % 2)
                dve.wait_ge(w4_done, j + 1)
                dve.wait_ge(decay_in[i], 16 * (j // 2 + 1))
                if j >= 2:
                    dve.wait_ge(sized, j - 1)
                for half in range(2):
                    nc.vector.tensor_tensor(taps[:, i, half], ps[:, bank + half, :], decay[:, i, :], ALU.mult)\
                      .then_inc(tapped, 1)
                dve.wait_ge(tapped, 2 * j + 2)
                if j in (0, 8):
                    nc.vector.memset(taps[0:1, i, 1, :], 0.0).then_inc(edge, 1)
                    dve.wait_ge(edge, 1 + j // 8)
                if j >= 2:
                    dve.wait_ge(k_lo_done, j - 1)
                nc.vector.tensor_tensor(summed[:, i, 0, :], taps[:, i, 0], taps[:, i, 1], ALU.add).then_inc(sums, 1)
                nc.vector.tensor_tensor(summed[:, i, 1, :], taps[:, i, 0], taps[:, i, 1], ALU.subtract).then_inc(sums, 1)
                if j >= 1:
                    accumulate(j - 1)
                for p in part_at[3 + j]:
                    if p >= SHARED:
                        split_ada_lo(nc.vector, p, SHARE, UNIT, ada_lo_share)
            accumulate(NT - 1)
            dve.wait_ge(norm_mm, 1)
            step.do(nc.vector.tensor_copy(norm[:], ps[:, 4, 0:2 * CH]))
            step.do(nc.vector.reciprocal(mem["filter_gain"][:], norm[:]))
            dve.wait_ge(mod_turned, 1)
            mod = mem["mod"]
            W = BLOCKS
            for j in range(2):
                step.do(nc.vector.tensor_copy(mod[:, :, j], ps[:, 5, (2 + j) * W:(3 + j) * W]))
                step.do(nc.vector.tensor_tensor(mod[:, :, j], ps[:, 5, j * W:(j + 1) * W], mod[:, :, j], ALU.add))
                step.do(nc.vector.tensor_tensor(mod[:, :, j], mod[:, :, j], par[:, PA["ada_b"]:PA["ada_b"] + W], ALU.add))
            for dst, w, blk_at in (("gain_mix", "norm_mix_w", 8), ("gain_ffn", "norm_ffn_w", 32)):
                for j in range(2):
                    step.do(nc.vector.scalar_tensor_tensor(
                        out=mem[dst][:, :, j], in0=mod[:, blk_at:blk_at + 8, j], scalar=1.0,
                        in1=par[:, PA[w]:PA[w] + 8], op0=ALU.add, op1=ALU.mult))


def transform_products(nc, pe, mem, ring, x_hi, x_lo, two, full, prompt_read, row_done, banks_read):
    ps = mem["psum"]

    def sums(bank, w, blocks, i, tokens):
        pairs = list(zip(blocks, tokens))
        return product(nc, [ps[:, bank, :]], lambda a: w[0][:, a[0], :], lambda a: w[1][:, a[0], :],
                       lambda a, _: x_hi[:, i, a[1], :], lambda a, _: x_lo[:, i, a[1], :], pairs)

    for u in range(5):
        ring.ready(pe, u)
        w = [half.rearrange("p (b k) -> p b k", k=P) for half in (ring.hi(u), ring.lo(u))]
        if u == 0:
            sums(4, w, [0], 0, [NT - 1])
            last = sums(5, w, [1], 1 if two else 0, [NT - 1])
            if two:
                last = sums(6, w, [1], 0, [NT - 1])
            last.then_inc(full, 1)
            continue
        kt = u - 1
        if kt == 1:
            pe.wait_ge(prompt_read, 1)
            if two:
                pe.wait_ge(row_done, 2)
        if kt >= 2:
            pe.wait_ge(banks_read, 4 * (kt - 1))
        for t in range(4):
            last = sums(4 * (kt % 2) + t, w, range(4 * t, 4 * t + 4), t // 2 if two else 0, range(4 * (t % 2), 4 * (t % 2) + 4))
        if two and kt == 0:
            last = sums(7, w, range(8, 12), 0, range(4))
        last.then_inc(full, 1)


def filter_spectra(nc, io, mem, dram, x_hi, x_lo, norm):
    with Phase(nc, "kt") as ph:
        full = ph.sem("sums_done")
        odd = ph.sem("odd_copied")
        spec_done = ph.sem("spectrum_done")
        row_done = ph.sem("row_done")
        spec_out = [ph.sem(f"spectrum_out{i}") for i in range(2)]
        prompt_copied = ph.sem("prompt_copied")
        prompt_read = ph.sem("prompt_read")
        prompt_out = ph.sem("prompt_out")
        norm.semaphores(ph)
        ring = WeightRing(nc, ph, mem, lambda u: (full, u + 1))
        spec = ph.sb("spec", [P, 2, 4, DH])
        prompt = ph.sb("prompt", [P, 2, DH])
        ps = mem["psum"]
        blk = ph.block()

        @blk.sync
        def _(sp):
            for u in range(5):
                load_forward(sp, ring, io, u)
                if u >= 2:
                    norm.load(sp, u - 2)
            sp.wait_ge(prompt_read, 1)
            sp.dma_start(dram["kt_prompt"], prompt[:]).then_inc(prompt_out, 16)
            for kt in range(4):
                sp.wait_ge(spec_done, 4 * (kt + 1))
                if kt == 0:
                    sp.wait_ge(row_done, 2)
                sp.dma_start(dram["kt"][kt], spec[:, kt % 2]).then_inc(spec_out[kt % 2], 16)
            sp.wait_ge(prompt_out, 16)
            sp.wait_ge(spec_out[0], 32)
            sp.wait_ge(spec_out[1], 32)

        @blk.gpsimd
        def _(pool):
            for u in range(5):
                ring.split_lo(pool, u, forward_width(u))

        @blk.tensor
        def _(pe):
            transform_products(nc, pe, mem, ring, x_hi, x_lo, True, full, prompt_read, row_done, spec_done)

        @blk.scalar
        def _(act):
            ring.split_hi(act, 0, forward_width(0))
            ring.split_hi(act, 1, forward_width(1))
            for kt in range(4):
                if kt < 3:
                    ring.split_hi(act, kt + 2)
                act.wait_ge(full, kt + 2)
                b = 4 * (kt % 2)
                if kt >= 2:
                    act.wait_ge(spec_out[kt % 2], 16)
                nc.scalar.activation(spec[:, kt % 2, 1:4:2, :], ps[:, b + 1:b + 4:2, :], ACT.Copy).then_inc(odd, 1)
                if kt >= 2:
                    norm.take_root(act, kt - 2)
                if kt >= 1:
                    norm.squares(act, kt - 1)
            norm.take_root(act, 2)

        @blk.vector
        def _(dve):
            dve.wait_ge(full, 1)
            nc.vector.tensor_copy(prompt[:], ps[:, 4:6, :]).then_inc(prompt_copied, 1)
            dve.wait_ge(prompt_copied, 1)
            nc.vector.tensor_copy(prompt[0:1, 1, :], ps[0:1, 6, :]).then_inc(prompt_read, 1)
            for kt in range(4):
                dve.wait_ge(odd, kt + 1)
                combine(nc, ps, 4 * (kt % 2), spec[:, kt % 2], spec_done)
                if kt == 0:
                    dve.wait_ge(spec_done, 4)
                    for i, bank in ((2, 7), (3, 3)):
                        nc.vector.tensor_copy(spec[0:1, 0, i, :], ps[0:1, bank, :]).then_inc(row_done, 1)
                if kt >= 2:
                    norm.scale(dve, kt - 2)
                if kt >= 1:
                    norm.mean(dve, kt - 1)
            norm.scale(dve, 2)


def combine(nc, ps, b, spec, done):
    tt = nc.vector.tensor_tensor
    tt(spec[:, 0, :], ps[:, b, :], spec[:, 1, :], ALU.add).then_inc(done, 1)
    tt(spec[:, 1, :], ps[:, b, :], spec[:, 1, :], ALU.subtract).then_inc(done, 1)
    tt(spec[:, 2, :], ps[:, b + 2, :], spec[:, 3, :], ALU.add).then_inc(done, 1)
    nc.vector.scalar_tensor_tensor(out=spec[:, 3, :], in0=ps[:, b + 2, :], scalar=-1.0, in1=spec[:, 3, :],
                                   op0=ALU.mult, op1=ALU.add).then_inc(done, 1)


def phase_hyena(nc, io, mem, dram):
    with Phase(nc, "conv") as outer:
        y_hi = outer.sb("y_hi", [P, 4, 4, DH], F32R)
        y_lo = outer.sb("y_lo", [P, 4, 4, DH], F32R)
        yp_hi = outer.sb("yp_hi", [P, 2, DH], F32R)
        yp_lo = outer.sb("yp_lo", [P, 2, DH], F32R)
        spectra(nc, io, mem, dram, y_hi, y_lo, yp_hi, yp_lo)
        inverse_transform(nc, io, mem, dram, y_hi, y_lo, yp_hi, yp_lo)


def spectra(nc, io, mem, dram, y_hi, y_lo, yp_hi, yp_lo):
    ps = mem["psum"]
    with Phase(nc, "vspec") as outer:
        v_hi = outer.sb("v_hi", [P, 1, NT, DH], F32R)
        v_lo = outer.sb("v_lo", [P, 1, NT, DH], F32R)
        with Phase(nc, "vtok") as ph:
            v = ph.sb("v", [P, CH, T])
            v_in = [ph.sem(f"v_in{c}") for c in range(CH)]
            tr = ph.sem("transposed")
            hi = ph.sem("hi")
            lo = ph.sem("lo")
            unit_hi = ph.sem("unit_hi")
            unit = WeightRing(nc, ph, mem, None, first=1)
            blk = ph.block()

            @blk.gpsimd
            def _(pool):
                pool.wait_ge(unit_hi, 1)
                nc.gpsimd.tensor_tensor(unit.lo(0), unit.raw(0), unit.hi(0).bitcast(F32), ALU.subtract)

            @blk.sync
            def _(sp):
                for c in range(CH):
                    sp.dma_start(v[:, c, :], dram["hv"][c]).then_inc(v_in[c], 16)

            @blk.tensor
            def _(pe):
                for j in range(NT):
                    if j >= 4:
                        pe.wait_ge(lo, j - 3)
                    for c in range(CH):
                        if j == 0:
                            pe.wait_ge(v_in[c], 16)
                        s0 = (j // 4) + 256 * (j % 4)
                        src = v[:, c, s0:s0 + 255:2] if j < 8 else v[:, c, LS:T]
                        last = nc.tensor.transpose(ps[:, j % 4, c * P:(c + 1) * P], src, mem["ident"][:])
                    last.then_inc(tr, 1)

            @blk.scalar
            def _(act):
                nc.scalar.activation(unit.hi(0), unit.raw(0), ACT.Copy).then_inc(unit_hi, 1)
                for j in range(NT):
                    act.wait_ge(tr, j + 1)
                    nc.scalar.activation(v_hi[:, 0, j, :], ps[:, j % 4, :], ACT.Copy).then_inc(hi, 1)

            @blk.vector
            def _(dve):
                for j in range(NT):
                    dve.wait_ge(hi, j + 1)
                    nc.vector.tensor_tensor(v_lo[:, 0, j, :], ps[:, j % 4, :], v_hi[:, 0, j, :].bitcast(F32),
                                            ALU.subtract).then_inc(lo, 1)
        transform_and_multiply(nc, io, mem, dram, v_hi, v_lo, y_hi, y_lo, yp_hi, yp_lo)


def transform_and_multiply(nc, io, mem, dram, v_hi, v_lo, y_hi, y_lo, yp_hi, yp_lo):
    ps = mem["psum"]
    with Phase(nc, "vt") as ph:
        ks = ph.sb("k_spectrum", [P, 2, 4, DH])
        vs = ph.sb("v_spectrum", [P, 4, DH])
        t = ph.sb("cross", [P, 2, 2, DH])
        out = ph.sb("folded", [P, 4, DH])
        k_in = [ph.sem(f"k_in{i}") for i in range(2)]
        full = ph.sem("sums_done")
        prompt_read = ph.sem("prompt_read")
        row_read = ph.sem("row_read")
        odd = ph.sem("odd_copied")
        read = ph.sem("sums_read")
        used = ph.sem("spectra_used")
        folded_done = ph.sem("folded")
        hi = ph.sem("hi")
        lo = ph.sem("lo")
        step_sem = ph.sem("dve_step")
        ring = WeightRing(nc, ph, mem, lambda u: (full, u + 1), ahead=2)
        blk = ph.block()

        @blk.sync
        def _(sp):
            sp.dma_start(ks[:, 1, 0:2], dram["kt_prompt"]).then_inc(k_in[1], 16)
            load_forward(sp, ring, io, 2)
            sp.dma_start(ks[:, 0], dram["kt"][0]).then_inc(k_in[0], 16)
            load_forward(sp, ring, io, 3)
            for kt in range(1, 4):
                sp.wait_ge(used, kt)
                sp.dma_start(ks[:, kt % 2], dram["kt"][kt]).then_inc(k_in[kt % 2], 16)
                if kt == 1:
                    load_forward(sp, ring, io, 4)
                else:
                    ring.load(sp, kt + 3, io["k_inv"][kt - 2])

        @blk.tensor
        def _(pe):
            transform_products(nc, pe, mem, ring, v_hi, v_lo, False, full, prompt_read, None, read)

        def coefficients(n):
            return (y_hi[:, :, n - 1, :], y_lo[:, :, n - 1, :], out[:]) if n else (yp_hi[:], yp_lo[:], out[:, 0:2])

        @blk.scalar
        def _(act):
            def to_hi(n):
                act.wait_ge(folded_done, n + 1)
                nc.scalar.activation(coefficients(n)[0], coefficients(n)[2], ACT.Copy).then_inc(hi, 1)

            for kt in range(4):
                if kt < 3:
                    ring.split_hi(act, kt + 2)
                act.wait_ge(full, kt + 2)
                if kt == 0:
                    act.wait_ge(row_read, 1)
                else:
                    act.wait_ge(used, kt + 1)
                b = 4 * (kt % 2)
                nc.scalar.activation(vs[:, 1:4:2, :], ps[:, b + 1:b + 4:2, :], ACT.Copy).then_inc(odd, 1)
                to_hi(kt)
            for u in range(5, 7):
                ring.split_hi(act, u)
            to_hi(4)

        @blk.gpsimd
        def _(pool):
            def to_lo(n):
                pool.wait_ge(hi, n + 1)
                h, l, src = coefficients(n)
                nc.gpsimd.tensor_tensor(l, src, h.bitcast(F32), ALU.subtract).then_inc(lo, 1)

            for kt in range(4):
                if kt < 3:
                    ring.split_lo(pool, kt + 2)
                to_lo(kt)
            for u in range(5, 7):
                ring.split_lo(pool, u)
            to_lo(4)

        @blk.vector
        def _(dve):
            step = Chain(dve, step_sem)
            tt = nc.vector.tensor_tensor
            dve.wait_ge(full, 1)
            dve.wait_ge(k_in[1], 16)
            ka, kb = ks[:, 1, 0], ks[:, 1, 1]
            step.do(tt(t[:, 0, 0], ps[:, 4, :], ka, ALU.mult))
            step.do(tt(t[:, 0, 1], ps[:, 5, :], kb, ALU.mult))
            step.do(tt(t[:, 1, 0], ps[:, 4, :], kb, ALU.mult))
            step.do(tt(t[:, 1, 1], ps[:, 5, :], ka, ALU.mult))
            dve.sem_inc(prompt_read, 1)
            dve.sem_inc(used, 1)
            step.do(tt(out[:, 0, :], t[:, 0, 0], t[:, 0, 1], ALU.subtract))
            step.do(tt(out[:, 1, :], t[:, 1, 0], t[:, 1, 1], ALU.add))
            step.do(nc.vector.tensor_copy(out[0:1, 0:2, :], t[0:1, 0, :, :]))
            dve.sem_inc(folded_done, 1)
            dve.wait_ge(full, 2)
            dve.wait_ge(k_in[0], 16)
            row = ks[0:1, 0, 2:4]
            r = t[0:1].rearrange("p a b c -> p (a b) c")
            step.do(tt(r[:, 0, :], ps[0:1, 2, :], row[:, 0], ALU.mult))
            step.do(tt(r[:, 1, :], ps[0:1, 3, :], row[:, 1], ALU.mult))
            step.do(tt(r[:, 2, :], ps[0:1, 2, :], row[:, 1], ALU.mult))
            step.do(tt(r[:, 3, :], ps[0:1, 3, :], row[:, 0], ALU.mult))
            dve.sem_inc(row_read, 1)
            step.do(tt(row[:, 0], r[:, 0], r[:, 1], ALU.subtract))
            step.do(tt(row[:, 1], r[:, 2], r[:, 3], ALU.add))
            for kt in range(4):
                dve.wait_ge(odd, kt + 1)
                combine(nc, ps, 4 * (kt % 2), vs, read)
                dve.wait_ge(read, 4 * (kt + 1))
                dve.wait_ge(k_in[kt % 2], 16 * (kt // 2 + 1 + kt % 2))
                ka, kb = ks[:, kt % 2, 0:2], ks[:, kt % 2, 2:4]
                va, vb = vs[:, 0:2], vs[:, 2:4]
                step.do(tt(t[:, 0], vb, kb, ALU.mult))
                step.do(tt(t[:, 1], va, kb, ALU.mult))
                step.do(tt(va, va, ka, ALU.mult))
                step.do(tt(vb, vb, ka, ALU.mult))
                if kt == 0:
                    step.do(nc.vector.memset(t[0:1, 0], 0.0))
                step.do(tt(t[:, 0], va, t[:, 0], ALU.subtract))
                step.do(tt(t[:, 1], vb, t[:, 1], ALU.add))
                if kt >= 1:
                    dve.sem_inc(used, 1)
                dve.wait_ge(lo, kt + 1)
                step.do(tt(out[:, 0, :], t[:, 0, 0], t[:, 0, 1], ALU.add))
                step.do(tt(out[:, 2, :], t[:, 0, 0], t[:, 0, 1], ALU.subtract))
                step.do(tt(out[:, 1, :], t[:, 1, 0], t[:, 1, 1], ALU.subtract))
                step.do(tt(out[:, 3, :], t[:, 1, 0], t[:, 1, 1], ALU.add))
                if kt == 0:
                    step.do(nc.vector.tensor_copy(out[0:1, 1:4:2, :], row))
                    dve.sem_inc(used, 1)
                dve.sem_inc(folded_done, 1)


def inverse_transform(nc, io, mem, dram, y_hi, y_lo, yp_hi, yp_lo):
    ps = mem["psum"]
    with Phase(nc, "inv") as ph:
        full = ph.sem("product_done")
        unit_used = ph.sem("unit_used")
        ring = WeightRing(nc, ph, mem, lambda u: (unit_used, u + 1), ahead=2, first=1)
        v = ph.sb("v", [P, CH, T])
        x0 = ph.sb("x0", [P, CH, T])
        v_in = [ph.sem(f"v_in{c}") for c in range(CH)]
        bias_done = ph.sem("bias_done")
        summed = ph.sem("summed")
        gated = ph.sem("gated")
        y_out = ph.sem("y_out")
        blk = ph.block()

        @blk.sync
        def _(sp):
            ring.load(sp, 2, io["k_inv"][2])
            ring.load(sp, 3, io["k_inv"][3])
            for c in range(CH):
                sp.dma_start(v[:, c, :], dram["hv"][c]).then_inc(v_in[c], 16)
                sp.dma_start(x0[:, c, :], dram["x0"][c]).then_inc(v_in[c], 16)
            load_forward(sp, ring, io, 0, 4)
            for u in range(2):
                load_w_out(sp, ring, io, u, 5)
            for c in range(CH):
                sp.wait_ge(gated, CH + c + 1)
                sp.dma_start(dram["y"][c][:, 0:LS], x0[:, c, 0:LS]).then_inc(y_out, 16)
            sp.wait_ge(gated, 3 * CH)
            sp.dma_start(dram["y"].rearrange("k p t -> p k t")[:, 0:CH, LS:T], x0[:, :, LS:T]).then_inc(y_out, 16)
            sp.wait_ge(y_out, 16 * (CH + 1))

        @blk.gpsimd
        def _(pool):
            for u in range(2, 7):
                ring.split_lo(pool, u, 4 * P if u == 4 else UNIT)

        @blk.tensor
        def _(pe):
            for u in range(4):
                ring.ready(pe, u)
                xh, xl = cols(ring.hi(u), 512), cols(ring.lo(u), 512)
                for c in range(CH):
                    last = product(nc, [ps[:, 4 * (u // 2) + c, :]], lambda k: y_hi[:, u, k, c * P:(c + 1) * P],
                                   lambda k: y_lo[:, u, k, c * P:(c + 1) * P],
                                   lambda k, _: xh[:, k, :], lambda k, _: xl[:, k, :], range(4),
                                   first=u % 2 == 0, last=u % 2 == 1)
                    if u % 2:
                        last.then_inc(full, 1)
                    if c == CH - 1 and u % 2 == 0:
                        last.then_inc(unit_used, 1)
                if u % 2:
                    pe.wait_ge(full, 4 * (u // 2 + 1))
                    pe.sem_inc(unit_used, 1)
            ring.ready(pe, 4)
            pe.wait_ge(summed, 1)
            xh = ring.hi(4)[:, 0:4 * P].rearrange("p (t k) -> p t k", t=4)
            xl = ring.lo(4)[:, 0:4 * P].rearrange("p (t k) -> p t k", t=4)
            for c in range(CH):
                last = product(nc, [ps[:, 0, c * P:(c + 1) * P]], lambda t: yp_hi[:, t, c * P:(c + 1) * P],
                               lambda t: yp_lo[:, t, c * P:(c + 1) * P], lambda t, _: xh[:, 2 + t, :],
                               lambda t, _: xl[:, 2 + t, :], range(2))
            last.then_inc(full, 1)
            pe.wait_ge(full, 9)
            pe.sem_inc(unit_used, 1)

        @blk.scalar
        def _(act):
            for u in range(2, 7):
                ring.split_hi(act, u, 4 * P if u == 4 else UNIT)

        @blk.vector
        def _(dve):
            par = mem["par"]
            for c in range(CH):
                dve.wait_ge(v_in[c], 32)
                nc.vector.tensor_scalar_mul(v[:, c, :], v[:, c, :], par[:, PA["hy_bias"] + c:PA["hy_bias"] + c + 1])\
                  .then_inc(bias_done, 1)
            dve.wait_ge(bias_done, CH)
            for n in range(12):
                c = n % 4
                dve.wait_ge(full, n + 1 if n < 8 else 9)
                if n < 8:
                    seg = slice(n // 4, LS, 2)
                    src, gain = ps[:, n, :], mem["filter_gain"][:, c:c + 1]
                else:
                    seg = slice(LS, T)
                    src, gain = ps[:, 0, c * P:(c + 1) * P], mem["filter_gain"][:, CH + c:CH + c + 1]
                nc.vector.scalar_tensor_tensor(out=v[:, c, seg], in0=src, scalar=gain, in1=v[:, c, seg],
                                               op0=ALU.mult, op1=ALU.add).then_inc(summed, 1)
                dve.wait_ge(summed, n + 1)
                nc.vector.tensor_tensor(x0[:, c, seg], v[:, c, seg], x0[:, c, seg], ALU.mult).then_inc(gated, 1)


G_SRC, G_INTER, G_FLOOR, G_STATE = range(4)


def gate_rows(nc, io, mem, dram, col, wcb, mrow, q, k, kn, v, work, C):
    ps = mem["psum"]
    gates = mem["gates"]
    with Phase(nc, "rows") as ph:
        f, e, u, lnu = (work[0:ROWS].rearrange("p a b c -> p (a b c)")[:, i * T:(i + 1) * T] for i in range(4))
        reset = ph.sb("reset", [ROWS, T])
        sel = ph.sb("sel", [ROWS, 8, P])
        b = ph.sb("b", [ROWS, T])
        jump = ph.sb("jump", [ROWS, T])
        r1 = ph.sb("r1", [P, T])
        r2 = ph.sb("r2", [P, T])
        m0 = ph.sb("m0", [ROWS, 1])
        m_in = ph.sb("m_in", [ROWS, NT])
        m_end = ph.sb("m_end", [ROWS, NT])
        wc = ph.sb("wc", [ROWS, NT])
        m_new = ph.sb("m_new", [ROWS, 1])
        ins_in = ph.sem("inputs_in")
        zeroed = ph.sem("zeroed")
        act_step = ph.sem("act_step")
        dve_sem = ph.sem("dve_step")
        lin = ph.sem("log_parts")
        ready = ph.sem("exponents_ready")
        tr = ph.sem("transposed")
        stored = ph.sem("stored")
        c_rows = ph.sb("c_rows", [P, 8, HD])
        n_rows = ph.sb("n_rows", [8, HD])
        q_in = ph.sem("q_in")
        v_in = ph.sem("v_in")
        k_in = ph.sem("k_in")
        c_in = ph.sem("c_in")
        turned = ph.sem("keys_transposed")
        copied = ph.sem("keys_copied")
        g, M = r1[0:ROWS, :], mrow
        blk = ph.block()

        @blk.gpsimd
        def _(pool):
            nc.gpsimd.memset(m0[:], 0.0).then_inc(zeroed, 1)
            nc.gpsimd.memset(C[:, 0], 0.0)
            nc.gpsimd.memset(v[:, :, :, HD:HD + 1], 1.0)

        @blk.sync
        def _(sp):
            sp.wait_ge(zeroed, 1)
            for dst, src in ((reset, "k_reset"), (sel, "k_sel"), (mem["mask"], "k_mask")):
                sp.dma_start(dst[:], io[src]).then_inc(ins_in, 16)
            for d in range(2):
                sp.dma_start(m0[32 * d:32 * d + HEADS, :], io["state_mlstm_m"][0, 0, d].rearrange("(h o) -> h o", o=1))\
                  .then_inc(ins_in, 16)
            sp.dma_start(k[:], dram["k"].rearrange("h p t -> p h t")).then_inc(k_in, 16)
            sp.dma_start(c_rows[:], io["state_mlstm_C"][0, 0].rearrange("d h e k -> e (d h) k")).then_inc(c_in, 16)
            sp.dma_start(n_rows[:], io["state_mlstm_n"][0, 0].rearrange("d h k -> (d h) k")).then_inc(c_in, 16)
            sp.dma_start(q[:], dram["q"].rearrange("h p t -> p h t")).then_inc(q_in, 16)
            for t in range(NT):
                sp.dma_start(v[:, t, :, 0:HD], dram["v"][t].rearrange("p (h d) -> p h d", h=HEADS)).then_inc(v_in, 16)
            sp.wait_ge(act_step, 6)
            for d in range(2):
                for i, rows in enumerate((mrow, r1)):
                    p0 = 32 * d + ROWS * i
                    sp.dma_start(dram["scan_rows"][i, HEADS * d:HEADS * d + HEADS, :], rows[p0:p0 + HEADS, :]).then_inc(stored, 16)
            sp.wait_ge(ready, 5)
            for d in range(2):
                sp.dma_start(io["new_m"][0, 0, d].rearrange("(h o) -> h o", o=1), m_new[32 * d:32 * d + HEADS, :])\
                  .then_inc(stored, 16)
            sp.wait_ge(q_in, 16)
            sp.wait_ge(v_in, 16 * NT)
            sp.wait_ge(stored, 96)

        @blk.scalar
        def _(act):
            step = Chain(act, act_step)
            step.do(nc.scalar.activation(f, gates[ROWS:P, :], ACT.Copy))
            step.do(nc.scalar.activation(e, gates[ROWS:P, :], ACT.Abs))
            step.do(nc.scalar.activation(e, e, ACT.Exp, scale=-1.0))
            act.wait_ge(lin, 1)
            step.do(nc.scalar.activation(lnu, u, ACT.Ln))
            step.do(nc.scalar.activation(b[:], lnu, ACT.Exp, scale=-1.0))
            for c in range(NT + 3):
                act.wait_ge(turned, c + 1)
                src = ps[:, 6 + c % 2, :].rearrange("p (h d) -> p h d", h=HEADS)
                if c < NT:
                    dst = kn[:, c]
                elif c < NT + 2:
                    dst = C[:, 1, 4 * (c - NT):4 * (c - NT) + 4, 0:HD]
                else:
                    dst, src = C[:, 1, :, HD], ps[:, 6 + c % 2, 0:8]
                nc.scalar.activation(dst, src, ACT.Copy).then_inc(copied, 1)
            act.wait_ge(ready, 1)
            step.do(nc.scalar.activation(r1[ROWS:P, :], r1[ROWS:P, :], ACT.Exp))
            act.wait_ge(ready, 2)
            step.do(nc.scalar.activation(r2[0:ROWS, :], r2[0:ROWS, :], ACT.Exp, scale=-1.0))
            act.wait_ge(ready, 3)
            step.do(nc.scalar.activation(r2[ROWS:P, :], r2[ROWS:P, :], ACT.Exp))
            act.wait_ge(ready, 4)
            step.do(nc.scalar.activation(wc[:], wc[:], ACT.Exp))

        @blk.vector
        def _(dve):
            step = Chain(dve, dve_sem)
            tt, scan = nc.vector.tensor_tensor, nc.vector.tensor_tensor_scan
            step.do(nc.vector.memset(jump[:], 0.0))
            dve.wait_ge(act_step, 3)
            nc.vector.tensor_scalar_add(u, e, 1.0).then_inc(lin, 1)
            dve.wait_ge(lin, 1)
            step.do(nc.vector.scalar_tensor_tensor(out=e, in0=u, scalar=1.0, in1=e, op0=ALU.subtract, op1=ALU.subtract))
            dve.wait_ge(act_step, 5)
            step.do(tt(e, e, b[:], ALU.mult))
            step.do(tt(lnu, lnu, e, ALU.subtract))
            step.do(nc.vector.scalar_tensor_tensor(out=f, in0=f, scalar=0.0, in1=lnu, op0=ALU.min, op1=ALU.subtract))
            dve.wait_ge(ins_in, 80)
            F_, B_ = slice(0, 32), slice(32, 64)
            step.do(scan(out=b[F_, :], data0=reset[F_, :], data1=f[F_, :], initial=0.0, op0=ALU.mult, op1=ALU.add))
            step.do(scan(out=b[B_, ::-1], data0=reset[B_, ::-1], data1=f[B_, ::-1], initial=0.0, op0=ALU.mult, op1=ALU.add))
            step.do(tt(g, gates[0:ROWS, :], b[:], ALU.subtract))
            step.do(nc.vector.tensor_copy(jump[F_, P:LS:P], b[F_, P - 1:LS - 1:P]))
            step.do(nc.vector.tensor_copy(jump[B_, P - 1:LS - 1:P], b[B_, P:LS:P]))
            for rows, init in ((slice(0, LS), True), (slice(LS, T), False)):
                a, z = rows.start, rows.stop
                step.do(scan(out=M[F_, a:z], data0=jump[F_, a:z], data1=g[F_, a:z],
                             initial=m0[F_, :] if init else 0.0, op0=ALU.add, op1=ALU.max))
                step.do(scan(out=M[B_, a:z][:, ::-1], data0=jump[B_, a:z][:, ::-1], data1=g[B_, a:z][:, ::-1],
                             initial=m0[B_, :] if init else 0.0, op0=ALU.add, op1=ALU.max))
            step.do(nc.vector.memset(m_in[:], 0.0))
            step.do(nc.vector.tensor_copy(m_in[F_, 0:1], m0[F_, :]))
            step.do(nc.vector.tensor_copy(m_in[B_, 7:8], m0[B_, :]))
            step.do(tt(m_in[F_, 1:8], M[F_, P - 1:LS - 1:P], b[F_, P - 1:LS - 1:P], ALU.add))
            step.do(tt(m_in[B_, 0:7], M[B_, P:LS:P], b[B_, P:LS:P], ALU.add))
            step.do(nc.vector.tensor_copy(m_end[F_, :], M[F_, P - 1:T:P]))
            step.do(nc.vector.tensor_copy(m_end[B_, :], M[B_, 0:T:P]))

            def chunked(a):
                return a.rearrange("p (c t) -> p c t", t=P)

            def spread(a):
                return a.unsqueeze(2).broadcast_to([ROWS, NT, P])

            nc.vector.tensor_tensor(chunked(r1[ROWS:P, :]), spread(m_in[:]), chunked(M[:]), ALU.subtract).then_inc(ready, 1)
            tt(r2[0:ROWS, :], b[:], M[:], ALU.add).then_inc(ready, 1)
            tt(chunked(r2[ROWS:P, :]), chunked(g), spread(m_end[:]), ALU.subtract).then_inc(ready, 1)
            tt(wc[:], m_in[:], m_end[:], ALU.subtract).then_inc(ready, 1)
            step.do(tt(m_new[F_, :], m_end[F_, 8:9], b[F_, T - 1:T], ALU.add))
            step.do(tt(m_new[B_, :], m_end[B_, 8:9], b[B_, LS:LS + 1], ALU.add))
            dve.sem_inc(ready, 1)
            for i in range(5):
                dve.wait_ge(tr, i + 1)
                c0, n = 2 * i, min(4, 18 - 4 * i)
                step.do(nc.vector.tensor_copy(col[:, c0:c0 + n // 2, :, :].rearrange("p c g r -> p (c g r)"), ps[:, i, 0:n * P]))
            dve.wait_ge(tr, 6)
            step.do(nc.vector.tensor_copy(wcb[:].rearrange("p r c -> p (r c)"), ps[:, 5, 0:8 * NT]))

        @blk.tensor
        def _(pe):
            pe.wait_ge(k_in, 16)
            for c in range(NT + 3):
                if c == NT:
                    pe.wait_ge(c_in, 32)
                if c >= 2:
                    pe.wait_ge(copied, c - 1)
                if c == NT + 2:
                    nc.tensor.transpose(ps[:, 6 + c % 2, 0:8], n_rows[:], mem["ident"][0:8, 0:8]).then_inc(turned, 1)
                    continue
                for h in range(HEADS):
                    src = k[:, h, c * P:(c + 1) * P] if c < NT else c_rows[:, 4 * (c - NT) + h, :]
                    ins = nc.tensor.transpose(ps[:, 6 + c % 2, h * P:(h + 1) * P], src, mem["ident"][:])
                ins.then_inc(turned, 1)
            pe.wait_ge(act_step, 9)
            for c in range(NT):
                for j, r in enumerate((r1, r2)):
                    n = 2 * c + j
                    ins = nc.tensor.transpose(ps[:, n // 4, (n % 4) * P:(n % 4 + 1) * P], r[:, c * P:(c + 1) * P], mem["ident"][:])
                    if n % 4 == 3 or n == 17:
                        ins.then_inc(tr, 1)
            for r in range(8):
                ins = nc.tensor.matmul(ps[:, 5, r * NT:(r + 1) * NT], sel[:, r, :], wc[:], start=True, stop=True)
            ins.then_inc(tr, 1)


def chunk_units():
    units = [(0, 8, 0, True), (1, 8, 0, True)]
    for j in range(8):
        units += [(0, j, 1, j < 7), (1, 7 - j, 1, j < 7)]
    return units


def phase_mlstm(nc, io, mem, dram):
    HC = HEADS
    with Phase(nc, "mlstm") as outer:
        col = outer.sb("col", [P, NT, 4, ROWS])
        wcb = outer.sb("wcb", [P, 8, NT])
        mrow = outer.sb("M", [ROWS, T])
        mem.update(mask=outer.sb("mask", [P, 2, P]))
        q = outer.sb("q", [P, HC, T])
        k = outer.sb("k", [P, HC, T])
        kn = outer.sb("k_tok", [P, NT, HC, HD])
        v = outer.sb("v", [P, NT, HC, HD + 1])
        hacc = outer.sb("h", [P, NT, HC, HD])
        C = outer.sb("C", [P, 2, 8, HD + 1])
        gate_rows(nc, io, mem, dram, col, wcb, mrow, q, k, kn, v, hacc, C)
        sum_sq = outer.sb("sum_sq", [P, NT, HC])
        chunk_scan(nc, mem, dram, q, k, kn, v, hacc, C, col, wcb, sum_sq)
        mlstm_output(nc, io, mem, dram, hacc, C, q, sum_sq)


def chunk_scan(nc, mem, dram, q, k, kn, v, hacc, C, col, wcb, sum_sq):
    ps = mem["psum"]
    units = chunk_units()
    N = len(units)
    ups = [n for n, un in enumerate(units) if un[3]]
    HC = HEADS
    E = HD + 1
    RB = 3

    def updates_before(n):
        return sum(1 for i in ups if i < n)

    def updates_upto_same(n):
        d, c, s, _ = units[n]
        last = [i for i in ups if i < n and units[i][0] == d and units[i][2] == s]
        return updates_before(last[-1]) + 1 if last else 0

    with Phase(nc, "scan") as ph:
        spread = ph.sb("rows_spread", [P, RB, 2, HC, P])
        top = ph.sb("top", [P, 2, HC, P])
        dec = ph.sb("decay", [P, 2, HC, P])
        prob = ph.sb("prob", [P, 2, HC, P])
        qw = ph.sb("weighted_q", [P, 2, HC, P])
        wv = ph.sb("weighted_v", [P, 2, HC, E])
        den = ph.sb("den", [P, 2, HC])
        square = ph.sb("square", [P, HC, HD])
        squared = ph.sem("squared")
        cleared = ph.sem("h_cleared")
        rows_in = [ph.sem(f"rows_in{i}") for i in range(RB)]
        score = ph.sem("scores_done")
        top_done = ph.sem("top_done")
        dec_done = ph.sem("decay_done")
        prob_done = ph.sem("prob_done")
        qw_done = ph.sem("weighted_q_done")
        wv_done = ph.sem("weighted_v_done")
        num_done = ph.sem("numerators_done")
        state_mm = ph.sem("state_product_done")
        state_done = ph.sem("state_updated")
        out_done = ph.sem("h_added")
        step_sem = ph.sem("dve_step")
        B_S, B_N, B_C = 0, 2, 6
        blk = ph.block()

        def heads(bank):
            return ps[:, bank, :].rearrange("p (h d) -> p h d", h=HC)

        def wide(bank, h):
            return ps[:, bank + h // 2, (h % 2) * E:(h % 2) * E + E]

        @blk.sync
        def _(sp):
            for n in range(N):
                d, c, s, up = units[n]
                if n >= RB:
                    sp.wait_ge(top_done, n - RB + 1)
                    sp.wait_ge(qw_done, n - RB + 1)
                for i in range(2):
                    src = dram["scan_rows"][i:i + 1, HC * d:HC * d + HC, c * P:(c + 1) * P]
                    sp.dma_start(spread[:, n % RB, i], src.broadcast_to([P, HC, P])).then_inc(rows_in[n % RB], 16)

        @blk.tensor
        def _(pe):
            def scores(n):
                d, c, s, up = units[n]
                tok = slice(c * P, (c + 1) * P)
                if n >= 2:
                    pe.wait_ge(prob_done, n - 1)
                for h in range(HC):
                    ins = nc.tensor.matmul(heads(B_S + n % 2)[:, h, :], k[:, h, tok], q[:, h, tok], start=True, stop=True)
                ins.then_inc(score, 1)

            scores(0)
            for n in range(N):
                d, c, s, up = units[n]
                num = B_N + 2 * (n % 2)
                if n + 1 < N:
                    scores(n + 1)
                pe.wait_ge(prob_done, n + 1)
                if n >= 2:
                    pe.wait_ge(out_done, n - 1)
                pe.wait_ge(qw_done, n + 1)
                if updates_upto_same(n):
                    pe.wait_ge(state_done, updates_upto_same(n))
                for h in range(HC):
                    nc.tensor.matmul(wide(num, h), prob[:, n % 2, h, :], v[:, c, h, :], start=True, stop=False)
                    ins = nc.tensor.matmul(wide(num, h), qw[:, n % 2, h, :], C[:, s, 4 * d + h, :], start=False, stop=True)
                ins.then_inc(num_done, 1)
                if up:
                    j = updates_before(n)
                    pe.wait_ge(wv_done, j + 1)
                    if j >= 1:
                        pe.wait_ge(state_done, j)
                    for h in range(HC):
                        ins = nc.tensor.matmul(wide(B_C, h), kn[:, c, h, :], wv[:, j % 2, h, :], start=True, stop=True)
                    ins.then_inc(state_mm, 1)

        @blk.gpsimd
        def _(pool):
            def masked(n):
                d, c, s, up = units[n]
                pool.wait_ge(rows_in[n % RB], 32 * (n // RB + 1))
                if n >= 2:
                    pool.wait_ge(dec_done, n - 1)
                nc.gpsimd.tensor_tensor(top[:, n % 2], spread[:, n % RB, 0],
                                        mem["mask"][:, d, :].unsqueeze(1).broadcast_to([P, HC, P]), ALU.add).then_inc(top_done, 1)

            masked(0)
            masked(1)
            nc.gpsimd.memset(hacc[:], 0.0).then_inc(cleared, 1)
            for n in range(N):
                d, c, s, up = units[n]
                if n + 1 < N and n >= 1:
                    masked(n + 1)
                if n >= 2:
                    pool.wait_ge(num_done, n - 1)
                nc.gpsimd.tensor_tensor(qw[:, n % 2], q[:, :, c * P:(c + 1) * P], spread[:, n % RB, 1], ALU.mult)\
                  .then_inc(qw_done, 1)
                if up:
                    j = updates_before(n)
                    if j >= 2:
                        pool.wait_ge(state_mm, j - 1)
                    w = col[:, c, G_STATE, 32 * d:32 * d + HC].unsqueeze(2).broadcast_to([P, HC, E])
                    nc.gpsimd.tensor_tensor(wv[:, j % 2], v[:, c], w, ALU.mult).then_inc(wv_done, 1)

        @blk.scalar
        def _(act):
            second = {un[1]: n for n, un in enumerate(units)}

            def squares(n):
                c = units[n][1]
                if second[c] == n:
                    act.wait_ge(out_done, n + 1)
                    for h in range(HC):
                        nc.scalar.activation(square[:, h, :], hacc[:, c, h, :], ACT.Square, accum_out=sum_sq[:, c, h:h + 1])\
                          .then_inc(squared, 1)
                    act.wait_ge(squared, HC * (1 + sum(1 for m in second.values() if m < n)))

            for n in range(N):
                act.wait_ge(top_done, n + 1)
                if n >= 2:
                    act.wait_ge(prob_done, n - 1)
                d, c, s, up = units[n]
                for h in range(HC):
                    r = 32 * d + h
                    ins = nc.scalar.activation(dec[:, n % 2, h, :], top[:, n % 2, h, :], ACT.Exp, scale=-1.0,
                                               bias=col[:, c, G_SRC, r:r + 1])
                ins.then_inc(dec_done, 1)
                if n >= 3:
                    squares(n - 3)
            for n in range(N - 3, N):
                squares(n)

        @blk.vector
        def _(dve):
            step = Chain(dve, step_sem)
            tt, stt = nc.vector.tensor_tensor, nc.vector.scalar_tensor_tensor

            def probabilities(n):
                dve.wait_ge(dec_done, n + 1)
                dve.wait_ge(score, n + 1)
                if n >= 2:
                    dve.wait_ge(num_done, n - 1)
                tt(prob[:, n % 2], heads(B_S + n % 2), dec[:, n % 2], ALU.mult).then_inc(prob_done, 1)

            probabilities(0)
            dve.wait_ge(cleared, 1)
            for n in range(N):
                d, c, s, up = units[n]
                rows = slice(32 * d, 32 * d + HC)
                num = B_N + 2 * (n % 2)
                if n + 1 < N:
                    probabilities(n + 1)
                if up:
                    j, r0 = updates_before(n), 4 * d
                    dve.wait_ge(state_mm, j + 1)
                    for h in range(HC):
                        ins = stt(out=C[:, s, r0 + h, :], in0=C[:, s, r0 + h, :], scalar=wcb[:, r0 + h, c:c + 1],
                                  in1=wide(B_C, h), op0=ALU.mult, op1=ALU.add)
                    ins.then_inc(state_done, 1)
                dve.wait_ge(num_done, n + 1)
                sums = ps[:, num:num + 2, 0:2 * E].rearrange("p b (h e) -> p b h e", h=2)[:, :, :, HD]
                dn = den[:, n % 2]
                step.do(nc.vector.tensor_copy(dn.rearrange("p (b h) -> p b h", b=2), sums))
                step.do(stt(out=dn, in0=dn, scalar=-1.0, in1=dn, op0=ALU.mult, op1=ALU.max))
                step.do(tt(dn, dn, col[:, c, G_FLOOR, rows], ALU.max))
                step.do(nc.vector.reciprocal(dn, dn))
                for h in range(HC):
                    ins = stt(out=hacc[:, c, h, :], in0=wide(num, h)[:, 0:HD], scalar=dn[:, h:h + 1], in1=hacc[:, c, h, :],
                              op0=ALU.mult, op1=ALU.add)
                ins.then_inc(out_done, 1)
                dve.wait_ge(out_done, n + 1)


def mlstm_output(nc, io, mem, dram, hacc, C, stage, ss):
    ps = mem["psum"]
    HC = HEADS
    with Phase(nc, "mout") as ph:
        o = ph.sb("o", [P, NT, HC, HD])
        c_out = ph.sb("c_out", [P, 8, HD])
        n_out = ph.sb("n_out", [8, HD])
        o_in = [ph.sem(f"o_in{i}") for i in range(3)]
        c_tr = ph.sem("state_transposed")
        c_cp = ph.sem("state_copied")
        mean = ph.sem("mean_square")
        root = ph.sem("root")
        gated = ph.sem("gated")
        tr = ph.sem("transposed")
        cp = ph.sem("copied")
        step_sem = ph.sem("dve_step")
        stored = ph.sem("stored")
        blk = ph.block()

        @blk.sync
        def _(sp):
            for i in range(3):
                sp.dma_start(o[:, 3 * i:3 * i + 3].rearrange("p t h d -> p t (h d)"),
                             dram["o"][3 * i:3 * i + 3].rearrange("t p c -> p t c")).then_inc(o_in[i], 16)
            sp.wait_ge(c_cp, 3)
            sp.dma_start(io["new_C"][0, 0].rearrange("d h e k -> e (d h) k"), c_out[:]).then_inc(stored, 16)
            sp.dma_start(io["new_n"][0, 0].rearrange("d h k -> (d h) k"), n_out[:]).then_inc(stored, 16)
            for t in range(0, NT, 3):
                sp.wait_ge(cp, t + 3)
                at_ = slice(t * P, (t + 3) * P)
                sp.dma_start(dram["y"].rearrange("k p t -> p k t")[:, CH:KD, at_], stage[:, :, at_]).then_inc(stored, 16)
            sp.wait_ge(stored, 80)

        @blk.tensor
        def _(pe):
            for i in range(2):
                for h in range(HC):
                    ins = nc.tensor.transpose(ps[:, 4 + i, h * P:(h + 1) * P], C[:, 0, 4 * i + h, 0:HD], mem["ident"][:])
            nc.tensor.transpose(ps[0:8, 6, 0:P], C[:, 0, :, HD], mem["ident"][:]).then_inc(c_tr, 1)
            for t in range(NT):
                pe.wait_ge(gated, t + 1)
                if t >= 4:
                    pe.wait_ge(cp, t - 3)
                for h in range(HC):
                    ins = nc.tensor.transpose(ps[:, t % 4, h * P:(h + 1) * P], hacc[:, t, h, :], mem["ident"][:])
                ins.then_inc(tr, 1)

        @blk.scalar
        def _(act):
            act.wait_ge(c_tr, 1)
            for i in range(2):
                nc.scalar.activation(c_out[:, 4 * i:4 * i + 4, :].rearrange("p h d -> p (h d)"), ps[:, 4 + i, :], ACT.Copy)\
                  .then_inc(c_cp, 1)
            nc.scalar.activation(n_out[:], ps[0:8, 6, 0:P], ACT.Copy).then_inc(c_cp, 1)
            act.wait_ge(mean, 1)
            nc.scalar.activation(ss[:], ss[:], ACT.Sqrt).then_inc(root, 1)
            w0 = PA["ml_norm_w"]
            for t in range(NT):
                act.wait_ge(tr, t + 1)
                for h in range(HC):
                    ins = nc.scalar.activation(stage[:, h, t * P:(t + 1) * P], ps[:, t % 4, h * P:(h + 1) * P], ACT.Copy,
                                               scale=mem["par"][:, w0 + h:w0 + h + 1])
                ins.then_inc(cp, 1)

        @blk.vector
        def _(dve):
            step = Chain(dve, step_sem)
            tt = nc.vector.tensor_tensor
            nc.vector.tensor_scalar(ss[:], ss[:], 1.0 / HD, EPS, ALU.mult, ALU.add).then_inc(mean, 1)
            dve.wait_ge(root, 1)
            step.do(nc.vector.reciprocal(ss[:], ss[:]))
            for t in range(NT):
                step.do(tt(hacc[:, t], hacc[:, t], ss[:, t, :].unsqueeze(2).broadcast_to([P, HC, HD]), ALU.mult))
                dve.wait_ge(o_in[t // 3], 16)
                tt(hacc[:, t], hacc[:, t], o[:, t], ALU.mult).then_inc(gated, 1)


GRID_W = 64
GRID_H = LS // GRID_W
PADW = GRID_W + 2
GRID = (GRID_H + 2) * PADW
PADT = GRID + LP + 2
STEPS = JF // 2
TAPS = 9


def slot_banks(ps, n):
    return ps[:, 3 * (n % 2):3 * (n % 2) + 3, :]


def add_gated(nc, ps_slot, x, gate):
    stt = nc.vector.scalar_tensor_tensor
    a = x[:, 0:768].rearrange("p (b c) -> p b c", c=BW)
    stt(out=a, in0=ps_slot[:, 0:2, 0:BW], scalar=gate[:, 0:1], in1=a, op0=ALU.mult, op1=ALU.add)
    stt(out=x[:, 768:LS], in0=ps_slot[:, 2, 0:256], scalar=gate[:, 0:1], in1=x[:, 768:LS], op0=ALU.mult, op1=ALU.add)
    return stt(out=x[:, LS:T], in0=ps_slot[:, 2, 256:BW], scalar=gate[:, 1:2], in1=x[:, LS:T], op0=ALU.mult, op1=ALU.add)


def phase_out(nc, io, mem, dram):
    with Phase(nc, "tail") as outer:
        x = outer.sb("x", [P, KD, T])
        mean_sq = outer.sb("mean_sq", [P, NT])
        output_projection(nc, io, mem, dram, x, mean_sq)
        with Phase(nc, "ffn") as mid:
            h_hi = mid.sb("h_hi", [P, KD, T], F32R)
            h_lo = mid.sb("h_lo", [P, KD, T], F32R)
            ffn_norm(nc, mem, x, mean_sq, h_hi, h_lo)
            feed_forward(nc, io, mem, x, h_hi, h_lo)
        final_norm(nc, io, mem, x)


def ffn_norm(nc, mem, x, mean_sq, h_hi, h_lo):
    AFFINE_ON_DVE, LO_ON_DVE = (1, 5, 7), (2, 6)
    ps = mem["psum"]
    with Phase(nc, "norm2") as ph:
        root = ph.sb("root", [P, NT])
        rstd = ph.sb("rstd", [P, NT])
        diag = ph.sb("diag", [P, NT, P])
        normed = ph.sb("normed", [P, 2, T])
        full = ph.sb("h_full", [P, 3, T])
        root_done = ph.sem("root_done")
        rstd_done = ph.sem("rstd_done")
        diag_done = ph.sem("diagonals_done")
        spread = ph.sem("rstd_spread")
        normed_done = ph.sem("normed_done")
        full_by = {"act": ph.sem("full_by_act"), "dve": ph.sem("full_by_dve")}
        hi_done = ph.sem("h_hi_done")
        lo_by = {"pool": ph.sem("lo_by_pool"), "dve": ph.sem("lo_by_dve")}
        blk = ph.block()

        def maker(k):
            return "dve" if k in AFFINE_ON_DVE else "act"

        def splitter(k):
            return "dve" if k in LO_ON_DVE else "pool"

        def wait_full(eng, k):
            eng.wait_ge(full_by[maker(k)], sum(maker(i) == maker(k) for i in range(k + 1)))

        def wait_lo(eng, k):
            eng.wait_ge(lo_by[splitter(k)], sum(splitter(i) == splitter(k) for i in range(k + 1)))

        def affine(eng, k):
            if k >= 3:
                wait_lo(eng, k - 3)
            for j, (a, b) in enumerate(((0, LS), (LS, T))):
                src, dst = normed[:, k % 2, a:b], full[:, k % 3, a:b]
                gain, shift = mem["gain_ffn"][:, k, j:j + 1], mem["mod"][:, 24 + k, j:j + 1]
                if maker(k) == "act":
                    ins = nc.scalar.activation(dst, src, ACT.Identity, scale=gain, bias=shift)
                else:
                    ins = nc.vector.tensor_scalar(dst, src, gain, shift, ALU.mult, ALU.add)
            ins.then_inc(full_by[maker(k)], 1)

        def split_lo(eng, k):
            eng.wait_ge(hi_done, k + 1)
            eng.tensor_tensor(h_lo[:, k, :], full[:, k % 3, :], h_hi[:, k, :].bitcast(F32), ALU.subtract)\
               .then_inc(lo_by[splitter(k)], 1)

        @blk.tensor
        def _(pe):
            for t in range(NT):
                pe.wait_ge(diag_done, t + 1)
                last = nc.tensor.matmul(ps[:, t // 3, (t % 3) * P:(t % 3 + 1) * P], mem["ones"][:], diag[:, t, :],
                                        start=True, stop=True)
            last.then_inc(spread, 1)

        @blk.scalar
        def _(act):
            nc.scalar.activation(root[:], mean_sq[:], ACT.Sqrt).then_inc(root_done, 1)
            for k in range(KD):
                if maker(k) == "act":
                    act.wait_ge(normed_done, k + 1)
                    affine(act, k)
                wait_full(act, k)
                nc.scalar.activation(h_hi[:, k, :], full[:, k % 3, :], ACT.Copy).then_inc(hi_done, 1)

        @blk.gpsimd
        def _(pool):
            for k in range(KD):
                if splitter(k) == "pool":
                    split_lo(nc.gpsimd, k)

        @blk.vector
        def _(dve):
            dve.wait_ge(root_done, 1)
            nc.vector.reciprocal(rstd[:], root[:]).then_inc(rstd_done, 1)
            dve.wait_ge(rstd_done, 1)
            for t in range(NT):
                nc.vector.tensor_scalar_mul(diag[:, t, :], mem["ident"][:], rstd[:, t:t + 1]).then_inc(diag_done, 1)
            dve.wait_ge(spread, 1)
            for k in range(KD):
                if k >= 2:
                    wait_full(dve, k - 2)
                nc.vector.tensor_tensor(normed[:, k % 2, :].rearrange("p (b c) -> p b c", c=BW),
                                        x[:, k, :].rearrange("p (b c) -> p b c", c=BW), ps[:, 0:NB, 0:BW], ALU.mult)\
                    .then_inc(normed_done, 1)
                if maker(k) == "dve":
                    dve.wait_ge(normed_done, k + 1)
                    affine(dve, k)
                if k >= 1 and splitter(k - 1) == "dve":
                    split_lo(nc.vector, k - 1)


def output_projection(nc, io, mem, dram, x, mean_sq):
    ps = mem["psum"]
    with Phase(nc, "oproj") as ph:
        full = ph.sem("product_done")
        ring = WeightRing(nc, ph, mem, lambda u: (full, 2 * (u + 1)), ahead=2)
        y = ph.sb("y", [P, 4, T])
        y_hi = ph.sb("y_hi", [P, KD, T], F32R)
        y_lo = ph.sb("y_lo", [P, KD, T], F32R)
        y_in = [ph.sem(f"y_in{i}") for i in range(4)]
        x_rows = ph.sb("x_rows", [P, 3, D])
        x_in = [ph.sem(f"x_in{i}") for i in range(3)]
        x_turned = ph.sem("x_transposed")
        x_done = ph.sem("x_copied")
        hi = ph.sem("y_hi_done")
        lo = ph.sem("y_lo_done")
        added = ph.sem("added")
        sum_sq = ph.sb("sum_sq", [P, T])
        square = ph.sb("square", [P, T])
        sums = ph.sem("token_sums")
        squared = ph.sem("squared")
        summed = ph.sem("squares_summed")
        blk = ph.block()

        @blk.sync
        def _(sp):
            for k in range(KD):
                if k >= 4:
                    sp.wait_ge(lo, k - 3)
                sp.dma_start(y[:, k % 4, :], dram["y"][k]).then_inc(y_in[k % 4], 16)
            for t in range(NT):
                if t >= 3:
                    sp.wait_ge(x_turned, 2 * (t - 2))
                sp.dma_start(x_rows[:, t % 3, :], io["x_sample"][0, t * P:(t + 1) * P, :] if t < 8 else io["x_prompt"][0])\
                  .then_inc(x_in[t % 3], 16)
            for u in range(2, 4):
                load_w_out(sp, ring, io, u)
            ring.load(sp, 4, io["ffn_w_up"][0, :, 0:256].rearrange("(k p) c -> p k c", p=P), lambda r: cols(r, 256))

        @blk.scalar
        def _(act):
            for k in range(KD):
                act.wait_ge(y_in[k % 4], 16 * (k // 4 + 1))
                nc.scalar.activation(y_hi[:, k, :], y[:, k % 4, :], ACT.Copy).then_inc(hi, 1)
            for n in range(2 * NT):
                t, half = n // 2, n % 2
                act.wait_ge(x_turned, n + 1)
                nc.scalar.activation(x[:, 4 * half:4 * half + 4, t * P:(t + 1) * P],
                                     ps[:, 6 + half, :].rearrange("p (k t) -> p k t", t=P), ACT.Copy).then_inc(x_done, 1)
            ring.split_hi(act, 2)
            ring.split_hi(act, 3)
            for n in range(KD):
                act.wait_ge(added, n + 1)
                if n >= 1:
                    act.wait_ge(summed, n)
                nc.scalar.activation(square[:] if n else sum_sq[:], x[:, n, :], ACT.Square).then_inc(squared, 1)
                if n == 5:
                    ring.split_hi(act, 4)

        @blk.gpsimd
        def _(pool):
            for u in range(2, 4):
                ring.split_lo(pool, u)
            for n in range(KD):
                pool.wait_ge(squared, n + 1)
                if n:
                    nc.gpsimd.tensor_tensor(sum_sq[:], sum_sq[:], square[:], ALU.add).then_inc(summed, 1)
                else:
                    pool.sem_inc(summed, 1)
                if n == 5:
                    ring.split_lo(pool, 4)

        @blk.vector
        def _(dve):
            for k in range(KD):
                dve.wait_ge(hi, k + 1)
                nc.vector.tensor_tensor(y_lo[:, k, :], y[:, k % 4, :], y_hi[:, k, :].bitcast(F32), ALU.subtract).then_inc(lo, 1)
            dve.wait_ge(x_done, 2 * NT)
            for n in range(KD):
                dve.wait_ge(full, n + 1)
                add_gated(nc, slot_banks(ps, n), x[:, n, :], mem["mod"][:, 16 + n, :]).then_inc(added, 1)
            dve.wait_ge(sums, 1)
            nc.vector.tensor_scalar(mean_sq[:], ps[:, 6, 0:NT], 1.0 / D, EPS, ALU.mult, ALU.add)

        @blk.tensor
        def _(pe):
            def transposes():
                for n in range(2 * NT):
                    t, half = n // 2, n % 2
                    if half == 0:
                        pe.wait_ge(x_in[t % 3], 16 * (t // 3 + 1))
                    if n >= 2:
                        pe.wait_ge(x_done, n - 1)
                    for j in range(4):
                        last = nc.tensor.transpose(ps[:, 6 + half, j * P:(j + 1) * P],
                                                   x_rows[:, t % 3, (4 * half + j) * P:(4 * half + j + 1) * P], mem["ident"][:])
                    last.then_inc(x_turned, 1)

            for n in range(KD):
                ring.ready(pe, n // 2)
                if n >= 2:
                    pe.wait_ge(added, n - 1)
                wh, wl = cols(ring.hi(n // 2), 256), cols(ring.lo(n // 2), 256)
                c = (n % 2) * P
                slot = slot_banks(ps, n)
                for k in range(KD):
                    if n == 0:
                        pe.wait_ge(lo, k + 1)
                    last = product(nc, [slot[:, i, 0:BW] for i in range(NB)], lambda k: wh[:, k, c:c + P],
                                   lambda k: wl[:, k, c:c + P], lambda k, i: y_hi[:, k, i * BW:(i + 1) * BW],
                                   lambda k, i: y_lo[:, k, i * BW:(i + 1) * BW], [k], first=k == 0, last=k == KD - 1)
                last.then_inc(full, 1)
                if n == 0:
                    transposes()
            pe.wait_ge(summed, KD)
            for t in range(NT):
                last = nc.tensor.matmul(ps[:, 6, t:t + 1], sum_sq[:, t * P:(t + 1) * P], mem["ones"][:, 0:1], start=True, stop=True)
            last.then_inc(sums, 1)


def feed_forward(nc, io, mem, x, h_hi, h_lo):
    ps, par = mem["psum"], mem["par"]
    up, down = io["ffn_w_up"][0], io["ffn_w_down"][0]
    with Phase(nc, "mlp") as ph:
        pad = ph.sb("pad", [P, 2, PADT])
        acc_a = ph.sb("acc_a", [P, 2, T])
        acc_v = ph.sb("acc_v", [P, 2, T])
        g_hi = ph.sb("g_hi", [P, 2, T], F32R)
        g_lo = ph.sb("g_lo", [P, 2, T], F32R)
        taps = ph.sb("taps", [P, 2, 2, TAPS + 1, 2])
        pads_zero = ph.sem("pads_zero")
        raw_in = [ph.sem(f"weights_loaded{i}") for i in range(2)]
        w_hi_done = ph.sem("weights_hi")
        w_lo_done = ph.sem("weights_lo")
        taps_ready = ph.sem("taps_ready")
        full = ph.sem("product_done")
        evac = ph.sem("product_copied")
        tap0_done = ph.sem("first_tap_done")
        conv_done = ph.sem("conv_done")
        silu_done = ph.sem("silu_done")
        gated = ph.sem("gated")
        g_hi_done = ph.sem("gated_hi")
        g_lo_done = ph.sem("gated_lo")
        added = ph.sem("down_added")
        step_sem = ph.sem("dve_step")
        row_sem = ph.sem("row_step")
        blk = ph.block()

        w_raw, w_hi, w_lo = mem["w_raw"], mem["w_hi"], mem["w_lo"]

        def products(i):
            return 12 * i - 8 if not (isinstance(i, int) and i == 0) else 0

        class Unit:

            def __init__(self, i, odd, kind):
                k = {"a": -1, "d": 0, "v": 1}[kind]
                if isinstance(i, int) and i == 0:
                    self.u, self.slot = {"a": 0, "v": 1}[kind], {"a": 0, "v": 1}[kind]
                else:
                    self.u = 3 * i + k
                    self.slot = (3 * odd + k) % 2
                self.i, self.kind = i, kind
                self.u_even = self.u - self.slot

            def loads(self):
                return 8 * self.u_even + 16

        def load(sp, un):
            if not isinstance(un.u, int) or un.u >= 2:
                sp.wait_ge(w_lo_done, un.u - 1)
            dst = w_raw[:, un.slot, :]
            if un.kind == "d":
                src = down[bass.ds(256 * (un.i - 1), 256), :].rearrange("(j p) c -> p j c", p=P)
                dst = dst.rearrange("p (j c) -> p j c", j=2)
            else:
                src = up[:, bass.ds(256 * un.i + (DFF if un.kind == "v" else 0), 256)].rearrange("(k p) c -> p k c", p=P)
                dst = cols(dst, 256)
            sp.dma_start(dst, src).then_inc(raw_in[un.slot], 16)

        def split_hi(act, un, used):
            act.wait_ge(raw_in[un.slot], un.loads())
            if used is not None:
                act.wait_ge(full, used)
            nc.scalar.activation(w_hi[:, un.slot, :], w_raw[:, un.slot, :], ACT.Copy).then_inc(w_hi_done, 1)

        def split_lo(pool, un):
            pool.wait_ge(w_hi_done, un.u + 1)
            nc.gpsimd.tensor_tensor(w_lo[:, un.slot, :], w_raw[:, un.slot, :], w_hi[:, un.slot, :].bitcast(F32),
                                    ALU.subtract).then_inc(w_lo_done, 1)

        def grid(j, dy, dx):
            return pad[:, j, 0:GRID].rearrange("p (r c) -> p r c", c=PADW)[:, dy:dy + GRID_H, dx:dx + GRID_W]

        def row(j, dx):
            return pad[:, j, GRID + dx:GRID + dx + LP]

        def image(a):
            return a[:, 0:LS].rearrange("p (r c) -> p r c", c=GRID_W)

        def steps(eng, body, last):
            body(0, 0)
            with eng.Fori(0, (STEPS - 1) // 2) as turn:
                body(2 * turn + 1, 1)
                body(2 * turn + 2, 0)
            last(STEPS, 1)

        @blk.sync
        def _(sp):
            def body(i, odd):
                if not isinstance(i, int):
                    load(sp, Unit(i, odd, "a"))
                    load(sp, Unit(i, odd, "d"))
                    load(sp, Unit(i, odd, "v"))
                else:
                    sp.sem_inc(raw_in[0], 16)
                    load(sp, Unit(0, 0, "v"))

            def last(i, odd):
                un = Unit(i, odd, "a")
                un.kind = "d"
                load(sp, un)
            steps(sp, body, last)

        @blk.gpsimd
        def _(pool):
            nc.gpsimd.memset(pad[:], 0.0).then_inc(pads_zero, 1)
            view = par[:, PA["ffn_conv_w"]:PA["ffn_conv_w"] + (TAPS + 1) * 2 * JF].rearrange("p (t b) -> p t b", b=2 * JF)

            def fetch_taps(i, odd):
                if not (isinstance(i, int) and i < 2):
                    pool.wait_ge(conv_done, 4 * i - 3)
                for half in range(2):
                    nc.gpsimd.tensor_copy(taps[:, odd, half], view[:, :, bass.ds(2 * i + JF * half, 2)]).then_inc(taps_ready, 1)

            def gated_lo(i, j):
                pool.wait_ge(g_hi_done, 2 * i + j + 1)
                nc.gpsimd.tensor_tensor(g_lo[:, j, :], acc_a[:, j, :], g_hi[:, j, :].bitcast(F32), ALU.subtract)\
                  .then_inc(g_lo_done, 1)

            def body(i, odd):
                if isinstance(i, int):
                    pool.sem_inc(w_lo_done, 1)
                    split_lo(pool, Unit(0, 0, "v"))
                    fetch_taps(0, 0)
                else:
                    split_lo(pool, Unit(i, odd, "d"))
                    fetch_taps(i, odd)
                    gated_lo(i - 1, 0)
                    gated_lo(i - 1, 1)
                    split_lo(pool, Unit(i, odd, "v"))
                split_lo(pool, Unit(i + 1, 1 - odd, "a"))

            def last(i, odd):
                gated_lo(i - 1, 0)
                gated_lo(i - 1, 1)
            steps(pool, body, last)

        @blk.scalar
        def _(act):
            def copy_out(i, loc, odd):
                first = isinstance(i, int)
                n = products(i) + (loc if first else (0, 1, 6, 11)[loc])
                slot = ps[:, 3 * (loc % 2):3 * (loc % 2) + 3, :]
                j = loc % 2
                act.wait_ge(full, n + 1)
                if first and loc < 2:
                    act.wait_ge(pads_zero, 1)
                else:
                    act.wait_ge(conv_done, 4 * i + loc - 1)
                g = pad[:, j, 0:GRID].rearrange("p (r c) -> p r c", c=PADW)
                nc.scalar.activation(g[:, 1:13, 1:65].rearrange("p (b r) c -> p b r c", b=2),
                                     slot[:, 0:2, 0:BW].rearrange("p b (r c) -> p b r c", c=GRID_W), ACT.Copy)
                nc.scalar.activation(g[:, 13:17, 1:65], slot[:, 2, 0:256].rearrange("p (r c) -> p r c", c=GRID_W), ACT.Copy)
                nc.scalar.activation(pad[:, j, GRID + 1:GRID + 1 + LP], slot[:, 2, 256:BW], ACT.Copy).then_inc(evac, 1)
                if loc == 0:
                    act.wait_ge(taps_ready, 2 * i + 2)
                act.wait_ge(evac, 4 * i + loc + 1)
                half = loc // 2
                if half == 0:
                    if not first:
                        act.wait_ge(g_lo_done, 2 * i - 1 + j)
                    acc = acc_a[:, j, :]
                else:
                    if not first:
                        act.wait_ge(gated, 2 * i - 1 + j)
                    acc = acc_v[:, j, :]
                tp = taps[:, odd, half, :, j:j + 1]
                nc.scalar.activation(image(acc), grid(j, 0, 0), ACT.Identity, scale=tp[:, 0], bias=tp[:, TAPS])
                nc.scalar.activation(acc[:, LS:T], row(j, 0), ACT.Identity, scale=tp[:, 3], bias=tp[:, TAPS])\
                  .then_inc(tap0_done, 1)

            def silu(i, j):
                act.wait_ge(conv_done, 4 * i + j + 1)
                nc.scalar.activation(acc_a[:, j, :], acc_a[:, j, :], ACT.Silu).then_inc(silu_done, 1)

            def gated_hi(i, j):
                act.wait_ge(gated, 2 * i + j + 1)
                nc.scalar.activation(g_hi[:, j, :], acc_a[:, j, :], ACT.Copy).then_inc(g_hi_done, 1)

            def body(i, odd):
                if isinstance(i, int):
                    act.sem_inc(w_hi_done, 1)
                    split_hi(act, Unit(0, 0, "v"), None)
                else:
                    split_hi(act, Unit(i, odd, "d"), products(i))
                    gated_hi(i - 1, 0)
                copy_out(i, 0, odd)
                if not isinstance(i, int):
                    gated_hi(i - 1, 1)
                copy_out(i, 1, odd)
                if not isinstance(i, int):
                    split_hi(act, Unit(i, odd, "v"), products(i) + 2)
                silu(i, 0)
                silu(i, 1)
                copy_out(i, 2, odd)
                split_hi(act, Unit(i + 1, 1 - odd, "a"), 2 if isinstance(i, int) else products(i) + 11)
                copy_out(i, 3, odd)

            def last(i, odd):
                gated_hi(i - 1, 0)
                gated_hi(i - 1, 1)
            steps(act, body, last)

        @blk.vector
        def _(dve):
            OWN = 4 * 8

            def tap(i, loc, odd, acc, t):
                j, half = loc % 2, loc // 2
                tp = taps[:, odd, half, :, j:j + 1]
                if t == 1:
                    dve.wait_ge(tap0_done, 4 * i + loc + 1)
                else:
                    dve.wait_ge(step_sem, OWN * i + 8 * loc + t - 1)
                nc.vector.scalar_tensor_tensor(out=image(acc), in0=grid(j, t // 3, t % 3), scalar=tp[:, t], in1=image(acc),
                                               op0=ALU.mult, op1=ALU.add).then_inc(step_sem, 1)
                if t in (1, 2):
                    if t == 2:
                        dve.wait_ge(row_sem, 8 * i + 2 * loc + 1)
                    nc.vector.scalar_tensor_tensor(out=acc[:, LS:T], in0=row(j, t), scalar=tp[:, 3 + t], in1=acc[:, LS:T],
                                                   op0=ALU.mult, op1=ALU.add).then_inc(row_sem, 1)
                if t == TAPS - 1:
                    dve.wait_ge(row_sem, 8 * i + 2 * loc + 2)
                    dve.wait_ge(step_sem, OWN * i + 8 * loc + 8)
                    dve.sem_inc(conv_done, 1)

            def conv(i, loc, odd, acc):
                for t in range(1, TAPS):
                    tap(i, loc, odd, acc, t)

            def down_add(n, cb, slot):
                dve.wait_ge(full, n + 1)
                add_gated(nc, ps[:, 3 * slot:3 * slot + 3, :], x[:, cb, :], mem["mod"][:, 40 + cb, :]).then_inc(added, 1)

            def gate(i, j):
                dve.wait_ge(silu_done, 2 * i + j + 1)
                nc.vector.tensor_tensor(acc_a[:, j, :], acc_a[:, j, :], acc_v[:, j, :], ALU.mult).then_inc(gated, 1)

            def body(i, odd):
                conv(i, 0, odd, acc_a[:, 0, :])
                for loc, acc, cb0, at_ in ((1, acc_a[:, 1, :], 0, 2), (2, acc_v[:, 0, :], 4, 7)):
                    for t in range(1, TAPS):
                        if t <= 4 and not isinstance(i, int):
                            cb = cb0 + t - 1
                            down_add(products(i) + at_ + t - 1, cb, (at_ + t - 1) % 2)
                        tap(i, loc, odd, acc, t)
                gate(i, 0)
                conv(i, 3, odd, acc_v[:, 1, :])
                gate(i, 1)

            def last(i, odd):
                for cb in range(KD):
                    down_add(products(i) + cb, cb, cb % 2)
            dve.sem_inc(added, 1)
            steps(dve, body, last)

        @blk.tensor
        def _(pe):
            def up_product(un, i, loc):
                wh, wl = cols(w_hi[:, un.slot, :], 256), cols(w_lo[:, un.slot, :], 256)
                j = loc % 2
                if j == 0:
                    pe.wait_ge(w_lo_done, un.u + 1)
                slot = ps[:, 3 * j:3 * j + 3, :]
                c = j * P
                product(nc, [slot[:, b, 0:BW] for b in range(NB)], lambda k: wh[:, k, c:c + P], lambda k: wl[:, k, c:c + P],
                        lambda k, b: h_hi[:, k, b * BW:(b + 1) * BW], lambda k, b: h_lo[:, k, b * BW:(b + 1) * BW],
                        range(KD)).then_inc(full, 1)

            def down_product(un, cb, s):
                wh = w_hi[:, un.slot, :].rearrange("p (j c) -> p j c", j=2)
                wl = w_lo[:, un.slot, :].rearrange("p (j c) -> p j c", j=2)
                slot = ps[:, 3 * s:3 * s + 3, :]
                c = cb * P
                product(nc, [slot[:, b, 0:BW] for b in range(NB)], lambda k: wh[:, k, c:c + P], lambda k: wl[:, k, c:c + P],
                        lambda k, b: g_hi[:, k, b * BW:(b + 1) * BW], lambda k, b: g_lo[:, k, b * BW:(b + 1) * BW],
                        range(2)).then_inc(full, 1)

            def sums(i, n):
                pe.wait_ge(added, 8 * i - 8 + n + 1)

            def body(i, odd):
                a, v = Unit(i, odd, "a"), Unit(i, odd, "v")
                if isinstance(i, int):
                    for loc in range(4):
                        if loc >= 2:
                            pe.wait_ge(evac, loc - 1)
                        up_product(a if loc < 2 else v, i, loc)
                    return
                d = Unit(i, odd, "d")
                sums(i, 0)
                pe.wait_ge(evac, 4 * i - 1)
                up_product(a, i, 0)
                pe.wait_ge(evac, 4 * i)
                up_product(a, i, 1)
                pe.wait_ge(w_lo_done, d.u + 1)
                pe.wait_ge(g_lo_done, 2 * i)
                for cb in range(4):
                    if cb < 2:
                        pe.wait_ge(evac, 4 * i + 1 + cb)
                    else:
                        sums(i, cb - 1)
                    down_product(d, cb, cb % 2)
                sums(i, 3)
                up_product(v, i, 2)
                for cb in range(4, 8):
                    if cb == 5:
                        pe.wait_ge(evac, 4 * i + 3)
                    else:
                        sums(i, cb if cb == 4 else cb - 1)
                    down_product(d, cb, (cb + 1) % 2)
                sums(i, 7)
                up_product(v, i, 3)

            def last(i, odd):
                d = Unit(i, odd, "a")
                pe.wait_ge(w_lo_done, d.u + 1)
                pe.wait_ge(g_lo_done, 2 * i)
                pe.wait_ge(evac, 4 * i)
                for cb in range(KD):
                    sums(i, max(cb - 1, 0))
                    down_product(d, cb, cb % 2)
            steps(pe, body, last)


def final_norm(nc, io, mem, x):
    ps = mem["psum"]
    with Phase(nc, "final") as ph:
        w = ph.sb("w", [P, D])
        square = ph.sb("square", [P, D])
        sum_sq = ph.sb("sum_sq", [P, NT])
        mean_sq = ph.sb("mean_sq", [P, NT])
        root = ph.sb("root", [P, NT])
        rstd = ph.sb("rstd", [P, NT])
        y = ph.sb("y", [P, 4, D])
        w_in = ph.sem("w_in")
        turned = ph.sem("transposed")
        summed = ph.sem("squares_summed")
        means = ph.sem("mean_squares")
        roots = ph.sem("roots")
        rstds = ph.sem("rstds")
        scaled = ph.sem("scaled")
        stored = [ph.sem(f"stored{i}") for i in range(4)]
        blk = ph.block()

        def pair(t):
            b = 2 * (t % 4)
            return ps[:, b:b + 2, :]

        def halves(row):
            return row.rearrange("p (b c) -> p b c", b=2)

        @blk.sync
        def _(sp):
            sp.dma_start(w[:], io["final_norm_w"].rearrange("(o c) -> o c", o=1).broadcast_to([P, D])).then_inc(w_in, 16)
            for t in range(NT):
                sp.wait_ge(scaled, t + 1)
                dst = io["y_sample"][0, t * P:(t + 1) * P, :] if t < 8 else io["y_prompt"][0]
                sp.dma_start(dst, y[:, t % 4, :]).then_inc(stored[t % 4], 16)
            for i in range(4):
                sp.wait_ge(stored[i], 16 * ((NT - i + 3) // 4))

        @blk.tensor
        def _(pe):
            for t in range(NT):
                if t >= 4:
                    pe.wait_ge(scaled, t - 3)
                for k in range(KD):
                    last = nc.tensor.transpose(pair(t)[:, k // 4, (k % 4) * P:(k % 4 + 1) * P], x[:, k, t * P:(t + 1) * P],
                                               mem["ident"][:])
                last.then_inc(turned, 1)

        @blk.scalar
        def _(act):
            for t in range(NT):
                act.wait_ge(turned, t + 1)
                if t:
                    act.wait_ge(summed, t)
                nc.scalar.activation(halves(square[:]), pair(t), ACT.Square, accum_out=sum_sq[:, t:t + 1]).then_inc(summed, 1)
                act.wait_ge(means, t + 1)
                nc.scalar.activation(root[:, t:t + 1], mean_sq[:, t:t + 1], ACT.Sqrt).then_inc(roots, 1)

        @blk.vector
        def _(dve):
            def mean(t):
                dve.wait_ge(summed, t + 1)
                nc.vector.tensor_scalar(mean_sq[:, t:t + 1], sum_sq[:, t:t + 1], 1.0 / D, EPS, ALU.mult, ALU.add).then_inc(means, 1)

            dve.wait_ge(w_in, 16)
            mean(0)
            for t in range(NT):
                dve.wait_ge(roots, t + 1)
                nc.vector.reciprocal(rstd[:, t:t + 1], root[:, t:t + 1]).then_inc(rstds, 1)
                if t + 1 < NT:
                    mean(t + 1)
                dve.wait_ge(rstds, t + 1)
                if t >= 4:
                    dve.wait_ge(stored[t % 4], 16 * (t // 4))
                nc.vector.scalar_tensor_tensor(out=halves(y[:, t % 4, :]), in0=pair(t), scalar=rstd[:, t:t + 1],
                                               in1=halves(w[:]), op0=ALU.mult, op1=ALU.mult).then_inc(scaled, 1)


OUTS = [("y_prompt", (1, LP, D)), ("y_sample", (1, LS, D)), ("new_C", (1, 1, 2, HEADS, HD, HD)),
        ("new_n", (1, 1, 2, HEADS, HD)), ("new_m", (1, 1, 2, HEADS))]


def build(nc, io):
    with ExitStack() as ctx:
        def sb(name, shape, dt=F32):
            return ctx.enter_context(nc.sbuf_tensor(name, shape, dt))

        mem = {"psum": ctx.enter_context(nc.psum_tensor("psum", [P, 8, 512], F32)),
               "par": sb("par", [P, NPAR]), "mod": sb("mod", [P, 48, 2]),
               "gain_mix": sb("gain_mix", [P, KD, 2]), "gain_ffn": sb("gain_ffn", [P, KD, 2]),
               "ident": sb("ident", [P, P]), "ones": sb("ones", [P, P]),
               "filter_gain": sb("filter_gain", [P, 2 * CH]),
               "w_raw": sb("w_raw", [P, 2, UNIT]), "w_hi": sb("w_hi", [P, 2, UNIT], F32R),
               "w_lo": sb("w_lo", [P, 2, UNIT], F32R)}
        dram = {n: nc.dram_tensor(f"scratch_{n}", shape, F32).ap() for n, shape in dict(
            x0=(CH, P, T), hv=(CH, P, T), q=(CH, P, T), k=(CH, P, T),
            v=(NT, P, DH), o=(NT, P, DH), y=(KD, P, T), scan_rows=(2, 2 * HEADS, T),
            kt=(4, P, 4, DH), kt_prompt=(P, 2, DH)).items()}

        with Phase(nc, "init") as ph:
            blk = ph.block()

            @blk.vector
            def _(dve):
                nc.vector.memset(mem["ones"][:], 1.0)
        with Phase(nc, "front") as front:
            with Phase(nc, "head") as head:
                big_hi, big_lo = (head.sb(n, [P, KD * T], F32R) for n in ("big_hi", "big_lo"))
                k_hi, k_lo = (b[:].rearrange("p (i t c) -> p i t c", i=2, t=NT) for b in (big_hi, big_lo))
                h_hi, h_lo = (b[:].rearrange("p (k t) -> p k t", k=KD) for b in (big_hi, big_lo))
                modulation_and_taps(nc, io, mem, k_hi, k_lo)
                mem["gates"] = front.sb("gates", [P, T], side="right")
                with Phase(nc, "rownorm") as ph:
                    norm = RowNorm(nc, io, ph)
                    filter_spectra(nc, io, mem, dram, k_hi, k_lo, norm)
                    mixing_norm(nc, io, mem, norm.x, h_hi, h_lo)
                phase_project(nc, io, mem, dram, h_hi, h_lo)
            phase_hyena(nc, io, mem, dram)
            phase_mlstm(nc, io, mem, dram)
        phase_out(nc, io, mem, dram)
        Phase.cleared.close()
        Phase.cleared = None


def kernel(**inputs):
    import concourse.bacc as bacc
    from concourse.bass_utils import run_bass_kernel_spmd

    nc = bacc.Bacc("TRN2", target_bir_lowering=False, num_devices=1)
    arrays = {n: np.ascontiguousarray(a) for n, a in inputs.items()}
    arrays.update(constants())
    io = {n: nc.dram_tensor(n, a.shape, F32, kind="ExternalInput").ap() for n, a in arrays.items()}
    for n, shape in OUTS:
        io[n] = nc.dram_tensor(n, shape, F32, kind="ExternalOutput").ap()
    build(nc, io)
    r = run_bass_kernel_spmd(nc, [arrays], core_ids=[0])
    return tuple(np.asarray(r.results[0][n]) for n, _ in OUTS)
```
